# Optimizing a Trainium2 kernel written in Bass

```python
import jax, jax.numpy as jnp
from jax import lax
import numpy as np
import math

D_MODEL = 2048
BATCH = 1
SEQ = 512
DEPTH = 1

HEAD_DIM = 64
RWKV_WIDTH = 3 * D_MODEL // 8
POOL_WIDTH = D_MODEL // 4
SB_WIDTH = D_MODEL - RWKV_WIDTH - POOL_WIDTH
D_MIX = RWKV_WIDTH + POOL_WIDTH + SB_WIDTH
RWKV_HEADS = RWKV_WIDTH // HEAD_DIM
SB_HEADS = SB_WIDTH // HEAD_DIM
DECAY_RANK = 64
ICLR_RANK = 64
POOL_WINDOWS = (2, 4, 8, 16)
POOL_GROUPS = len(POOL_WINDOWS)
POOL_GROUP_WIDTH = POOL_WIDTH // POOL_GROUPS
SB_BLOCK = 128
RMS_EPS = 1e-6
GN_EPS = 64e-5
A_COLS = 4 * RWKV_WIDTH + DECAY_RANK + ICLR_RANK
B_COLS = 2 * POOL_WIDTH
C_COLS = 4 * SB_WIDTH
IN_COLS = A_COLS + B_COLS + C_COLS


def _rms(x, g):
    xf = x.astype(jnp.float32)
    y = xf * lax.rsqrt(jnp.mean(jnp.square(xf), axis=-1, keepdims=True) + RMS_EPS)
    return (y * g.astype(jnp.float32)).astype(x.dtype)

def _split(u, sizes):
    cuts = [int(c) for c in np.cumsum(sizes)[:-1]]
    return jnp.split(u, cuts, axis=-1)

def _token_shift(u, mu):
    prev = jnp.pad(u, ((0, 0), (1, 0), (0, 0)))[:, :-1]
    return u + (prev - u) * mu

def _rwkv7(r, k, v, wd, ad, w_up, w0, a_up, a0, k_k, k_a, r_k, gn_g, gn_b):
    f32 = jnp.float32
    B, S, C = r.shape
    H, N = C // HEAD_DIM, HEAD_DIM
    r, k, v, wd, ad = (t.astype(f32) for t in (r, k, v, wd, ad))
    logw = -jax.nn.softplus(-(w0 + jnp.tanh(wd) @ w_up)) - 0.5
    decay = jnp.exp(-jnp.exp(logw))
    a = jax.nn.sigmoid(a0 + ad @ a_up)
    kk = (k * k_k).reshape(B, S, H, N)
    kk = kk / jnp.maximum(jnp.sqrt(jnp.sum(jnp.square(kk), axis=-1, keepdims=True)), 1e-12)
    k = k * (1.0 + (a - 1.0) * k_a)

    def heads_t(t):
        return t.reshape(B, S, H, N).transpose(1, 0, 2, 3)

    xs = (heads_t(r), heads_t(k), heads_t(v), heads_t(decay),
          kk.transpose(1, 0, 2, 3), heads_t(a))

    def step(state, inp):
        r_t, k_t, v_t, w_t, kk_t, a_t = inp
        sa = jnp.einsum('bhvk,bhk->bhv', state, -kk_t)
        state = (state * w_t[:, :, None, :]
                 + sa[..., None] * (kk_t * a_t)[:, :, None, :]
                 + v_t[..., None] * k_t[:, :, None, :])
        return state, jnp.einsum('bhvk,bhk->bhv', state, r_t)

    _, y = lax.scan(step, jnp.zeros((B, H, N, N), f32), xs)
    y = y.transpose(1, 0, 2, 3)
    mu = jnp.mean(y, axis=-1, keepdims=True)
    var = jnp.mean(jnp.square(y - mu), axis=-1, keepdims=True)
    y = ((y - mu) * lax.rsqrt(var + GN_EPS)).reshape(B, S, C) * gn_g + gn_b
    bonus = jnp.sum((r * k).reshape(B, S, H, N) * r_k, axis=-1, keepdims=True) * v.reshape(B, S, H, N)
    return y + bonus.reshape(B, S, C)

def _pool(u, pool_w, pool_scale):
    f32 = jnp.float32
    B, S, C = u.shape
    uf = u.astype(f32)
    cs = jnp.cumsum(uf, axis=1)
    pos = jnp.arange(1, S + 1, dtype=f32)[None, :, None]
    groups = []
    for gi, win in enumerate(POOL_WINDOWS):
        sl = slice(gi * POOL_GROUP_WIDTH, (gi + 1) * POOL_GROUP_WIDTH)
        c = cs[..., sl]
        lag = jnp.pad(c, ((0, 0), (win, 0), (0, 0)))[:, :S]
        mean = (c - lag) / jnp.minimum(pos, float(win))
        groups.append(mean - uf[..., sl])
    d = jnp.stack(groups, axis=2)
    y = jnp.einsum('bsgc,gcd->bsgd', d, pool_w.astype(f32)).reshape(B, S, C)
    return y * pool_scale

def _stick_breaking(q, k, v, qn_g, kn_g):
    f32 = jnp.float32
    B, S, C = q.shape
    H = C // HEAD_DIM

    def heads(t):
        return t.reshape(B, S, H, HEAD_DIM).transpose(0, 2, 1, 3)

    q = _rms(heads(q), qn_g).astype(f32) * (HEAD_DIM ** -0.5)
    k = _rms(heads(k), kn_g).astype(f32)
    v = heads(v).astype(f32)
    outs = []
    for q0 in range(0, S, SB_BLOCK):
        kend = q0 + SB_BLOCK
        z = jnp.einsum('bhqd,bhkd->bhqk', q[:, :, q0:kend], k[:, :, :kend])
        causal = jnp.arange(kend)[None, :] < (q0 + jnp.arange(SB_BLOCK))[:, None]
        log_1m = jnp.where(causal, jax.nn.log_sigmoid(-z), 0.0)
        after = lax.cumsum(log_1m, axis=3, reverse=True) - log_1m
        w = jnp.where(causal, jnp.exp(jax.nn.log_sigmoid(z) + after), 0.0)
        outs.append(jnp.einsum('bhqk,bhkd->bhqd', w, v[:, :, :kend]))
    o = jnp.concatenate(outs, axis=2)
    return o.transpose(0, 2, 1, 3).reshape(B, S, C)

def first_inputs(seed: int = 0) -> dict:
    key = jax.random.key(seed)
    ks = jax.random.split(key, 20)
    f32 = jnp.float32
    nrm = lambda kk, shape, s: jax.random.normal(kk, shape, f32) * s
    L = DEPTH
    return {
        "x": nrm(ks[0], (BATCH, SEQ, D_MODEL), 1.0),
        "norm_g": 1.0 + nrm(ks[1], (L, D_MODEL), 0.02),
        "w_in": nrm(ks[2], (L, D_MODEL, IN_COLS), D_MODEL ** -0.5),
        "mu_a": jax.random.uniform(ks[3], (L, A_COLS), f32, 0.0, 1.0),
        "w_up": nrm(ks[4], (L, DECAY_RANK, RWKV_WIDTH), 0.1 * DECAY_RANK ** -0.5),
        "w0": jax.random.uniform(ks[5], (L, RWKV_WIDTH), f32, -6.0, 1.0),
        "a_up": nrm(ks[6], (L, ICLR_RANK, RWKV_WIDTH), 0.1 * ICLR_RANK ** -0.5),
        "a0": nrm(ks[7], (L, RWKV_WIDTH), 0.1),
        "k_k": 0.85 + nrm(ks[8], (L, RWKV_WIDTH), 0.02),
        "k_a": 1.0 + nrm(ks[9], (L, RWKV_WIDTH), 0.02),
        "r_k": nrm(ks[10], (L, RWKV_HEADS, HEAD_DIM), 0.1),
        "gn_g": 1.0 + nrm(ks[11], (L, RWKV_WIDTH), 0.02),
        "gn_b": nrm(ks[12], (L, RWKV_WIDTH), 0.02),
        "pool_w": nrm(ks[13], (L, POOL_GROUPS, POOL_GROUP_WIDTH, POOL_GROUP_WIDTH), POOL_GROUP_WIDTH ** -0.5),
        "pool_scale": 1.0 + nrm(ks[14], (L, POOL_WIDTH), 0.02),
        "qn_g": 1.0 + nrm(ks[15], (L, HEAD_DIM), 0.02),
        "kn_g": 1.0 + nrm(ks[16], (L, HEAD_DIM), 0.02),
        "w_out": nrm(ks[17], (L, D_MIX, D_MODEL), D_MIX ** -0.5),
    }

def first_block(x, norm_g, w_in, mu_a, w_up, w0, a_up, a0, k_k, k_a, r_k, gn_g, gn_b,
              pool_w, pool_scale, qn_g, kn_g, w_out):
    f32 = jnp.float32
    for l in range(DEPTH):
        h = _rms(x, norm_g[l])
        proj = h @ w_in[l]
        pa, pb, pc = _split(proj, (A_COLS, B_COLS, C_COLS))
        pa = _token_shift(pa, mu_a[l])
        r, k, v, ga, wd, ad = _split(pa, (RWKV_WIDTH,) * 4 + (DECAY_RANK, ICLR_RANK))
        ya = _rwkv7(r, k, v, wd, ad, w_up[l], w0[l], a_up[l], a0[l], k_k[l], k_a[l],
                    r_k[l], gn_g[l], gn_b[l]) * jax.nn.silu(ga.astype(f32))
        pu, pg = _split(pb, (POOL_WIDTH, POOL_WIDTH))
        yb = _pool(pu, pool_w[l], pool_scale[l]) * jax.nn.silu(pg.astype(f32))
        qc, kc, vc, gc = _split(pc, (SB_WIDTH,) * 4)
        yc = _stick_breaking(qc, kc, vc, qn_g[l], kn_g[l]) * jax.nn.silu(gc.astype(f32))
        y = jnp.concatenate([ya, yb, yc], axis=-1).astype(x.dtype) @ w_out[l]
        x = x + y.astype(x.dtype)
    return x


_first_inputs = first_inputs


def first_inputs(seed=0):
    import zlib

    import numpy as np

    out = dict(_first_inputs(seed))
    spreads = {}
    factors = {'norm_g': 3.662,
     'w_up': 8.0,
     'a_up': 5.013,
     'a0': 4.886,
     'k_k': 8.0,
     'k_a': 8.0,
     'gn_g': 8.0,
     'gn_b': 8.0,
     'pool_scale': 8.0,
     'qn_g': 8.0,
     'kn_g': 8.0}
    for name, (base, spread) in spreads.items():
        noise = np.random.default_rng([zlib.crc32(name.encode()), seed]).standard_normal(out[name].shape)
        drawn = base * np.exp(spread * noise) if base else spread * noise
        out[name] = __import__('jax').numpy.asarray(drawn.astype(out[name].dtype))
    for name, factor in factors.items():
        out[name] = (out[name] * factor).astype(out[name].dtype)
    return out


_narrow_inputs = first_inputs


def first_inputs(seed=0):

    out = dict(_narrow_inputs(seed))
    wider = {'w_up': 10.58,
     'k_k': 12.0,
     'gn_g': 12.0,
     'gn_b': 12.0,
     'pool_scale': 11.17,
     'qn_g': 12.0,
     'kn_g': 12.0}
    for name, times in wider.items():
        mean = out[name].mean()
        out[name] = (mean + times * (out[name] - mean)).astype(out[name].dtype)
    return out


DEPTH_2 = 2

CHUNK = 64
N_LEFT_CHUNKS = 8
BAND = (N_LEFT_CHUNKS + 1) * CHUNK

A_HEADS = 16
A_HEAD_DIM = 64
A_WIDTH = A_HEADS * A_HEAD_DIM
MAX_REL = 128
N_REL = 2 * MAX_REL + 1

S5_WIDTH = D_MODEL // 2
S5_GROUP = 16
S5_GROUPS = S5_WIDTH // S5_GROUP
S5_STATE = 64
DT_MIN = 0.001
DT_MAX = 0.1

C_HEADS = 16
C_HEAD_DIM = 128
C_WIDTH = C_HEADS * C_HEAD_DIM
Q_BLOCK = 128

EVEN_MIX = A_WIDTH + S5_WIDTH
W_IN_EVEN = 3 * A_WIDTH + S5_WIDTH + A_WIDTH + S5_WIDTH
W_IN_ODD = 3 * C_WIDTH + C_WIDTH + C_HEADS
N_EVEN = (DEPTH_2 + 1) // 2
N_ODD = DEPTH_2 // 2
EPS = 1e-6


def rmsnorm(x, g):
    xf = x.astype(jnp.float32)
    y = xf * lax.rsqrt(jnp.mean(xf * xf, axis=-1, keepdims=True) + EPS)
    return (y * g.astype(jnp.float32)).astype(x.dtype)

def chunked_relpos_attention(q, k, v, rel_bias):
    b, l, h, dh = q.shape
    nc = l // CHUNK
    qc = q.reshape(b, nc, CHUNK, h, dh)
    pad = ((0, 0), (N_LEFT_CHUNKS, 0), (0, 0), (0, 0), (0, 0))
    kc = jnp.pad(k.reshape(b, nc, CHUNK, h, dh), pad)
    vc = jnp.pad(v.reshape(b, nc, CHUNK, h, dh), pad)
    band_idx = jnp.arange(nc)[:, None] + jnp.arange(N_LEFT_CHUNKS + 1)[None, :]
    kb = jnp.take(kc, band_idx, axis=1).reshape(b, nc, BAND, h, dh)
    vb = jnp.take(vc, band_idx, axis=1).reshape(b, nc, BAND, h, dh)
    scale = 1.0 / math.sqrt(dh)
    s = jnp.einsum('bcqhd,bckhd->bhcqk', qc, kb).astype(jnp.float32) * scale
    rel = jnp.arange(CHUNK)[:, None] + N_LEFT_CHUNKS * CHUNK - jnp.arange(BAND)[None, :]
    rel_idx = jnp.clip(rel, -MAX_REL, MAX_REL) + MAX_REL
    bias = rel_bias.astype(jnp.float32)[:, rel_idx]
    key_chunk = jnp.arange(nc)[:, None] - N_LEFT_CHUNKS + jnp.arange(BAND)[None, :] // CHUNK
    valid = key_chunk >= 0
    s = s + bias[None, :, None]
    s = jnp.where(valid[None, None, :, None, :], s, -jnp.inf)
    p = jax.nn.softmax(s, axis=-1).astype(v.dtype)
    o = jnp.einsum('bhcqk,bckhd->bcqhd', p, vb)
    return o.reshape(b, l, h * dh)

def s5_ssm(u, lam_re, lam_im, log_dt, b_re, b_im, c_re, c_im, d_skip):
    bsz, l, _ = u.shape
    uf = u.astype(jnp.float32).reshape(bsz, l, S5_GROUPS, S5_GROUP)
    lr = lam_re.astype(jnp.float32)
    li = lam_im.astype(jnp.float32)
    dt = jnp.exp(log_dt.astype(jnp.float32))[:, None]
    mag = jnp.exp(lr * dt)
    ang = li * dt
    a_re = mag * jnp.cos(ang)
    a_im = mag * jnp.sin(ang)
    den = lr * lr + li * li
    nr = a_re - 1.0
    ni = a_im
    coef_re = (nr * lr + ni * li) / den
    coef_im = (ni * lr - nr * li) / den
    br = b_re.astype(jnp.float32)
    bi = b_im.astype(jnp.float32)
    bb_re = coef_re[..., None] * br - coef_im[..., None] * bi
    bb_im = coef_re[..., None] * bi + coef_im[..., None] * br
    bu_re = jnp.einsum('blgc,gpc->blgp', uf, bb_re)
    bu_im = jnp.einsum('blgc,gpc->blgp', uf, bb_im)
    a_re_t = jnp.broadcast_to(a_re, (1, l, S5_GROUPS, S5_STATE))
    a_im_t = jnp.broadcast_to(a_im, (1, l, S5_GROUPS, S5_STATE))

    def combine(e1, e2):
        ar1, ai1, xr1, xi1 = e1
        ar2, ai2, xr2, xi2 = e2
        return (ar2 * ar1 - ai2 * ai1,
                ar2 * ai1 + ai2 * ar1,
                ar2 * xr1 - ai2 * xi1 + xr2,
                ar2 * xi1 + ai2 * xr1 + xi2)

    _, _, xr, xi = lax.associative_scan(combine, (a_re_t, a_im_t, bu_re, bu_im), axis=1)
    y = (jnp.einsum('blgp,gcp->blgc', xr, c_re.astype(jnp.float32))
         - jnp.einsum('blgp,gcp->blgc', xi, c_im.astype(jnp.float32))
         + d_skip.astype(jnp.float32) * uf)
    return y.reshape(bsz, l, S5_WIDTH)

def forgetting_attention(q, k, v, log_f):
    b, l, h, dh = q.shape
    nqb = l // Q_BLOCK
    cum = jnp.cumsum(log_f, axis=1).transpose(0, 2, 1)
    qb = q.reshape(b, nqb, Q_BLOCK, h, dh).transpose(1, 0, 3, 2, 4)
    cq = cum.reshape(b, h, nqb, Q_BLOCK).transpose(2, 0, 1, 3)
    kpos = jnp.arange(l)
    scale = 1.0 / math.sqrt(dh)

    def block(args):
        qi, cqi, bi = args
        s = jnp.einsum('bhqd,bkhd->bhqk', qi, k).astype(jnp.float32) * scale
        s = s + cqi[..., None] - cum[:, :, None, :]
        qpos = bi * Q_BLOCK + jnp.arange(Q_BLOCK)
        s = jnp.where(kpos[None, :] <= qpos[:, None], s, -jnp.inf)
        p = jax.nn.softmax(s, axis=-1).astype(v.dtype)
        return jnp.einsum('bhqk,bkhd->bqhd', p, v)

    o = lax.map(block, (qb, cq, jnp.arange(nqb)))
    return o.transpose(1, 0, 2, 3, 4).reshape(b, l, h * dh)

def even_layer(x, norm_g, w_in, rel_bias, lam_re, lam_im, log_dt, b_re, b_im,
               c_re, c_im, d_skip, w_glu, b_glu, w_out):
    bsz, l, _ = x.shape
    hn = rmsnorm(x, norm_g)
    proj = hn @ w_in
    cuts = [A_WIDTH, 2 * A_WIDTH, 3 * A_WIDTH, 3 * A_WIDTH + S5_WIDTH,
            4 * A_WIDTH + S5_WIDTH]
    q, k, v, u, z_a, z_b = jnp.split(proj, cuts, axis=-1)
    shp = (bsz, l, A_HEADS, A_HEAD_DIM)
    o_a = chunked_relpos_attention(q.reshape(shp), k.reshape(shp), v.reshape(shp), rel_bias)
    o_a = o_a * jax.nn.silu(z_a)
    y = jax.nn.gelu(s5_ssm(u, lam_re, lam_im, log_dt, b_re, b_im, c_re, c_im, d_skip).astype(x.dtype))
    o_b = y * jax.nn.sigmoid(y @ w_glu + b_glu)
    o_b = o_b * jax.nn.silu(z_b)
    return x + jnp.concatenate([o_a, o_b], axis=-1) @ w_out

def odd_layer(x, norm_g, w_in, b_forget, w_out):
    bsz, l, _ = x.shape
    hn = rmsnorm(x, norm_g)
    proj = hn @ w_in
    cuts = [C_WIDTH, 2 * C_WIDTH, 3 * C_WIDTH, 4 * C_WIDTH]
    q, k, v, z, f_logit = jnp.split(proj, cuts, axis=-1)
    log_f = jax.nn.log_sigmoid((f_logit + b_forget).astype(jnp.float32))
    shp = (bsz, l, C_HEADS, C_HEAD_DIM)
    o = forgetting_attention(q.reshape(shp), k.reshape(shp), v.reshape(shp), log_f)
    o = o * jax.nn.silu(z)
    return x + o @ w_out

def second_inputs(seed: int = 0) -> dict:
    key = jax.random.key(seed)
    ks = jax.random.split(key, 20)
    f32 = jnp.float32
    x = jax.random.normal(ks[0], (BATCH, SEQ, D_MODEL), f32)
    norm_even_g = 1.0 + 0.05 * jax.random.normal(ks[1], (N_EVEN, D_MODEL), f32)
    w_in_even = jax.random.normal(ks[2], (N_EVEN, D_MODEL, W_IN_EVEN), f32) * D_MODEL ** -0.5
    rel_bias = 0.2 * jax.random.normal(ks[3], (N_EVEN, A_HEADS, N_REL), f32)
    n = jnp.arange(S5_STATE, dtype=f32)
    s5_lambda_re = -0.5 + 0.01 * jax.random.normal(ks[4], (N_EVEN, S5_GROUPS, S5_STATE), f32)
    s5_lambda_im = math.pi * n + 0.01 * jax.random.normal(ks[5], (N_EVEN, S5_GROUPS, S5_STATE), f32)
    s5_log_dt = jax.random.uniform(ks[6], (N_EVEN, S5_GROUPS), f32,
                                   math.log(DT_MIN), math.log(DT_MAX))
    s5_b_re = jax.random.normal(ks[7], (N_EVEN, S5_GROUPS, S5_STATE, S5_GROUP), f32) * (2 * S5_GROUP) ** -0.5
    s5_b_im = jax.random.normal(ks[8], (N_EVEN, S5_GROUPS, S5_STATE, S5_GROUP), f32) * (2 * S5_GROUP) ** -0.5
    s5_c_re = jax.random.normal(ks[9], (N_EVEN, S5_GROUPS, S5_GROUP, S5_STATE), f32) * (2 * S5_STATE) ** -0.5
    s5_c_im = jax.random.normal(ks[10], (N_EVEN, S5_GROUPS, S5_GROUP, S5_STATE), f32) * (2 * S5_STATE) ** -0.5
    s5_d = 0.5 * jax.random.normal(ks[11], (N_EVEN, S5_GROUPS, S5_GROUP), f32)
    w_glu = jax.random.normal(ks[12], (N_EVEN, S5_WIDTH, S5_WIDTH), f32) * S5_WIDTH ** -0.5
    b_glu = 0.02 * jax.random.normal(ks[13], (N_EVEN, S5_WIDTH), f32)
    w_out_even = jax.random.normal(ks[14], (N_EVEN, EVEN_MIX, D_MODEL), f32) * EVEN_MIX ** -0.5
    norm_odd_g = 1.0 + 0.05 * jax.random.normal(ks[15], (N_ODD, D_MODEL), f32)
    w_in_odd = jax.random.normal(ks[16], (N_ODD, D_MODEL, W_IN_ODD), f32) * D_MODEL ** -0.5
    b_forget = jax.random.uniform(ks[17], (N_ODD, C_HEADS), f32, 1.0, 4.0)
    w_out_odd = jax.random.normal(ks[18], (N_ODD, C_WIDTH, D_MODEL), f32) * C_WIDTH ** -0.5
    final_norm_g = 1.0 + 0.05 * jax.random.normal(ks[19], (D_MODEL,), f32)
    return {"x": x, "norm_even_g": norm_even_g, "w_in_even": w_in_even, "rel_bias": rel_bias,
            "s5_lambda_re": s5_lambda_re, "s5_lambda_im": s5_lambda_im, "s5_log_dt": s5_log_dt,
            "s5_b_re": s5_b_re, "s5_b_im": s5_b_im, "s5_c_re": s5_c_re, "s5_c_im": s5_c_im,
            "s5_d": s5_d, "w_glu": w_glu, "b_glu": b_glu, "w_out_even": w_out_even,
            "norm_odd_g": norm_odd_g, "w_in_odd": w_in_odd, "b_forget": b_forget,
            "w_out_odd": w_out_odd, "final_norm_g": final_norm_g}

def second_block(x, norm_even_g, w_in_even, rel_bias, s5_lambda_re, s5_lambda_im, s5_log_dt,
              s5_b_re, s5_b_im, s5_c_re, s5_c_im, s5_d, w_glu, b_glu, w_out_even,
              norm_odd_g, w_in_odd, b_forget, w_out_odd, final_norm_g):
    for layer in range(DEPTH_2):
        i = layer // 2
        if layer % 2 == 0:
            x = even_layer(x, norm_even_g[i], w_in_even[i], rel_bias[i], s5_lambda_re[i],
                           s5_lambda_im[i], s5_log_dt[i], s5_b_re[i], s5_b_im[i], s5_c_re[i],
                           s5_c_im[i], s5_d[i], w_glu[i], b_glu[i], w_out_even[i])
        else:
            x = odd_layer(x, norm_odd_g[i], w_in_odd[i], b_forget[i], w_out_odd[i])
    return rmsnorm(x, final_norm_g)


def setup_inputs(seed=0):
    out = dict(first_inputs(seed))
    for name, value in second_inputs(seed + 1).items():
        if name != "x":
            out[name + "_2"] = value
    return out


def reference(
    x, norm_g, w_in, mu_a, w_up, w0, a_up, a0, k_k, k_a, r_k, gn_g, gn_b, pool_w, pool_scale,
    qn_g, kn_g, w_out, norm_even_g_2, w_in_even_2, rel_bias_2, s5_lambda_re_2, s5_lambda_im_2,
    s5_log_dt_2, s5_b_re_2, s5_b_im_2, s5_c_re_2, s5_c_im_2, s5_d_2, w_glu_2, b_glu_2,
    w_out_even_2, norm_odd_g_2, w_in_odd_2, b_forget_2, w_out_odd_2, final_norm_g_2,
):
    x = first_block(
        x, norm_g, w_in, mu_a, w_up, w0, a_up, a0, k_k, k_a, r_k, gn_g, gn_b, pool_w,
        pool_scale, qn_g, kn_g, w_out,
    )
    return second_block(
        x, norm_even_g_2, w_in_even_2, rel_bias_2, s5_lambda_re_2, s5_lambda_im_2, s5_log_dt_2,
        s5_b_re_2, s5_b_im_2, s5_c_re_2, s5_c_im_2, s5_d_2, w_glu_2, b_glu_2, w_out_even_2,
        norm_odd_g_2, w_in_odd_2, b_forget_2, w_out_odd_2, final_norm_g_2,
    )


_drawn_inputs = setup_inputs


def setup_inputs(seed=0):
    import zlib

    import numpy as np

    out = dict(_drawn_inputs(seed))
    spreads = {}
    factors = {'k_k': 7.946,
     'norm_even_g_2': 8.0,
     'w_in_even_2': 8.0,
     'rel_bias_2': 8.0,
     's5_lambda_re_2': 64.0,
     's5_lambda_im_2': 64.0,
     's5_log_dt_2': 64.0,
     's5_b_re_2': 64.0,
     's5_b_im_2': 64.0,
     's5_c_re_2': 64.0,
     's5_c_im_2': 64.0,
     's5_d_2': 8.0,
     'w_glu_2': 8.0,
     'b_glu_2': 30.462,
     'w_out_even_2': 8.0,
     'norm_odd_g_2': 8.0,
     'w_in_odd_2': 8.0,
     'b_forget_2': 8.0,
     'w_out_odd_2': 8.0}
    for name, (base, spread) in spreads.items():
        noise = np.random.default_rng([zlib.crc32(name.encode()), seed]).standard_normal(out[name].shape)
        drawn = base * np.exp(spread * noise) if base else spread * noise
        out[name] = __import__('jax').numpy.asarray(drawn.astype(out[name].dtype))
    for name, factor in factors.items():
        out[name] = (out[name] * factor).astype(out[name].dtype)
    return out
```

```python
from contextlib import ExitStack

import numpy as np

import concourse.bass as bass
from concourse import mybir

F32 = mybir.dt.float32
F32R = mybir.dt.float32r
ACT = mybir.ActivationFunctionType
ALU = mybir.AluOpType
AX = mybir.AxisListType

P = 128
T = 512
TB = T // P
D = 2048
KT = D // P
HK = KT // 2

RW_PAIRS, POOL_GROUPS, SB_PAIRS, EV_PAIRS, ODD_HEADS = 6, 4, 6, 8, 16
N_WDAD = 0
N_RWKV = 1
N_POOL = N_RWKV + 4 * RW_PAIRS
N_SB = N_POOL + 2 * POOL_GROUPS
N_OUT1 = N_SB + 4 * SB_PAIRS
N_U = N_OUT1 + KT
N_EVEN = N_U + 8
N_ZB = N_EVEN + 4 * EV_PAIRS
N_GLU = N_ZB + 8
N_OUT2 = N_GLU + 4
N_F = N_OUT2 + KT
N_ODD = N_F + 1
N_OUT3 = N_ODD + 4 * ODD_HEADS
N_TILES = N_OUT3 + KT

NEG = -1.0e30
RMS_EPS = 1e-6
GN_EPS = 64e-5

PRM_G = 0
PRM_MU_WDAD = PRM_G + 4 * KT
PRM_RW = PRM_MU_WDAD + 1
RW_MU, RW_W0, RW_A0, RW_KK, RW_KA, RW_RK, RW_GNG, RW_GNB, RW_COLS = 0, 4, 5, 6, 7, 8, 9, 10, 11
PRM_POOL = PRM_RW + 6 * RW_COLS
PRM_QN = PRM_POOL + POOL_GROUPS
PRM_KN = PRM_QN + 1
PRM_LRE = PRM_KN + 1
PRM_LIM = PRM_LRE + 32
PRM_LDT = PRM_LIM + 32
PRM_SD = PRM_LDT + 32
PRM_BGLU = PRM_SD + 8
PRM_BF = PRM_BGLU + 8
PRM_COLS = PRM_BF + 1

C_IDENT = 0
C_HEAD = C_IDENT + P
C_ONES = C_HEAD + P
C_SB = C_ONES + P
C_INV = C_SB + 4 * P
C_RW = C_INV + 4 * 16
C_RW_MASK = C_RW
C_RW_LEVEL = C_RW_MASK + 2 * P
C_RW_CHUNK = C_RW_LEVEL + 6 * P
C_ODD = C_RW_CHUNK + T
C_TIME = C_ODD + P
C_FLIP = C_TIME + T
C_COLS = C_FLIP + P
CHUNK = 64


def constants():
    c = np.zeros((P, C_COLS), np.float32)
    i, j = np.arange(P)[:, None], np.arange(P)[None, :]
    c[:, C_IDENT:C_IDENT + P] = i == j
    c[:, C_HEAD:C_HEAD + P] = i // 64 == j // 64
    c[:, C_ONES:C_ONES + P] = 1
    c[:, C_SB:C_SB + P] = i < j
    c[:, C_SB + P:C_SB + 2 * P] = np.where(i < j, 0, NEG)
    c[:, C_SB + 2 * P:C_SB + 3 * P] = -(i >= j).astype(np.float32)
    c[:, C_SB + 3 * P:C_SB + 4 * P] = -1
    for g in range(4):
        c[:, C_INV + 16 * g:C_INV + 16 * g + 16] = 1.0 / np.minimum(np.arange(1, 17), 2 << g)
    same = i // CHUNK == j // CHUNK
    c[:, C_RW_MASK:C_RW_MASK + P] = same & (i < j)
    c[:, C_RW_MASK + P:C_RW_MASK + 2 * P] = same & (i <= j)
    for lv in range(6):
        c[:, C_RW_LEVEL + lv * P:C_RW_LEVEL + (lv + 1) * P] = (
            (i >> (lv + 1) == j >> (lv + 1)) & ((i >> lv) % 2 == 0) & ((j >> lv) % 2 == 1))
    c[:, C_RW_CHUNK:C_RW_CHUNK + T] = np.arange(T) % CHUNK != 0
    c[:, C_ODD:C_ODD + P] = np.where(j > i, NEG, 0)
    c[:, C_TIME:C_TIME + T] = np.arange(1, T + 1)
    c[:, C_FLIP:C_FLIP + P] = i + j == P - 1
    return c


def slots(arena, first, count=1):
    return arena[:, first * T:(first + count) * T]


class Order:

    def __init__(self, eng, sem, base=0):
        self.eng, self.sem, self.base, self.turn, self.per, self.k = eng, sem, base, 0, 0, 0

    def loop(self, turn, per):
        self.turn, self.per, self.k = turn, per, 0

    def check(self):
        assert self.k == self.per, f"{self.k} increments, not {self.per}"

    def done(self, ins):
        ins.then_inc(self.sem, 1)
        self.k += 1
        return self.turn * self.per + (self.base + self.k)

    def then(self, ins):
        self.eng.wait_ge(self.sem, self.done(ins))


class Steps:

    def __init__(self, sem, names):
        self.sem, self.names = sem, names.split()
        assert len(set(self.names)) == len(self.names)

    def start(self, unit):
        self.unit, self.k = unit, 0

    def mark(self, ins, name):
        assert self.names[self.k] == name, (self.names[self.k], name)
        ins.then_inc(self.sem, 1)
        self.k += 1

    def finish(self):
        assert self.k == len(self.names), self.names[self.k]

    def wait(self, eng, name, unit):
        eng.wait_ge(self.sem, unit * len(self.names) + (self.names.index(name) + 1))

    def wait_before(self, eng, unit):
        if not (isinstance(unit, int) and unit == 0):
            eng.wait_ge(self.sem, unit * len(self.names))


def build_program(nc, stream, x, params, consts, rel_bias, lora, pool_w, s5_b, s5_c, out):
    with ExitStack() as ctx:
        def sb(name, shape, dt=F32):
            return ctx.enter_context(nc.sbuf_tensor(name, shape, dt))

        def sem(name):
            return ctx.enter_context(nc.semaphore(name))

        act_hi = sb("act_hi", [P, KT, T], F32R)
        act_lo = sb("act_lo", [P, KT, T], F32R)
        mix = sb("mix", [P, KT * T])
        raw = sb("raw", [P, 2, HK, P])
        w_hi = sb("w_hi", [P, 4, HK, P], F32R)
        w_lo = sb("w_lo", [P, 4, HK, P], F32R)
        arena = sb("arena", [P, 30 * T])
        ident = sb("ident", [P, P])
        head_ones = sb("head_ones", [P, P])
        ones = sb("ones", [P, P])
        prm = sb("prm", [P, PRM_COLS])
        eps = sb("eps", [P, 8])
        ps = ctx.enter_context(nc.psum_tensor("ps", [P, 8, T], F32))
        psf = ps[:, :, :].rearrange("p b t -> p (b t)")
        residual = nc.dram_tensor("residual", (KT, P, T), F32, kind="Internal").ap()

        raw_loaded = [sem("raw_loaded0"), sem("raw_loaded1")]
        cast_done = sem("cast_done")
        split_done = sem("split_done")
        pe_half = sem("pe_half")
        evac_act = sem("evac_act")
        evac_dve = sem("evac_dve")
        consts_loaded = sem("consts_loaded")
        eps_set = sem("eps_set")
        x_loaded = sem("x_loaded")
        x_turned = sem("x_turned")
        x_tile = sem("x_tile")
        res_stored = sem("res_stored")
        res_loaded = [sem("res_loaded0"), sem("res_loaded1")]
        norm_sq = sem("norm_sq")
        norm_mm = sem("norm_mm")
        norm_root = sem("norm_root")
        norm_rstd = sem("norm_rstd")
        norm_t = sem("norm_t")
        norm_hi = sem("norm_hi")
        norm_lo = sem("norm_lo")
        mix_hi = sem("mix_hi")
        mix_lo = sem("mix_lo")
        met = sem("met")
        sb_const = sem("sb_const")
        sb_sq = sem("sb_sq")
        sb_sum = sem("sb_sum")
        sb_root = sem("sb_root")
        sb_rec = sem("sb_rec")
        sb_qk = sem("sb_qk")
        sb_turn = sem("sb_turn")
        sb_vn = sem("sb_vn")
        sb_z = sem("sb_z")
        sb_dve = sem("sb_dve")
        sb_n = sem("sb_n")
        sb_e = sem("sb_e")
        sb_l = sem("sb_l")
        sb_sp = sem("sb_sp")
        sb_tri = sem("sb_tri")
        sb_neg = sem("sb_neg")
        sb_w = sem("sb_w")
        sb_pv = sem("sb_pv")
        sb_mix = sem("sb_mix")
        pl_dve = sem("pl_dve")
        pl_const = sem("pl_const")
        pl_d = sem("pl_d")
        pl_y = sem("pl_y")
        pl_mix = sem("pl_mix")
        out_t = sem("out_t")
        out_turned = sem("out_turned")
        out_copied = sem("out_copied")
        out_stored = sem("out_stored")

        block = ctx.enter_context(nc.Block())

        def meet(eng, k):
            eng.drain().then_inc(met, 1)
            eng.wait_ge(met, 3 * k)

        @block.sync
        def _(sp):
            sp.dma_start(ident[:], consts[:, C_IDENT:C_IDENT + P]).then_inc(consts_loaded, 16)
            sp.dma_start(head_ones[:], consts[:, C_HEAD:C_HEAD + P]).then_inc(consts_loaded, 16)
            sp.dma_start(ones[:], consts[:, C_ONES:C_ONES + P]).then_inc(consts_loaded, 16)
            sp.dma_start(prm[:], params).then_inc(consts_loaded, 16)

            def load(tile, h):
                return sp.dma_start(raw[:, h, :, :].rearrange("p k c -> p (k c)"),
                                    stream[bass.ds(tile, 1), h, :, :].rearrange("a p w -> (a p) w"))
            load(0, 0).then_inc(raw_loaded[0], 16)
            load(0, 1).then_inc(raw_loaded[1], 16)
            with sp.Fori(1, N_TILES) as n:
                for h in range(2):
                    sp.wait_ge(split_done, n * 2 + h - 1)
                    load(n, h).then_inc(raw_loaded[h], 16)

        @block.gpsimd
        def _(pool):
            for c, v in enumerate((64 * RMS_EPS, RMS_EPS, GN_EPS, 1.0, np.pi / 2)):
                last = nc.gpsimd.memset(eps[:, c:c + 1], float(v))
            last.then_inc(eps_set, 1)
            with pool.Fori(0, N_TILES // 2) as i:
                for s in range(4):
                    pool.wait_ge(cast_done, i * 4 + s + 1)
                    nc.gpsimd.tensor_tensor(w_lo[:, s, :, :], raw[:, s % 2, :, :],
                                            w_hi[:, s, :, :].bitcast(F32),
                                            ALU.subtract).then_inc(split_done, 1)

        def gemm(pe, n, par, free=None, act_ready=None, halves=(0, 1), outputs=1):
            for h in halves:
                if h == 0 or outputs == 2:
                    if free is not None:
                        pe.wait_ge(free[0], free[1] + (h if outputs == 2 else 0))
                bank = h if outputs == 2 else par
                slot = 2 * par + h
                pe.wait_ge(split_done, n * 2 + h + 1)
                for j in range(HK):
                    kt = j if outputs == 2 else HK * h + j
                    if act_ready is not None and (outputs == 1 or h == 0):
                        pe.wait_ge(act_ready[0], act_ready[1] + kt + 1)
                    dst = ps[:, bank, :]
                    first = kt == 0
                    last = kt == (HK - 1 if outputs == 2 else KT - 1)
                    pe.matmul(dst, w_hi[:, slot, j, :], act_hi[:, kt, :], start=first, stop=False)
                    pe.matmul(dst, w_lo[:, slot, j, :], act_hi[:, kt, :], start=False, stop=False)
                    mm = pe.matmul(dst, w_hi[:, slot, j, :], act_lo[:, kt, :], start=False,
                                   stop=last)
                mm.then_inc(pe_half, 1)

        sq = [slots(arena, 24), slots(arena, 25)]
        root, rstd = slots(arena, 26), slots(arena, 27)
        norm_in = [slots(arena, 28), slots(arena, 29)]
        res_in = [slots(arena, 22), slots(arena, 23)]

        def mix_tile(ft):
            return mix[:, bass.ds(ft * T, T)] if not isinstance(ft, int) else mix[:, ft * T:(ft + 1) * T]

        def norm_mm_tensor(pe, norm, ft, slot, first=False, last=False):
            pe.wait_ge(norm_sq, ft + (KT * norm + 1))
            pe.matmul(ps[:, 7, :], ones[:], sq[slot], start=first,
                      stop=last, skip_group_check=True).then_inc(norm_mm, 1)

        def out_tensor(pe, layer, n0, before):
            for ft in (0, 1):
                gemm(pe, n0 + ft, (n0 + ft) % 2, free=(evac_act, before),
                     act_ready=(mix_lo, KT * layer) if ft == 0 else None)
            norm_mm_tensor(pe, layer + 1, 0, 0, first=True)
            with pe.Fori(1, KT // 2) as two:
                ft = two * 2
                for j in range(2):
                    gemm(pe, ft + (n0 + j), (n0 + j) % 2, free=(evac_dve, ft + (KT * layer + j - 1)))
                    norm_mm_tensor(pe, layer + 1, ft + (j - 1), (j + 1) % 2)
            norm_mm_tensor(pe, layer + 1, KT - 1, 1, last=True)

        def out_vector(dve, layer, n0):
            with dve.Fori(0, KT // 2) as two:
                ft = two * 2
                for j in range(2):
                    dve.wait_ge(res_loaded[j], ft * 8 + (16 * 8 * layer + 16))
                    dve.wait_ge(pe_half, ft * 2 + (2 * (n0 + j) + 2))
                    nc.vector.tensor_tensor(mix_tile(ft + j), ps[:, (n0 + j) % 2, :], res_in[j],
                                            ALU.add).then_inc(evac_dve, 1)

        def res_load(act, ft, j):
            return act.dma_start(res_in[j], residual[bass.ds(ft, 1), :, :].rearrange("a p t -> (a p) t"))

        def res_store(act, ft):
            return act.dma_start(residual[bass.ds(ft, 1), :, :].rearrange("a p t -> (a p) t"), mix_tile(ft))

        def square(act, norm, ft, j):
            if not (isinstance(ft, int) and ft < 2):
                act.wait_ge(norm_mm, ft + (KT * norm - 1))
            nc.scalar.activation(sq[j], mix_tile(ft), ACT.Square).then_inc(norm_sq, 1)

        def out_scalar(act, layer, n0):
            last_layer = layer == 2
            act.wait_ge(res_stored, 16 * KT * (layer + 1))
            for j in range(2):
                res_load(act, j, j).then_inc(res_loaded[j], 16)

            def tile(ft, j, more=True):
                if more:
                    cast(act, ft * 2 + 2 * (n0 + j + 2), (2 * (n0 + j)) % 4)
                act.wait_ge(evac_dve, ft + (KT * layer + j + 1))
                square(act, layer + 1, ft + j, j)
                if not last_layer:
                    res_store(act, ft + j).then_inc(res_stored, 16)
                if more:
                    cast(act, ft * 2 + (2 * (n0 + j + 2) + 1), (2 * (n0 + j) + 1) % 4)

            for j in range(2):
                tile(0, j)
                res_load(act, 2 + j, j).then_inc(res_loaded[j], 16)
            with act.Fori(1, KT // 2 - 1) as two:
                ft = two * 2
                for j in range(2):
                    tile(ft, j)
                    res_load(act, ft + 2 + j, j).then_inc(res_loaded[j], 16)
            for j in range(2):
                tile(KT - 2, j, more=not last_layer)
            if not last_layer:
                act.wait_ge(res_stored, 16 * KT * (layer + 2))

        def mix_split_scalar(act, layer):
            act.wait_ge(pe_half, 2 * (N_OUT1, N_OUT2, N_OUT3)[layer])
            with act.Fori(0, KT) as ft:
                nc.scalar.activation(act_hi[:, bass.ds(ft, 1), :].rearrange("p a t -> p (a t)"),
                                     mix_tile(ft), ACT.Copy).then_inc(mix_hi, 1)

        def mix_split_vector(dve, layer):
            with dve.Fori(0, KT) as ft:
                dve.wait_ge(mix_hi, ft + (KT * layer + 1))
                nc.vector.tensor_tensor(act_lo[:, bass.ds(ft, 1), :].rearrange("p a t -> p (a t)"),
                                        mix_tile(ft),
                                        act_hi[:, bass.ds(ft, 1), :].rearrange("p a t -> p (a t)").bitcast(F32),
                                        ALU.subtract).then_inc(mix_lo, 1)

        def norm_scalar(act, norm):
            act.wait_ge(norm_mm, KT * (norm + 1))
            nc.scalar.activation(root, ps[:, 7, :], ACT.Sqrt, bias=eps[:, 1:2],
                                 scale=1.0 / D).then_inc(norm_root, 1)
            if norm == 3:
                return
            with act.Fori(0, KT // 2) as two:
                ft = two * 2
                for j in range(2):
                    act.wait_ge(norm_t, ft + (KT * norm + j + 1))
                    nc.scalar.activation(act_hi[:, bass.ds(ft + j, 1), :].rearrange("p a t -> p (a t)"),
                                         norm_in[j], ACT.Copy).then_inc(norm_hi, 1)

        def norm_vector(dve, norm):
            dve.wait_ge(norm_root, norm + 1)
            nc.vector.reciprocal(rstd, root).then_inc(norm_rstd, 1)
            dve.wait_ge(norm_rstd, norm + 1)
            with dve.Fori(0, KT // 2) as two:
                ft = two * 2
                for j in range(2):
                    if norm == 3:
                        dve.wait_ge(out_turned, ft + j)
                    else:
                        dve.wait_ge(norm_lo, ft + KT * norm)
                    nc.vector.scalar_tensor_tensor(
                        out=norm_in[j], in0=mix_tile(ft + j), scalar=prm[:, bass.ds(ft + (PRM_G + KT * norm + j), 1)],
                        in1=rstd, op0=ALU.mult, op1=ALU.mult).then_inc(norm_t, 1)
                if norm < 3:
                    for j in range(2):
                        dve.wait_ge(norm_hi, ft + (KT * norm + j + 1))
                        nc.vector.tensor_tensor(
                            act_lo[:, bass.ds(ft + j, 1), :].rearrange("p a t -> p (a t)"), norm_in[j],
                            act_hi[:, bass.ds(ft + j, 1), :].rearrange("p a t -> p (a t)").bitcast(F32),
                            ALU.subtract).then_inc(norm_lo, 1)

        def cast(act, m, s):
            act.wait_ge(raw_loaded[s % 2], (m - s) * 8 + (16 * (s // 2) + 16))
            if not (isinstance(m, int) and m < 4):
                act.wait_ge(pe_half, m - 3)
            nc.scalar.activation(w_hi[:, s, :, :], raw[:, s % 2, :, :], ACT.Copy).then_inc(cast_done, 1)

        def taken(act, n, par, body):
            cast(act, n * 2 + 4, (2 * par) % 4)
            act.wait_ge(pe_half, n * 2 + 2)
            body().then_inc(evac_act, 1)
            cast(act, n * 2 + 5, (2 * par + 1) % 4)

        x_in = slots(arena, 0, 16).rearrange("p (b d) -> p b d", b=TB)

        def load_tensor(pe):
            pe.wait_ge(consts_loaded, 64)
            pe.wait_ge(x_loaded, 64)
            for ft in range(KT):
                if ft >= 2:
                    pe.wait_ge(x_tile, ft - 1)
                for b in range(TB):
                    mm = pe.transpose(ps[:, 2 + ft % 2, b * P:(b + 1) * P],
                                      x_in[:, b, ft * P:(ft + 1) * P], ident[:])
                mm.then_inc(x_turned, 1)
                if ft >= 1:
                    norm_mm_tensor(pe, 0, ft - 1, (ft - 1) % 2, first=ft == 1)
            norm_mm_tensor(pe, 0, KT - 1, 1, last=True)

        def load_vector(dve):
            for ft in range(KT):
                dve.wait_ge(x_turned, ft + 1)
                nc.vector.tensor_copy(mix_tile(ft), ps[:, 2 + ft % 2, :]).then_inc(x_tile, 1)

        def load_scalar(act):
            for b in range(TB):
                act.dma_start(x_in[:, b, :], x[b * P:(b + 1) * P, :]).then_inc(x_loaded, 16)
            act.wait_ge(eps_set, 1)
            for m in range(4):
                cast(act, m, m)
            for ft in range(KT):
                act.wait_ge(x_tile, ft + 1)
                if ft >= 2:
                    act.wait_ge(norm_mm, ft - 1)
                nc.scalar.activation(sq[ft % 2], mix_tile(ft), ACT.Square).then_inc(norm_sq, 1)
                res_store(act, ft).then_inc(res_stored, 16)
            act.wait_ge(res_stored, 16 * KT)

        pl_raw, pl_gate = slots(arena, 0), slots(arena, 1)
        pl_w = slots(arena, 2).rearrange("p (g d) -> p g d", g=POOL_GROUPS)
        pl_inv = slots(arena, 3)[:, 0:POOL_GROUPS * 16].rearrange("p (g t) -> p g t", g=POOL_GROUPS)
        pl_sum = [slots(arena, 4), slots(arena, 5)]
        pl_in = slots(arena, 6)
        pl_out = slots(arena, 7)

        def pool_tensor(pe):
            for g in range(POOL_GROUPS):
                for j in range(2):
                    n = N_POOL + 2 * g + j
                    gemm(pe, n, n % 2, free=(evac_act, n - 1))
                if g == 0:
                    pe.wait_ge(pl_const, 32)
                pe.wait_ge(pl_d, g + 1)
                if g >= 1:
                    pe.wait_ge(pl_mix, g)
                pe.matmul(ps[:, 2, :], pl_w[:, g, :], pl_in, start=True, stop=True).then_inc(pl_y, 1)

        def pool_scalar(act):
            act.dma_start(pl_w, pool_w.rearrange("g c d -> c g d")).then_inc(pl_const, 16)
            act.dma_start(slots(arena, 3)[:, 0:POOL_GROUPS * 16],
                          consts[:, C_INV:C_INV + POOL_GROUPS * 16]).then_inc(pl_const, 16)
            for g in range(POOL_GROUPS):
                n = N_POOL + 2 * g
                if g >= 1:
                    act.wait_ge(pl_d, g)
                taken(act, n, n % 2, lambda: nc.scalar.activation(pl_raw, ps[:, n % 2, :], ACT.Copy))
                if g >= 1:
                    act.wait_ge(pl_mix, g)
                n += 1
                taken(act, n, n % 2, lambda: nc.scalar.activation(pl_gate, ps[:, n % 2, :], ACT.Silu))

        def pool_vector(dve):
            order = Order(dve, pl_dve)
            dve.wait_ge(pl_const, 32)
            for g in range(POOL_GROUPS):
                window = 2 << g
                n = N_POOL + 2 * g
                dve.wait_ge(evac_act, n + 1)
                cur, shift, k = pl_raw, 1, 0
                while shift < window:
                    nxt = pl_sum[k % 2]
                    order.done(nc.vector.tensor_copy(nxt[:, 0:shift], cur[:, 0:shift]))
                    order.then(nc.vector.tensor_tensor(nxt[:, shift:T], cur[:, shift:T],
                                                       cur[:, 0:T - shift], ALU.add))
                    cur, shift, k = nxt, 2 * shift, k + 1
                if g >= 1:
                    dve.wait_ge(pl_y, g)
                mean = pl_sum[k % 2]
                order.done(nc.vector.tensor_tensor(mean[:, 0:16], cur[:, 0:16], pl_inv[:, g, :], ALU.mult))
                order.then(nc.vector.tensor_scalar(mean[:, 16:T], cur[:, 16:T], 1.0 / window, None, ALU.mult))
                nc.vector.tensor_tensor(pl_in, mean, pl_raw, ALU.subtract).then_inc(pl_d, 1)
                dve.wait_ge(pl_d, g + 1)
                dve.wait_ge(pl_y, g + 1)
                dve.wait_ge(evac_act, n + 2)
                nc.vector.scalar_tensor_tensor(
                    out=mix_tile(6 + g), in0=ps[:, 2, :], scalar=prm[:, PRM_POOL + g:PRM_POOL + g + 1],
                    in1=pl_gate, op0=ALU.mult, op1=ALU.mult).then_inc(pl_mix, 1)

        sq_q, sq_k = slots(arena, 7), slots(arena, 8)
        sb_q, sb_k, sb_v, sb_gate = (slots(arena, i) for i in range(4))
        sb_qn, sb_kn, sb_vt = (slots(arena, i) for i in range(4, 7))
        sb_rt = [slots(arena, 9), slots(arena, 10)]
        ZW = 1280
        sb_m, sb_l_, sb_spt, sb_wt = (slots(arena, i, 3)[:, 0:ZW] for i in (11, 14, 17, 20))
        sb_c = slots(arena, 23)
        c_valid, c_neg, c_ntri, c_nones = (sb_c[:, i * P:(i + 1) * P] for i in range(4))
        ZOFF = (0, 512, 1024, 896)
        zb = psf[:, 2 * T:2 * T + ZW]

        def diag(view, which):
            if which == 0:
                return view[:, 0:1152].rearrange("p (a b) -> p a b", b=128)[:, 0:9:4, :]
            return view[:, 896:1024].rearrange("p (a b) -> p a b", a=1)

        def sb_tensor(pe):
            pe.wait_ge(sb_const, 16)

            def unit(u, more):
                n = u * 4 + N_SB
                pe.wait_ge(sb_sq, u * 2 + 1)
                if not (isinstance(u, int) and u == 0):
                    pe.wait_ge(sb_mix, u)
                pe.matmul(ps[:, 5, :], head_ones[:], sq_q, start=True, stop=True).then_inc(sb_sum, 1)
                pe.wait_ge(sb_sq, u * 2 + 2)
                pe.matmul(ps[:, 6, :], head_ones[:], sq_k, start=True, stop=True).then_inc(sb_sum, 1)
                pe.wait_ge(evac_act, n + 3)
                for b in range(TB):
                    mm = pe.transpose(ps[:, 7, b * P:(b + 1) * P], sb_v[:, b * P:(b + 1) * P], ident[:])
                mm.then_inc(sb_turn, 1)
                for hd in range(2):
                    rows = slice(64 * hd, 64 * hd + 64)
                    if more:
                        gemm(pe, n + (4 + 2 * hd), 1, free=(evac_act, n + (3 + 2 * hd)))
                    pe.wait_ge(sb_qk, u * 2 + 2)
                    if not (isinstance(u, int) and u == 0 and hd == 0):
                        pe.wait_ge(sb_w, u * 2 + hd)
                    for kb in range(TB):
                        mm = pe.matmul(ps_z(kb, kb), sb_kn[rows, kb * P:(kb + 1) * P],
                                       sb_qn[rows, kb * P:T], start=kb != 3, stop=False,
                                       skip_group_check=True)
                    mm.then_inc(sb_z, 1)
                    if more:
                        gemm(pe, n + (5 + 2 * hd), 0, free=(evac_act, n + (4 + 2 * hd)))
                    pe.wait_ge(sb_sp, u * 4 + (2 * hd + 2))
                    for kb in range(TB):
                        for jb in range(kb, TB):
                            mm = pe.matmul(ps_z(kb, jb), c_ntri if jb == kb else c_nones,
                                           sb_spt[:, ZOFF[jb]:ZOFF[jb] + (TB - jb) * P],
                                           start=False, stop=True, skip_group_check=True)
                    mm.then_inc(sb_tri, 1)
                    pe.wait_ge(sb_vn, u + 1)
                    pe.wait_ge(sb_w, u * 2 + hd + 1)
                    for kb in range(TB):
                        mm = pe.matmul(ps[rows, 5, kb * P:T],
                                       sb_vt[:, kb * P + 64 * hd:kb * P + 64 * hd + 64],
                                       sb_wt[:, ZOFF[kb]:ZOFF[kb] + (TB - kb) * P],
                                       start=kb == 0, stop=kb == TB - 1, skip_group_check=True)
                    mm.then_inc(sb_pv, 1)

            def ps_z(kb, jb):
                return zb[:, ZOFF[kb] + (jb - kb) * P:ZOFF[kb] + (TB - kb) * P]

            for j in range(4):
                gemm(pe, N_SB + j, (N_SB + j) % 2, free=(evac_act, N_SB + j - 1))
            with pe.Fori(0, SB_PAIRS - 1) as u:
                unit(u, True)
            unit(SB_PAIRS - 1, False)

        def sb_scalar(act):
            def take(u, j):
                n = u * 4 + (N_SB + j)
                par = (N_SB + j) % 2
                if j < 3:
                    dst, fn = (sb_q, sb_k, sb_v)[j], ACT.Copy
                else:
                    dst, fn = sb_gate, ACT.Silu
                taken(act, n, par, lambda: nc.scalar.activation(dst, ps[:, par, :], fn))

            def unit(u, more):
                act.wait_ge(evac_act, u * 4 + (N_SB + 1))
                if not (isinstance(u, int) and u == 0):
                    act.wait_ge(sb_sum, u * 2)
                nc.scalar.activation(sq_q, sb_q, ACT.Square).then_inc(sb_sq, 1)
                act.wait_ge(evac_act, u * 4 + (N_SB + 2))
                nc.scalar.activation(sq_k, sb_k, ACT.Square).then_inc(sb_sq, 1)
                if not (isinstance(u, int) and u == 0):
                    act.wait_ge(sb_qk, u * 2)
                act.wait_ge(sb_sum, u * 2 + 1)
                nc.scalar.activation(sb_rt[0], ps[:, 5, :], ACT.Sqrt, bias=eps[:, 0:1],
                                     scale=1.0).then_inc(sb_root, 1)
                act.wait_ge(sb_sum, u * 2 + 2)
                nc.scalar.activation(sb_rt[1], ps[:, 6, :], ACT.Sqrt, bias=eps[:, 1:2],
                                     scale=1.0 / 64).then_inc(sb_root, 1)
                act.wait_ge(sb_turn, u + 1)
                if not (isinstance(u, int) and u == 0):
                    act.wait_ge(sb_pv, u * 2)
                nc.scalar.activation(sb_vt, ps[:, 7, :], ACT.Copy).then_inc(sb_vn, 1)
                for hd in range(2):
                    if more:
                        if hd == 0:
                            act.wait_ge(sb_qk, u * 2 + 1)
                            take(u + 1, 0)
                        else:
                            act.wait_ge(sb_vn, u + 1)
                            take(u + 1, 2)
                    act.wait_ge(sb_n, u * 2 + hd + 1)
                    if not (isinstance(u, int) and u == 0 and hd == 0):
                        act.wait_ge(sb_sp, u * 4 + 2 * hd)
                    nc.scalar.activation(sb_l_, sb_spt, ACT.Exp).then_inc(sb_e, 1)
                    act.wait_ge(sb_e, u * 2 + hd + 1)
                    nc.scalar.activation(sb_l_, sb_l_, ACT.Ln, bias=eps[:, 3:4]).then_inc(sb_l, 1)
                    if more:
                        if hd == 0:
                            act.wait_ge(sb_qk, u * 2 + 2)
                            take(u + 1, 1)
                    act.wait_ge(sb_neg, u * 4 + 2 * hd + 2)
                    if not (isinstance(u, int) and u == 0 and hd == 0):
                        act.wait_ge(sb_pv, u * 2 + hd)
                    nc.scalar.activation(sb_wt, zb, ACT.Exp).then_inc(sb_w, 1)
                if more:
                    act.wait_ge(sb_mix, u + 1)
                    take(u + 1, 3)

            act.dma_start(sb_c, consts[:, C_SB:C_SB + T]).then_inc(sb_const, 16)
            for j in range(4):
                take(0, j)
            with act.Fori(0, SB_PAIRS - 1) as u:
                unit(u, True)
            unit(SB_PAIRS - 1, False)

        def sb_vector(dve):
            dve.wait_ge(sb_const, 16)
            order = Order(dve, sb_dve)

            def unit(u):
                order.loop(u, 6)
                for i, (src, dst, g) in enumerate(((sb_q, sb_qn, PRM_QN), (sb_k, sb_kn, PRM_KN))):
                    dve.wait_ge(sb_root, u * 2 + i + 1)
                    order.then(nc.vector.reciprocal(sb_rt[i], sb_rt[i]))
                    if not (isinstance(u, int) and u == 0):
                        dve.wait_ge(sb_z, u * 2)
                    nc.vector.scalar_tensor_tensor(out=dst, in0=src, scalar=prm[:, g:g + 1], in1=sb_rt[i],
                                                   op0=ALU.mult, op1=ALU.mult).then_inc(sb_qk, 1)
                for hd in range(2):
                    dve.wait_ge(sb_z, u * 2 + hd + 1)
                    if not (isinstance(u, int) and u == 0 and hd == 0):
                        dve.wait_ge(sb_tri, u * 2 + hd)
                    order.then(nc.vector.tensor_scalar(sb_m, zb, 0.0, None, ALU.max))
                    nc.vector.scalar_tensor_tensor(out=sb_spt, in0=sb_m, scalar=-2.0, in1=zb,
                                                   op0=ALU.mult, op1=ALU.add).then_inc(sb_n, 1)
                    dve.wait_ge(sb_l, u * 2 + hd + 1)
                    order.then(nc.vector.tensor_tensor(sb_spt, sb_m, sb_l_, ALU.add))
                    for which, n in ((0, 3), (1, 1)):
                        d = diag(sb_spt, which)
                        ins = nc.vector.tensor_tensor(
                            d, d, c_valid.rearrange("p (a b) -> p a b", a=1).broadcast_to([P, n, P]), ALU.mult)
                        ins.then_inc(sb_sp, 1)
                    dve.wait_ge(sb_tri, u * 2 + hd + 1)
                    for which, n in ((0, 3), (1, 1)):
                        d = diag(zb, which)
                        nc.vector.tensor_tensor(
                            d, d, c_neg.rearrange("p (a b) -> p a b", a=1).broadcast_to([P, n, P]),
                            ALU.add).then_inc(sb_neg, 1)
                dve.wait_ge(sb_pv, u * 2 + 2)
                dve.wait_ge(evac_act, u * 4 + (N_SB + 4))
                nc.vector.tensor_tensor(mix_tile(u + 10), ps[:, 5, :], sb_gate, ALU.mult).then_inc(sb_mix, 1)
                order.check()

            with dve.Fori(0, SB_PAIRS - 1) as u:
                unit(u)
            unit(SB_PAIRS - 1)

        LEVELS = 6
        NB = T // P
        NC = T // CHUNK
        rw_pc = sb("rw_pc", [P, NC])
        rw_fold = sb("rw_fold", [P, CHUNK])
        rw_up = sb("rw_up", [P, P])
        rw_pre = sem("rw_pre")
        rw_folded = sem("rw_folded")
        rw_up_loaded = sem("rw_up_loaded")
        rw_consts = sem("rw_consts")
        dve_names = []
        for s_ in "rkvg":
            dve_names += [f"d_{s_}", f"d0_{s_}", f"s_{s_}"]
        dve_names += ["kk0", "cs", "csp", "t", "kn", "rk", "qr_r", "pc", "kdt", "kkmax", "kkrec", "kk", "qr_k",
                      "b", "bt", "bon", "ln0", "mq0", "ln1", "mq1"]
        for e in range(2):
            dve_names += [f"lt0_{e}"]
        for e in range(2):
            dve_names += [f"z0_{e}", f"x0_{e}"]
        for lv in range(1, LEVELS):
            dve_names += [f"lt{lv}_{e}" for e in range(2)]
            for e in range(2):
                dve_names += [f"z{lv}_{e}"] + ([f"x{lv}_{e}"] if lv < LEVELS - 1 else [])
        dve_names += ["zero", "at0_0", "at0_1", "f0", "at1_0", "at1_1", "f1"]
        dve_names += [f"st{c}" for c in range(1, NC - 1)]
        dve_names += ["rg", "yc", "vrec", "yn", "ynb", "mix"]
        rw_dve = Steps(sem("rw_dve"), " ".join(dve_names))
        rw_act = Steps(sem("rw_act"), "sg a gs kksq p pinv pprev kkroot n_kq n_b n_kd n_v "
                       + " ".join(f"u{lv}_{e}" for lv in range(1, LEVELS) for e in range(2))
                       + " mv gh0 gh1 y0 y1 ysq vroot")
        rw_pe = Steps(sem("rw_pe"), "w a kksum bonus t_kq t_b t_kd t_v ln0 mq0 ln1 mq1 u0_0 u0_1 "
                      + " ".join(f"u{lv}_0 u{lv}_1 xz{lv}_0 xz{lv}_1" for lv in range(1, LEVELS))
                      + " mv gh0 gh1 ng atf " + " ".join(f"st{c}" for c in range(1, NC - 1))
                      + " y mu var")

        def spare(i, count=1):
            return mix[:, (6 + i) * T:(6 + i + count) * T]

        rw_tw = slots(arena, 0)
        rw_raw = [slots(arena, 1 + j) for j in range(4)]
        rw_r, rw_k, rw_v, rw_gate = (slots(arena, 5 + j) for j in range(4))
        rw_tmp, rw_sg, rw_cs, rw_p, rw_pinv, rw_pprev, rw_a, rw_kk, rw_kn = (
            slots(arena, 9 + j) for j in range(9))
        rw_qr = slots(arena, 18, 2).rearrange("p (g a t) -> p g a t", g=NB, a=2)
        rw_bt, rw_kdt, rw_bon, rw_sq = (slots(arena, 20 + j) for j in range(4))
        rw_km = spare(0, 2).rearrange("p (e g a c) -> p e g a c", e=2, g=NB, a=2)
        rw_bn, rw_kdn, rw_vn = (spare(2 + j).rearrange("p (g c) -> p g c", g=NB) for j in range(3))
        rw_mask = spare(5)[:, 0:2 * P]
        rw_level = spare(6, 2)[:, 0:LEVELS * P]
        rw_chunk = spare(8)
        rw_ln = [slots(arena, 9 + 2 * e, 2).rearrange("p (g a t) -> p g a t", g=NB, a=2) for e in range(2)]
        rw_mq = [slots(arena, 13 + 2 * e, 2).rearrange("p (g a t) -> p g a t", g=NB, a=2) for e in range(2)]
        rw_x = [slots(arena, 24), slots(arena, 25)]
        rw_z = [slots(arena, 26), slots(arena, 27)]
        rw_u = [slots(arena, 28), slots(arena, 29)]
        rw_lt = [slots(arena, 17), slots(arena, 5)]
        rw_gh = [slots(arena, 6), slots(arena, 7)]
        rw_at = slots(arena, 24, 2).rearrange("p (c w) -> p c w", c=NC)
        rw_state = slots(arena, 20).rearrange("p (c w) -> p c w", c=NC)
        rw_rg, rw_y = slots(arena, 28), slots(arena, 29)
        rw_yc, rw_ysq, rw_vr = slots(arena, 24), slots(arena, 26), slots(arena, 27)

        def blocks(view):
            return view.rearrange("p (g t) -> p g t", g=NB)

        def over_blocks(view, width):
            return view.rearrange("p (a w) -> p a w", a=1).broadcast_to([P, NB, width])

        def rw_col(u, j):
            return prm[:, bass.ds(u * RW_COLS + (PRM_RW + j), 1)] if not isinstance(u, int) else \
                prm[:, PRM_RW + u * RW_COLS + j:PRM_RW + u * RW_COLS + j + 1]

        def rwkv_tensor(pe):
            A, V, S = rw_act, rw_dve, rw_pe

            def unit(u, more):
                n = u * 4 + N_RWKV
                S.start(u)

                def fill(j, halves=(0, 1)):
                    if more:
                        gemm(pe, n + (4 + j), (N_RWKV + j) % 2, free=(evac_act, n + (3 + j)), halves=halves)

                V.wait_before(pe, u)
                pe.wait_ge(rw_up_loaded, u * 16 + 16)
                pe.wait_ge(rw_pre, 4)
                S.mark(pe.matmul(ps[:, 2, :], rw_up[0:64, :], rw_tw[0:64, :], start=True, stop=True), "w")
                S.mark(pe.matmul(ps[:, 3, :], rw_up[64:128, :], rw_tw[64:128, :], start=True,
                                 stop=True), "a")
                fill(0)
                A.wait(pe, "kksq", u)
                S.mark(pe.matmul(ps[:, 4, :], head_ones[:], rw_sq, start=True, stop=True), "kksum")
                V.wait(pe, "rk", u)
                S.mark(pe.matmul(ps[:, 5, :], head_ones[:], rw_sg, start=True, stop=True), "bonus")
                fill(1)
                V.wait(pe, "bon", u)
                A.wait(pe, "kkroot", u)
                for bank, name, src in ((2, "t_kq", None), (3, "t_b", rw_bt), (4, "t_kd", rw_kdt),
                                        (5, "t_v", rw_v)):
                    for g in range(NB):
                        view = rw_qr[:, g, 0, :] if src is None else src[:, g * P:(g + 1) * P]
                        mm = pe.transpose(ps[:, bank, g * P:(g + 1) * P], view, ident[:])
                    S.mark(mm, name)
                for e, left, bank, name in ((0, rw_bt, 6, "ln0"), (0, rw_kdt, 2, "mq0"),
                                            (1, rw_bt, 4, "ln1"), (1, rw_kdt, 6, "mq1")):
                    rows = slice(64 * e, 64 * e + 64)
                    if bank == 2:
                        A.wait(pe, "n_b", u)
                    elif name == "ln1":
                        A.wait(pe, "n_v", u)
                    elif name == "mq1":
                        V.wait(pe, "ln0", u)
                    for g in range(NB):
                        mm = pe.matmul(psf[:, bank * T + 256 * g:bank * T + 256 * g + 256],
                                       left[rows, g * P:(g + 1) * P],
                                       rw_qr[rows, g, :, :].rearrange("p a t -> p (a t)"),
                                       start=g % 2 == 0, stop=True, skip_group_check=True)
                    S.mark(mm, name)
                for e in range(2):
                    V.wait(pe, f"lt0_{e}", u)
                    for g in range(NB):
                        mm = pe.matmul(ps[:, 2 + e, g * P:(g + 1) * P], rw_lt[e][:, g * P:(g + 1) * P],
                                       ident[:], start=True, stop=True, skip_group_check=True)
                    S.mark(mm, f"u0_{e}")
                fill(2, (0,))
                for lv in range(1, LEVELS):
                    for e in range(2):
                        V.wait(pe, f"x{lv - 1}_{e}", u)
                        V.wait(pe, f"lt{lv}_{e}", u)
                        for g in range(NB):
                            c = slice(g * P, (g + 1) * P)
                            mm = pe.matmul(ps[:, 2 + e, c], rw_lt[e][:, c], rw_x[e][:, c], start=True,
                                           stop=True, skip_group_check=True)
                        S.mark(mm, f"u{lv}_{e}")
                    if lv == 1:
                        fill(2, (1,))
                    if lv == 2:
                        fill(3, (0,))
                    if lv == 3:
                        fill(3, (1,))
                    for e in range(2):
                        A.wait(pe, f"u{lv}_{e}", u)
                        for g in range(NB):
                            c = slice(g * P, (g + 1) * P)
                            mm = pe.matmul(ps[:, 6 + e, c], rw_u[e][:, c], rw_z[e][:, c], start=True,
                                           stop=True, skip_group_check=True)
                        if lv < LEVELS - 1:
                            for g in range(NB):
                                c = slice(g * P, (g + 1) * P)
                                mm = pe.matmul(ps[:, 4 + e, c], rw_z[e][:, c], rw_u[e][:, c], start=True,
                                               stop=True, skip_group_check=True)
                        S.mark(mm, f"xz{lv}_{e}")
                for e in range(2):
                    for g in range(NB):
                        mm = pe.matmul(ps[:, 2, e * 256 + g * 64:e * 256 + g * 64 + 64],
                                       rw_mq[e][:, g, 0, :], rw_vn[:, g, 64 * e:64 * e + 64],
                                       start=e == 0 and g == 0, stop=True, skip_group_check=True)
                S.mark(mm, "mv")
                A.wait(pe, "mv", u)
                for e in range(2):
                    V.wait(pe, f"z{LEVELS - 1}_{e}", u)
                    for g in range(NB):
                        c = slice(g * P, (g + 1) * P)
                        mm = pe.matmul(ps[:, 4 + e, c], rw_z[e][:, c],
                                       rw_km[:, e, g, :, :].rearrange("p a c -> p (a c)"),
                                       start=True, stop=True, skip_group_check=True)
                    S.mark(mm, f"gh{e}")
                A.wait(pe, "gh1", u)
                for e in range(2):
                    for g in range(NB):
                        mm = pe.matmul(ps[64 * e:64 * e + 64, 4, g * P:(g + 1) * P],
                                       rw_gh[e][:, g * P:g * P + 64], rw_ln[e][:, g, 1, :], start=g == 0,
                                       stop=True, skip_group_check=True)
                S.mark(mm, "ng")
                for half in range(2):
                    rows = slice(64 * half, 64 * half + 64)
                    for e in range(2):
                        o = slice(64 * e, 64 * e + 64)
                        for g in range(NB):
                            gh = rw_gh[e]
                            at = ps[o, 6 + half, g * P:g * P + 64]
                            f = ps[o, 6 + half, g * P + 64:g * P + 128]
                            pe.matmul(at, gh[rows, g * P:g * P + 64], rw_bn[rows, g, o], start=g == 0,
                                      stop=True, skip_group_check=True)
                            pe.matmul(f, rw_bn[rows, g, o], gh[rows, g * P + 64:g * P + 128], start=False,
                                      stop=False, skip_group_check=True)
                            mm = pe.matmul(f, rw_kdn[rows, g, o], rw_vn[rows, g, o], start=False, stop=True,
                                           skip_group_check=True)
                S.mark(mm, "atf")
                for c in range(1, NC - 1):
                    V.wait(pe, "f1" if c == 1 else f"st{c - 1}", u)
                    mm = pe.matmul(ps[:, 2, 0:64], rw_at[:, c, :], rw_state[:, c - 1, :], start=True, stop=True)
                    S.mark(mm, f"st{c}")
                V.wait(pe, "rg", u)
                for e in range(2):
                    rows = slice(64 * e, 64 * e + 64)
                    for g in range(NB):
                        dst = ps[rows, 5 + e, g * P:(g + 1) * P]
                        pe.matmul(dst, rw_gh[e][:, g * P + 64:(g + 1) * P], rw_ln[e][:, g, 1, :],
                                  start=g == 0, stop=False, skip_group_check=True)
                        mm = pe.matmul(dst, rw_vn[:, g, rows], rw_mq[e][:, g, 1, :], start=False,
                                       stop=False, skip_group_check=True)
                    for c in range(1, NC):
                        t = slice(c * CHUNK, (c + 1) * CHUNK)
                        mm = pe.matmul(ps[rows, 5 + e, t], rw_state[rows, c - 1, :], rw_rg[rows, t],
                                       start=False, stop=True, skip_group_check=True)
                S.mark(mm, "y")
                A.wait(pe, "y1", u)
                S.mark(pe.matmul(ps[:, 7, :], head_ones[:], rw_y, start=True, stop=True), "mu")
                A.wait(pe, "ysq", u)
                S.mark(pe.matmul(ps[:, 2, :], head_ones[:], rw_ysq, start=True, stop=True), "var")
                S.finish()

            for j in range(4):
                gemm(pe, N_RWKV + j, (N_RWKV + j) % 2, free=(evac_act, N_RWKV + j - 1) if j else None)
            with pe.Fori(0, RW_PAIRS - 1) as u:
                unit(u, True)
            unit(RW_PAIRS - 1, False)

        DECAY = float(np.exp(-0.5))

        def rwkv_scalar(act):
            A, V, S = rw_act, rw_dve, rw_pe
            for dst, c0, w in ((rw_mask, C_RW_MASK, 2 * P), (rw_level, C_RW_LEVEL, LEVELS * P),
                               (rw_chunk, C_RW_CHUNK, T)):
                act.dma_start(dst, consts[:, c0:c0 + w]).then_inc(rw_consts, 16)
            def load_up(u):
                act.dma_start(rw_up[:], lora[bass.ds(u, 1), :, :].rearrange("a p c -> (a p) c")).then_inc(
                    rw_up_loaded, 16)

            load_up(0)
            act.wait_ge(rw_pre, 3)
            nc.scalar.activation(rw_tw[0:64, :], rw_tw[0:64, :], ACT.Tanh).then_inc(rw_pre, 1)

            def take(u, j):
                par = (N_RWKV + j) % 2
                taken(act, u * 4 + (N_RWKV + j), par,
                      lambda: nc.scalar.activation(rw_raw[j], ps[:, par, :], ACT.Copy))

            def unit(u, more):
                A.start(u)

                def fill(j):
                    if more:
                        V.wait(act, "s_" + "rkvg"[j], u)
                        take(u + 1, j)

                V.wait_before(act, u)
                S.wait(act, "w", u)
                A.mark(nc.scalar.activation(rw_sg, ps[:, 2, :], ACT.Sigmoid, bias=rw_col(u, RW_W0)), "sg")
                S.wait(act, "a", u)
                A.mark(nc.scalar.activation(rw_a, ps[:, 3, :], ACT.Sigmoid, bias=rw_col(u, RW_A0)), "a")
                if more:
                    load_up(u + 1)
                V.wait(act, "s_g", u)
                A.mark(nc.scalar.activation(rw_gate, rw_gate, ACT.Silu), "gs")
                V.wait(act, "kk0", u)
                A.mark(nc.scalar.activation(rw_sq, rw_kk, ACT.Square), "kksq")
                V.wait(act, "cs", u)
                A.mark(nc.scalar.activation(rw_p, rw_cs, ACT.Exp, scale=-DECAY), "p")
                A.mark(nc.scalar.activation(rw_pinv, rw_cs, ACT.Exp, scale=DECAY), "pinv")
                V.wait(act, "csp", u)
                A.mark(nc.scalar.activation(rw_pprev, rw_pprev, ACT.Exp, scale=-DECAY), "pprev")
                fill(0)
                S.wait(act, "kksum", u)
                A.mark(nc.scalar.activation(rw_sq, ps[:, 4, :], ACT.Sqrt), "kkroot")
                fill(1)
                S.wait(act, "t_kq", u)
                A.mark(nc.scalar.activation(
                    rw_km[:, :, :, 0, :], ps[:, 2, :].rearrange("p (g e c) -> p e g c", g=NB, e=2),
                    ACT.Copy), "n_kq")
                for bank, name, dst in ((3, "b", rw_bn), (4, "kd", rw_kdn), (5, "v", rw_vn)):
                    S.wait(act, "t_" + name, u)
                    A.mark(nc.scalar.activation(dst, blocks(ps[:, bank, :]), ACT.Copy), "n_" + name)
                for lv in range(1, LEVELS):
                    for e in range(2):
                        S.wait(act, f"u{lv}_{e}", u)
                        A.mark(nc.scalar.activation(rw_u[e], ps[:, 2 + e, :], ACT.Copy), f"u{lv}_{e}")
                    if lv == 1:
                        fill(2)
                    if lv == 3:
                        fill(3)
                S.wait(act, "mv", u)
                A.mark(nc.scalar.activation(
                    rw_km[:, :, :, 1, :], ps[:, 2, :].rearrange("p (e g c) -> p e g c", g=NB, e=2),
                    ACT.Copy), "mv")
                for e in range(2):
                    S.wait(act, f"gh{e}", u)
                    A.mark(nc.scalar.activation(rw_gh[e], ps[:, 4 + e, :], ACT.Copy), f"gh{e}")
                S.wait(act, "y", u)
                for e in range(2):
                    rows = slice(64 * e, 64 * e + 64)
                    A.mark(nc.scalar.activation(rw_y[rows, :], ps[rows, 5 + e, :], ACT.Copy), f"y{e}")
                V.wait(act, "yc", u)
                A.mark(nc.scalar.activation(rw_ysq, rw_yc, ACT.Square), "ysq")
                S.wait(act, "var", u)
                A.mark(nc.scalar.activation(rw_vr, ps[:, 2, :], ACT.Sqrt, bias=eps[:, 2:3],
                                            scale=1.0 / 64), "vroot")
                A.finish()

            for j in range(4):
                take(0, j)
            with act.Fori(0, RW_PAIRS - 1) as u:
                unit(u, True)
            unit(RW_PAIRS - 1, False)

        def rwkv_vector(dve):
            A, V, S = rw_act, rw_dve, rw_pe
            tt, ts, stt = nc.vector.tensor_tensor, nc.vector.tensor_scalar, nc.vector.scalar_tensor_tensor
            order = Order(dve, rw_pre)
            dve.wait_ge(rw_consts, 16 * 3)

            def shifted(dst, src, mu, tmp, then):
                then(tt(tmp[:, 1:T], src[:, 0:T - 1], src[:, 1:T], ALU.subtract), 0)
                then(ts(tmp[:, 0:1], src[:, 0:1], -1.0, None, ALU.mult), 1)
                then(stt(out=dst, in0=tmp, scalar=mu, in1=src, op0=ALU.mult, op1=ALU.add), 2)

            dve.wait_ge(evac_act, 1)
            shifted(rw_tw, slots(arena, 29), prm[:, PRM_MU_WDAD:PRM_MU_WDAD + 1], slots(arena, 9),
                    lambda ins, _: order.then(ins))
            tt(rw_fold[:], ident[:, 0:CHUNK], ident[:, CHUNK:P], ALU.add).then_inc(rw_folded, 1)

            def unit(u):
                V.start(u)

                def then(ins, name):
                    V.mark(ins, name)
                    V.wait(dve, name, u)

                for j, s in enumerate("rkvg"):
                    dve.wait_ge(evac_act, u * 4 + (j + 2))
                    shifted((rw_r, rw_k, rw_v, rw_gate)[j], rw_raw[j], rw_col(u, RW_MU + j), rw_tmp,
                            lambda ins, i, s=s: then(ins, ("d_", "d0_", "s_")[i] + s))
                then(ts(rw_kk, rw_k, rw_col(u, RW_KK), None, ALU.mult), "kk0")
                A.wait(dve, "sg", u)
                then(nc.vector.tensor_tensor_scan(rw_cs, rw_chunk, rw_sg, 0.0, ALU.mult, ALU.add), "cs")
                then(tt(rw_pprev, rw_cs, rw_sg, ALU.subtract), "csp")
                A.wait(dve, "a", u)
                then(ts(rw_tmp, rw_a, 1.0, rw_col(u, RW_KA), ALU.subtract, ALU.mult), "t")
                then(stt(out=rw_kn, in0=rw_tmp, scalar=1.0, in1=rw_k, op0=ALU.add, op1=ALU.mult), "kn")
                then(stt(out=rw_sg, in0=rw_r, scalar=rw_col(u, RW_RK), in1=rw_kn, op0=ALU.mult,
                         op1=ALU.mult), "rk")
                A.wait(dve, "p", u)
                then(tt(rw_qr[:, :, 1, :], blocks(rw_r), blocks(rw_p), ALU.mult), "qr_r")
                then(nc.vector.tensor_copy(rw_pc[:], rw_p[:, CHUNK - 1:T:CHUNK]), "pc")
                A.wait(dve, "pinv", u)
                then(tt(rw_kdt, rw_kn, rw_pinv, ALU.mult), "kdt")
                A.wait(dve, "kkroot", u)
                then(ts(rw_sq, rw_sq, 1e-12, None, ALU.max), "kkmax")
                then(nc.vector.reciprocal(rw_sq, rw_sq), "kkrec")
                then(tt(rw_kk, rw_kk, rw_sq, ALU.mult), "kk")
                A.wait(dve, "pprev", u)
                then(stt(out=rw_qr[:, :, 0, :], in0=blocks(rw_pprev), scalar=-1.0, in1=blocks(rw_kk),
                         op0=ALU.mult, op1=ALU.mult), "qr_k")
                then(tt(rw_tmp, rw_kk, rw_a, ALU.mult), "b")
                then(tt(rw_bt, rw_tmp, rw_pinv, ALU.mult), "bt")
                S.wait(dve, "bonus", u)
                then(tt(rw_bon, ps[:, 5, :], rw_v, ALU.mult), "bon")
                for name, bank in (("ln0", 6), ("mq0", 2), ("ln1", 4), ("mq1", 6)):
                    dst = (rw_ln if name[:2] == "ln" else rw_mq)[int(name[2])]
                    S.wait(dve, name, u)
                    then(tt(dst.rearrange("p g a t -> p g (a t)"),
                            psf[:, bank * T:(bank + 2) * T].rearrange("p (g w) -> p g w", g=NB),
                            over_blocks(rw_mask, 2 * P), ALU.mult), name)

                def level(lv, e):
                    then(tt(blocks(rw_lt[e]), rw_ln[e][:, :, 0, :],
                            over_blocks(rw_level[:, lv * P:(lv + 1) * P], P), ALU.mult), f"lt{lv}_{e}")

                S.wait(dve, "t_v", u)
                for e in range(2):
                    level(0, e)
                for e in range(2):
                    then(tt(blocks(rw_z[e]), blocks(rw_lt[e]), over_blocks(ident[:], P), ALU.add), f"z0_{e}")
                    S.wait(dve, f"u0_{e}", u)
                    then(tt(blocks(rw_x[e]), blocks(ps[:, 2 + e, :]), over_blocks(ident[:], P), ALU.add),
                         f"x0_{e}")
                for lv in range(1, LEVELS):
                    for e in range(2):
                        level(lv, e)
                    for e in range(2):
                        S.wait(dve, f"xz{lv}_{e}", u)
                        then(tt(rw_z[e], ps[:, 6 + e, :], rw_z[e], ALU.add), f"z{lv}_{e}")
                        if lv < LEVELS - 1:
                            then(tt(rw_x[e], ps[:, 4 + e, :], rw_x[e], ALU.add), f"x{lv}_{e}")
                then(nc.vector.memset(slots(arena, 24, 2), 0.0), "zero")
                S.wait(dve, "atf", u)
                dve.wait_ge(rw_folded, 1)
                at = rw_at.rearrange("p (g q) w -> p g q w", q=2)
                start = rw_state.rearrange("p (g q) w -> p g q w", q=2)
                pc = rw_pc[:].rearrange("p (g q) -> p g q", q=2)
                for q in range(2):
                    bank = blocks(ps[:, 6 + q, :])
                    for e in range(2):
                        rows = slice(64 * e, 64 * e + 64)
                        fold = rw_fold[rows].rearrange("p (a w) -> p a w", a=1).broadcast_to([64, NB, CHUNK])
                        then(tt(at[rows, :, q, rows], bank[rows, :, 0:64], fold, ALU.add), f"at{q}_{e}")
                    then(tt(start[:, :, q, :], bank[:, :, 64:128],
                            pc[:, :, q:q + 1].broadcast_to([P, NB, CHUNK]), ALU.mult), f"f{q}")
                for c in range(1, NC - 1):
                    S.wait(dve, f"st{c}", u)
                    then(stt(out=rw_state[:, c, :], in0=ps[:, 2, 0:64], scalar=rw_pc[:, c:c + 1],
                             in1=rw_state[:, c, :], op0=ALU.mult, op1=ALU.add), f"st{c}")
                S.wait(dve, "ng", u)
                then(tt(blocks(rw_rg), blocks(ps[:, 4, :]), rw_qr[:, :, 1, :], ALU.add), "rg")
                S.wait(dve, "mu", u)
                then(stt(out=rw_yc, in0=ps[:, 7, :], scalar=-1.0 / 64, in1=rw_y, op0=ALU.mult, op1=ALU.add),
                     "yc")
                A.wait(dve, "vroot", u)
                then(nc.vector.reciprocal(rw_vr, rw_vr), "vrec")
                then(stt(out=rw_yc, in0=rw_yc, scalar=rw_col(u, RW_GNG), in1=rw_vr, op0=ALU.mult,
                         op1=ALU.mult), "yn")
                then(stt(out=rw_yc, in0=rw_yc, scalar=rw_col(u, RW_GNB), in1=rw_bon, op0=ALU.add,
                         op1=ALU.add), "ynb")
                then(tt(mix_tile(u), rw_yc, rw_gate, ALU.mult), "mix")
                V.finish()

            with dve.Fori(0, RW_PAIRS - 1) as u:
                unit(u)
            unit(RW_PAIRS - 1)

        at_q_in, at_k_in, at_v_in, at_gate = (slots(arena, j) for j in range(4))
        at_q, at_k, at_v = (slots(arena, 4 + j) for j in range(3))
        at_p = slots(arena, 7, 4).rearrange("p (b k) -> p b k", b=TB)
        at_pt = slots(arena, 11, 3)[:, 0:ZW]
        at_bias = slots(arena, 18, 8).rearrange("p (h k) -> p h k", k=256)
        at_cmask = slots(arena, 15)[:, 0:P]
        at_cum, at_ncum = slots(arena, 16), slots(arena, 17)
        at_st = sb("at_st", [P, 3, TB])
        at_const = sem("at_const")
        bias_rows = nc.dram_tensor("bias_rows", (16, 384), F32, kind="Internal").ap()
        bias_ready = sem("bias_ready")
        bias_stored = sem("bias_stored")
        bias_loaded = sem("bias_loaded")
        bias_flipped = sem("bias_flipped")
        bias_copied = sem("bias_copied")
        bias_masked = sem("bias_masked")
        at_flip = slots(arena, 26)[:, 0:P]

        class Attention:

            def __init__(self, name, layer, n0, units, heads, shift, tile0, scale):
                self.layer, self.n0, self.units, self.heads, self.shift = layer, n0, units, heads, shift
                self.tile0, self.scale = tile0, scale
                hs = range(heads)
                self.pe = Steps(sem(name + "_pe"), "vt " + " ".join(f"s{h} tp{h} pv{h}" for h in hs))
                self.act = Steps(sem(name + "_act"), "vn " + " ".join(
                    " ".join(f"e{h}_{b}" for b in range(TB)) + f" pt{h}" for h in hs))
                pre = "" if heads == 2 else "nc "
                self.dve = Steps(sem(name + "_dve"), "qc kc " + pre + " ".join(
                    (f"near{h} diag{h} " if heads == 2 else f"diag{h} ")
                    + " ".join(f"mx{h}_{b}" for b in range(TB)) + f" rec{h} "
                    + " ".join(f"sc{h}_{b}" for b in range(TB)) for h in hs) + " mix")

        even = Attention("ev", 1, N_EVEN, EV_PAIRS, 2, 16, 0, 0.125)
        odd = Attention("od", 2, N_ODD, ODD_HEADS, 1, 28, 0, float(P) ** -0.5)

        def attention_tensor(pe, at):
            A, V, S = at.act, at.dve, at.pe
            width = P // at.heads

            def unit(u, more):
                n = u * 4 + at.n0
                S.start(u)

                def fill(j):
                    if more:
                        gemm(pe, n + (4 + j), (at.n0 + j) % 2, free=(evac_act, n + (3 + j - at.shift)))

                A.wait_before(pe, u)
                pe.wait_ge(evac_act, n + (3 - at.shift))
                for b in range(TB):
                    mm = pe.transpose(ps[:, 7, b * P:(b + 1) * P], at_v_in[:, b * P:(b + 1) * P], ident[:])
                S.mark(mm, "vt")
                for h in range(at.heads):
                    rows = slice(width * h, width * h + width)
                    V.wait(pe, "kc" if at.heads == 2 else "nc", u)
                    if h:
                        A.wait(pe, "pt0", u)
                    for b in range(TB):
                        dst = ps[:, 2 + b, 0:(b + 1) * P]
                        mm = pe.matmul(dst, at_q[rows, b * P:(b + 1) * P], at_k[rows, 0:(b + 1) * P],
                                       start=True, stop=at.heads == 2)
                        if at.heads == 1:
                            mm = pe.matmul(dst, ones[0:16, :], at_ncum[0:16, 0:(b + 1) * P], start=False,
                                           stop=True)
                    S.mark(mm, f"s{h}")
                    fill(2 * h)
                    V.wait(pe, f"sc{h}_3", u)
                    for kb in range(TB):
                        for qb in range(kb, TB):
                            mm = pe.transpose(
                                zb[:, ZOFF[kb] + (qb - kb) * P:ZOFF[kb] + (qb - kb + 1) * P],
                                at_p[:, qb, kb * P:(kb + 1) * P], ident[:])
                    S.mark(mm, f"tp{h}")
                    fill(2 * h + 1)
                    A.wait(pe, f"pt{h}", u)
                    if h == 0:
                        V.wait_before(pe, u)
                    for kb in range(TB):
                        mm = pe.matmul(ps[rows, 6, kb * P:T],
                                       at_v[:, kb * P + width * h:kb * P + width * h + width],
                                       at_pt[:, ZOFF[kb]:ZOFF[kb] + (TB - kb) * P],
                                       start=kb == 0, stop=kb == TB - 1, skip_group_check=True)
                    S.mark(mm, f"pv{h}")
                if at.heads == 1:
                    fill(2)
                    fill(3)
                S.finish()

            for j in range(4):
                gemm(pe, at.n0 + j, (at.n0 + j) % 2, free=(evac_act, at.n0 + j - 1 - at.shift))
            with pe.Fori(0, at.units - 1) as u:
                unit(u, True)
            unit(at.units - 1, False)

        def attention_scalar(act, at):
            A, V, S = at.act, at.dve, at.pe

            def take(u, j):
                par = (at.n0 + j) % 2
                src = ps[:, par, :]

                def body():
                    if j == 0:
                        return nc.scalar.activation(at_q_in, src, ACT.Copy, scale=at.scale)
                    if j == 3:
                        return nc.scalar.activation(at_gate, src, ACT.Silu)
                    return nc.scalar.activation((at_q_in, at_k_in, at_v_in)[j], src, ACT.Copy)
                taken(act, u * 4 + (at.n0 + j), par, body)

            def unit(u, more):
                A.start(u)

                def fill(j):
                    if more:
                        if j < 2:
                            V.wait(act, "qc" if j == 0 else "kc", u)
                        if j == 3:
                            V.wait(act, "mix", u)
                        take(u + 1, j)

                S.wait_before(act, u)
                S.wait(act, "vt", u)
                A.mark(nc.scalar.activation(at_v, ps[:, 7, :], ACT.Copy), "vn")
                for h in range(at.heads):
                    if h:
                        S.wait(act, f"tp{h - 1}", u)
                    for b in range(TB):
                        V.wait(act, f"mx{h}_{b}", u)
                        A.mark(nc.scalar.activation(
                            at_p[:, b, 0:(b + 1) * P], ps[:, 2 + b, 0:(b + 1) * P], ACT.Exp,
                            bias=at_st[:, 0, b:b + 1], accum_out=at_st[:, 1, b:b + 1]), f"e{h}_{b}")
                    fill(2 * h)
                    S.wait(act, f"tp{h}", u)
                    if h:
                        S.wait(act, f"pv{h - 1}", u)
                    A.mark(nc.scalar.activation(at_pt, zb, ACT.Copy), f"pt{h}")
                    if at.heads == 1:
                        fill(1)
                    elif h == 0:
                        fill(1)
                if at.heads == 1:
                    fill(2)
                fill(3)
                A.finish()

            for j in range(4):
                take(0, j)
            with act.Fori(0, at.units - 1) as u:
                unit(u, True)
            unit(at.units - 1, False)

        def attention_vector(dve, at):
            A, V, S = at.act, at.dve, at.pe
            tt, ts = nc.vector.tensor_tensor, nc.vector.tensor_scalar

            def unit(u):
                V.start(u)

                def then(ins, name):
                    V.mark(ins, name)
                    V.wait(dve, name, u)

                S.wait_before(dve, u)
                dve.wait_ge(evac_act, u * 4 + (at.n0 + 1 - at.shift))
                V.mark(nc.vector.tensor_copy(at_q, at_q_in), "qc")
                dve.wait_ge(evac_act, u * 4 + (at.n0 + 2 - at.shift))
                V.mark(nc.vector.tensor_copy(at_k, at_k_in), "kc")
                if at.heads == 1:
                    then(ts(at_ncum[0:16, :], at_cum[0:16, :], ident_col(u), -1.0, ALU.mult, ALU.mult), "nc")
                for h in range(at.heads):
                    S.wait(dve, f"s{h}", u)
                    if at.heads == 2:
                        near = psf[:, 3 * T:3 * T + 3 * 640].rearrange("p (b k) -> p b k", b=3)[:, :, 0:256]
                        bias = at_bias[:, bass.ds(u * 2 + h, 1), :]
                        V.mark(tt(near, near, bias.broadcast_to([P, 3, 256]), ALU.add), f"near{h}")
                        then(tt(ps[:, 2, 0:P], ps[:, 2, 0:P],
                                bias.rearrange("p a k -> p (a k)")[:, P:2 * P], ALU.add), f"diag{h}")
                        V.wait(dve, f"near{h}", u)
                    else:
                        d = psf[:, 2 * T:2 * T + 3 * 640 + P + 512][:, 0:4 * 640].rearrange(
                            "p (b k) -> p b k", b=4)[:, :, 0:P]
                        then(tt(d, d, at_cmask.rearrange("p (a k) -> p a k", a=1).broadcast_to([P, TB, P]),
                                ALU.add), f"diag{h}")
                    for b in range(TB):
                        V.mark(nc.vector.tensor_reduce(at_st[:, 0, b:b + 1], ps[:, 2 + b, 0:(b + 1) * P],
                                                       AX.X, ALU.max, negate=True), f"mx{h}_{b}")
                    A.wait(dve, f"e{h}_3", u)
                    then(nc.vector.reciprocal(at_st[:, 2, :], at_st[:, 1, :]), f"rec{h}")
                    for b in range(TB):
                        V.mark(ts(at_p[:, b, 0:(b + 1) * P], at_p[:, b, 0:(b + 1) * P],
                                  at_st[:, 2, b:b + 1], None, ALU.mult), f"sc{h}_{b}")
                S.wait(dve, f"pv{at.heads - 1}", u)
                dve.wait_ge(evac_act, u * 4 + (at.n0 + 4 - at.shift))
                V.mark(tt(mix_tile(u + at.tile0), ps[:, 6, :], at_gate, ALU.mult), "mix")
                V.finish()

            def ident_col(u):
                return ident[0:16, bass.ds(u, 1)] if not isinstance(u, int) else ident[0:16, u:u + 1]

            with dve.Fori(0, at.units - 1) as u:
                unit(u)
            unit(at.units - 1)

        def bias_scalar(act):
            act.dma_start(slots(arena, 16)[0:16, 0:257], rel_bias).then_inc(bias_ready, 16)
            act.wait_ge(bias_ready, 18)
            act.dma_start(bias_rows, slots(arena, 17)[0:16, 0:384]).then_inc(bias_stored, 16)
            act.wait_ge(bias_stored, 16)
            act.dma_start(at_bias, bass.AP(bias_rows.tensor, 0, [[1, P], [384, 16], [1, 256]])).then_inc(
                bias_loaded, 16)
            act.dma_start(at_flip, consts[:, C_FLIP:C_FLIP + P]).then_inc(bias_loaded, 16)

        def bias_tensor(pe):
            pe.wait_ge(bias_loaded, 32)
            for j in range(8):
                if j >= 4:
                    pe.wait_ge(bias_copied, j - 3)
                pe.matmul(ps[:, 2 + j % 4, :], at_flip, slots(arena, 18 + j), start=True,
                          stop=True).then_inc(bias_flipped, 1)
            pe.wait_ge(bias_copied, 8)

        def bias_vector(dve):
            rows, rel = slots(arena, 17)[0:16, 0:384], slots(arena, 16)[0:16, 0:257]
            dve.wait_ge(bias_ready, 16)
            nc.vector.memset(rows, 0.0).then_inc(bias_ready, 1)
            dve.wait_ge(bias_ready, 17)
            nc.vector.tensor_scalar(rows[:, 127:383], rel[:, 256:0:-1], rel[:, 256:257], None,
                                    ALU.subtract).then_inc(bias_ready, 1)
            for j in range(8):
                dve.wait_ge(bias_flipped, j + 1)
                nc.vector.tensor_copy(slots(arena, 18 + j), ps[:, 2 + j % 4, :]).then_inc(bias_copied, 1)
            dve.wait_ge(bias_copied, 8)
            nc.vector.memset(at_bias[0:64, :, 192:256], NEG).then_inc(bias_masked, 1)
            dve.wait_ge(bias_masked, 1)

        fg = Steps(sem("fg"), "y mn n e l ls cum")
        fg_t = [slots(arena, 18 + j)[0:16, :] for j in range(4)]

        def forget_tensor(pe):
            gemm(pe, N_F, N_F % 2, act_ready=(norm_lo, 2 * KT))

        def forget_scalar(act):
            act.dma_start(at_cmask, consts[:, C_ODD:C_ODD + P]).then_inc(at_const, 16)
            par = N_F % 2
            cast(act, N_F * 2 + 4, (2 * par) % 4)
            act.wait_ge(pe_half, N_F * 2 + 2)
            nc.scalar.activation(fg_t[0], ps[0:16, par, :], ACT.Identity,
                                 bias=prm[0:16, PRM_BF:PRM_BF + 1]).then_inc(evac_act, 1)
            cast(act, N_F * 2 + 5, (2 * par + 1) % 4)
            fg.wait(act, "n", 0)
            nc.scalar.activation(fg_t[2], fg_t[2], ACT.Exp).then_inc(fg.sem, 1)
            fg.wait(act, "e", 0)
            nc.scalar.activation(fg_t[2], fg_t[2], ACT.Ln, bias=eps[0:16, 3:4]).then_inc(fg.sem, 1)

        def forget_vector(dve):
            dve.wait_ge(at_const, 16)
            dve.wait_ge(evac_act, N_F + 1 - odd.shift)
            nc.vector.memset(fg_t[3], 1.0).then_inc(fg.sem, 1)
            fg.wait(dve, "y", 0)
            nc.vector.tensor_scalar(fg_t[1], fg_t[0], 0.0, None, ALU.min).then_inc(fg.sem, 1)
            fg.wait(dve, "mn", 0)
            nc.vector.scalar_tensor_tensor(out=fg_t[2], in0=fg_t[1], scalar=2.0, in1=fg_t[0], op0=ALU.mult,
                                           op1=ALU.subtract).then_inc(fg.sem, 1)
            fg.wait(dve, "l", 0)
            nc.vector.tensor_tensor(fg_t[1], fg_t[1], fg_t[2], ALU.subtract).then_inc(fg.sem, 1)
            fg.wait(dve, "ls", 0)
            nc.vector.tensor_tensor_scan(at_cum[0:16, :], fg_t[3], fg_t[1], 0.0, ALU.mult,
                                         ALU.add).then_inc(fg.sem, 1)
            fg.wait(dve, "cum", 0)

        S5_TILES, S5_PAIRS = 8, 32
        TWO_PI = 2 * np.pi
        PI_A = 6.28125
        PI_B = float(np.float32(np.round((TWO_PI - PI_A) * 2 ** 21) / 2 ** 21))
        PI_C = float(np.float32(TWO_PI - PI_A - PI_B))
        ROUND = 12582912.0
        UNDER_2PI = float(np.nextafter(np.float32(TWO_PI), np.float32(0)))
        s5_u = slots(arena, 0, 8)
        s5_bt = [slots(arena, 8 + 2 * e, 2) for e in range(2)]
        s5_ct = [slots(arena, 12 + 2 * e, 2) for e in range(2)]
        s5_time = slots(arena, 16)
        s5_ph, s5_cos, s5_sin, s5_tmp = (slots(arena, 17 + j) for j in range(4))
        s5_t = [slots(arena, 21 + j) for j in range(4)]
        s5_z = [slots(arena, 25), slots(arena, 26)]
        s5_in = slots(arena, 27)
        s5_y = slots(arena, 28)
        s5_bs, s5_cs = (slots(arena, 29)[:, 0:256], slots(arena, 29)[:, 256:512])
        s5_p = sb("s5_p", [P, 16, 32])
        (s5_dt, s5_la, s5_ang, s5_mag, s5_k, s5_r, s5_fh, s5_fl, s5_are, s5_aim, s5_cr, s5_ci,
         s5_den, s5_w1, s5_w2, s5_w3) = (s5_p[:, j, :] for j in range(16))
        s5_loaded = sem("s5_loaded")
        s5_pre = sem("s5_pre")
        s5_pre_act = sem("s5_pre_act")
        s5_pre_pe = sem("s5_pre_pe")
        s5_pe = Steps(sem("s5_pe"), " ".join(f"bu{k} y{k}" for k in range(4)))
        s5_act = Steps(sem("s5_act"), "cb cc " + " ".join(f"sin{k} abs{k} cos{k}" for k in range(4)) + " gelu")
        s5_dve = Steps(sem("s5_dve"), "cu " + " ".join(
            f"a{k} rd{k} ph{k} pl{k} cl{k} v0{k} v1{k} v2{k} v3{k} vr{k} vi{k} zr{k} zi{k} "
            f"x0{k} x1{k} x2{k} x3{k} xr{k} xi{k}" for k in range(4)) + " y")

        def s5_tensor(pe):
            for j in range(S5_TILES):
                n = N_U + j
                gemm(pe, n, n % 2, free=(evac_act, n - 17) if j >= 2 else None,
                     act_ready=(norm_lo, KT) if j == 0 else None)
            for e in range(2):
                pe.wait_ge(s5_pre, S5_PRE_BB + 4 * e)
                for i in range(S5_TILES):
                    mm = pe.transpose(psf[:, (2 + 2 * e) * T + i * P:(2 + 2 * e) * T + (i + 1) * P],
                                      s5_big(e)[:, i * P:(i + 1) * P], ident[:])
                mm.then_inc(s5_pre_pe, 1)
            A, V, S = s5_act, s5_dve, s5_pe
            with pe.Fori(0, S5_TILES) as i:
                S.start(i)
                for k in range(4):
                    rows = slice(32 * k, 32 * k + 32)
                    if k == 0:
                        V.wait_before(pe, i)
                        V.wait(pe, "cu", i)
                        A.wait(pe, "cc", i)
                        pe.wait_ge(s5_pre_act, S5_ACT_DONE)
                    elif k >= 1:
                        V.wait(pe, f"v3{k - 1}", i)
                    for e in range(2):
                        mm = pe.matmul(ps[:, 2 + e, :], s5_bs[rows, e * P:(e + 1) * P], s5_in[rows, :],
                                       start=True, stop=True)
                    S.mark(mm, f"bu{k}")
                    V.wait(pe, f"xi{k}", i)
                    for e in range(2):
                        mm = pe.matmul(ps[rows, 6, :], s5_cs[:, e * P + 32 * k:e * P + 32 * k + 32],
                                       s5_t[1 + e], start=e == 0, stop=e == 1, skip_group_check=True)
                    S.mark(mm, f"y{k}")
                S.finish()

        def s5_big(e):
            return slots(arena, 21 + 2 * e, 2)

        S5_ACT_DONE = 6 + 2

        def s5_scalar(act):
            act.dma_start(s5_time, consts[:, C_TIME:C_TIME + T]).then_inc(s5_loaded, 16)
            for e in range(2):
                act.dma_start(slots(arena, 17 + e), s5_b[e].rearrange("p q c -> p (q c)")).then_inc(s5_loaded, 16)
            for e in range(2):
                act.dma_start(slots(arena, 27 + e), s5_c[e].rearrange("p q c -> p (q c)")).then_inc(s5_loaded, 16)
            for j in range(S5_TILES):
                n = N_U + j
                taken(act, n, n % 2, lambda: nc.scalar.activation(s5_u[:, j * T:(j + 1) * T],
                                                                  ps[:, n % 2, :], ACT.Copy))
            nc.scalar.activation(s5_dt, prm[:, PRM_LDT:PRM_LDT + 32], ACT.Exp).then_inc(s5_pre_act, 1)
            act.wait_ge(s5_pre, S5_PRE_LA)
            nc.scalar.activation(s5_mag, s5_la, ACT.Exp).then_inc(s5_pre_act, 1)
            act.wait_ge(s5_pre, S5_PRE_R)
            nc.scalar.activation(s5_aim, s5_r, ACT.Sin).then_inc(s5_pre_act, 1)
            nc.scalar.activation(s5_w1, s5_r, ACT.Abs).then_inc(s5_pre_act, 1)
            act.wait_ge(s5_pre_act, 4)
            nc.scalar.activation(s5_are, s5_w1, ACT.Sin, bias=eps[:, 4:5], scale=-1.0).then_inc(s5_pre_act, 1)
            act.wait_ge(s5_pre_act, 5)
            nc.scalar.activation(s5_w2, s5_w1, ACT.Copy).then_inc(s5_pre_act, 1)
            for e in range(2):
                act.wait_ge(s5_pre_pe, e + 1)
                nc.scalar.activation(s5_bt[e], psf[:, (2 + 2 * e) * T:(4 + 2 * e) * T],
                                     ACT.Copy).then_inc(s5_pre_act, 1)
            act.wait_ge(s5_pre_act, S5_ACT_DONE)
            act.wait_ge(s5_pre, S5_PRE_END)
            A, V, S = s5_act, s5_dve, s5_pe
            with act.Fori(0, S5_TILES) as i:
                A.start(i)
                S.wait_before(act, i)
                V.wait_before(act, i)
                for dst, src, name in ((s5_bs, s5_bt, "cb"), (s5_cs, s5_ct, "cc")):
                    both = slots(arena, 8 if name == "cb" else 12, 4).rearrange("p (e w) -> p e w", e=2)
                    A.mark(nc.scalar.activation(dst.rearrange("p (e w) -> p e w", e=2),
                                                both[:, :, bass.ds(i * P, P)], ACT.Copy), name)
                for k in range(4):
                    V.wait(act, f"cl{k}", i)
                    if k:
                        V.wait(act, f"x3{k - 1}", i)
                    A.mark(nc.scalar.activation(s5_sin, s5_ph, ACT.Sin, scale=UNDER_2PI), f"sin{k}")
                    A.mark(nc.scalar.activation(s5_tmp, s5_ph, ACT.Abs), f"abs{k}")
                    A.wait(act, f"abs{k}", i)
                    A.mark(nc.scalar.activation(s5_cos, s5_tmp, ACT.Sin, bias=eps[:, 4:5],
                                                scale=-UNDER_2PI), f"cos{k}")
                V.wait(act, "y", i)
                A.mark(nc.scalar.activation(mix_tile(i + 8), s5_y, ACT.Gelu_apprx_tanh), "gelu")
                A.finish()

        S5_PRE_LA, S5_PRE_R, S5_PRE_BB, S5_PRE_END = 2, 8, 33, 42

        def s5_vector(dve):
            tt, ts, stt = nc.vector.tensor_tensor, nc.vector.tensor_scalar, nc.vector.scalar_tensor_tensor
            pre = Order(dve, s5_pre)
            lre, lim = prm[:, PRM_LRE:PRM_LRE + 32], prm[:, PRM_LIM:PRM_LIM + 32]
            dve.wait_ge(s5_loaded, 16 * 5)
            dve.wait_ge(s5_pre_act, 1)
            pre.then(tt(s5_ang, lim, s5_dt, ALU.mult))
            pre.then(tt(s5_la, lre, s5_dt, ALU.mult))
            assert pre.k == S5_PRE_LA
            pre.then(ts(s5_k, s5_ang, 1 / TWO_PI, ROUND, ALU.mult, ALU.add))
            pre.then(ts(s5_k, s5_k, ROUND, None, ALU.subtract))
            pre.then(stt(out=s5_r, in0=s5_k, scalar=-PI_A, in1=s5_ang, op0=ALU.mult, op1=ALU.add))
            pre.then(stt(out=s5_r, in0=s5_k, scalar=-PI_B, in1=s5_r, op0=ALU.mult, op1=ALU.add))
            pre.then(stt(out=s5_r, in0=s5_k, scalar=-PI_C, in1=s5_r, op0=ALU.mult, op1=ALU.add))
            pre.then(ts(s5_r, s5_r, UNDER_2PI / 2, -UNDER_2PI / 2, ALU.min, ALU.max))
            assert pre.k == S5_PRE_R
            pre.then(ts(s5_w3, s5_r, 1 / TWO_PI, None, ALU.mult))
            pre.then(ts(s5_fl, s5_w3, 4097.0, None, ALU.mult))
            pre.then(tt(s5_fh, s5_fl, s5_w3, ALU.subtract))
            pre.then(tt(s5_fh, s5_fl, s5_fh, ALU.subtract))
            pre.then(tt(s5_fl, s5_w3, s5_fh, ALU.subtract))
            dve.wait_ge(s5_pre_act, 6)
            pre.then(tt(s5_are, s5_are, s5_mag, ALU.mult))
            pre.then(tt(s5_aim, s5_aim, s5_mag, ALU.mult))
            pre.then(ts(s5_are, s5_are, 1.0, None, ALU.subtract))
            pre.then(tt(s5_den, lre, lre, ALU.mult))
            pre.then(tt(s5_w1, lim, lim, ALU.mult))
            pre.then(tt(s5_den, s5_den, s5_w1, ALU.add))
            pre.then(nc.vector.reciprocal(s5_den, s5_den))
            pre.then(tt(s5_w1, s5_are, lre, ALU.mult))
            pre.then(tt(s5_w2, s5_aim, lim, ALU.mult))
            pre.then(tt(s5_w1, s5_w1, s5_w2, ALU.add))
            pre.then(tt(s5_cr, s5_w1, s5_den, ALU.mult))
            pre.then(tt(s5_w1, s5_aim, lre, ALU.mult))
            pre.then(tt(s5_w2, s5_are, lim, ALU.mult))
            pre.then(tt(s5_w1, s5_w1, s5_w2, ALU.subtract))
            pre.then(tt(s5_ci, s5_w1, s5_den, ALU.mult))

            def by_pair(view):
                return view.rearrange("p (q a) -> p q a", a=1).broadcast_to([P, 32, 16])

            def chans(view):
                return view.rearrange("p (q c) -> p q c", c=16)

            br, bi, tmp = slots(arena, 17), slots(arena, 18), slots(arena, 19)
            pre.then(nc.vector.memset(slots(arena, 21, 4), 0.0))
            for e, (x0, x1, op) in enumerate(((br, bi, ALU.subtract), (bi, br, ALU.add))):
                pre.then(tt(chans(tmp), chans(x0), by_pair(s5_cr), ALU.mult))
                pre.then(tt(chans(slots(arena, 20)), chans(x1), by_pair(s5_ci), ALU.mult))
                big = s5_big(e).rearrange("p (q g c) -> p q g c", g=2, c=16)
                for g in range(2):
                    rows = slice(64 * g, 64 * g + 64)
                    ins = tt(big[rows, :, g, :], chans(tmp)[rows], chans(slots(arena, 20))[rows], op)
                    pre.then(ins)
            pre.then(nc.vector.memset(slots(arena, 12, 4), 0.0))
            for e in range(2):
                big = s5_ct[e].rearrange("p (q g c) -> p q g c", g=2, c=16)
                src = chans(slots(arena, 27 + e))
                for g in range(2):
                    rows = slice(64 * g, 64 * g + 64)
                    pre.then(ts(big[rows, :, g, :], src[rows], -1.0 if e else 1.0, None, ALU.mult))
            assert pre.k == S5_PRE_END, pre.k

            A, V, S = s5_act, s5_dve, s5_pe
            dve.wait_ge(s5_pre_act, S5_ACT_DONE)
            with dve.Fori(0, S5_TILES) as i:
                V.start(i)

                def then(ins, name):
                    V.mark(ins, name)
                    V.wait(dve, name, i)

                S.wait_before(dve, i)
                dve.wait_ge(evac_act, i + (N_U + 1 - 16))
                then(nc.vector.tensor_copy(s5_in, s5_u[:, bass.ds(i * T, T)]), "cu")
                for k in range(4):
                    def col(view):
                        return view[:, bass.ds(i * 4 + k, 1)]

                    if k:
                        A.wait(dve, f"cos{k - 1}", i)
                    else:
                        A.wait_before(dve, i)
                    then(ts(s5_ph, s5_time, col(s5_fh), None, ALU.mult), f"a{k}")
                    then(ts(s5_t[0], s5_ph, ROUND, ROUND, ALU.add, ALU.subtract), f"rd{k}")
                    then(tt(s5_ph, s5_ph, s5_t[0], ALU.subtract), f"ph{k}")
                    then(stt(out=s5_ph, in0=s5_time, scalar=col(s5_fl), in1=s5_ph, op0=ALU.mult,
                             op1=ALU.add), f"pl{k}")
                    then(ts(s5_ph, s5_ph, 0.5, -0.5, ALU.min, ALU.max), f"cl{k}")
                    A.wait(dve, f"cos{k}", i)
                    S.wait(dve, f"bu{k}", i)
                    if k:
                        S.wait(dve, f"y{k - 1}", i)
                    then(tt(s5_t[0], ps[:, 2, :], s5_cos, ALU.mult), f"v0{k}")
                    then(tt(s5_t[1], ps[:, 3, :], s5_sin, ALU.mult), f"v1{k}")
                    then(tt(s5_t[2], ps[:, 3, :], s5_cos, ALU.mult), f"v2{k}")
                    then(tt(s5_t[3], ps[:, 2, :], s5_sin, ALU.mult), f"v3{k}")
                    then(tt(s5_t[0], s5_t[0], s5_t[1], ALU.add), f"vr{k}")
                    then(tt(s5_t[2], s5_t[2], s5_t[3], ALU.subtract), f"vi{k}")
                    mag = col(s5_mag).broadcast_to([P, T])
                    then(nc.vector.tensor_tensor_scan(s5_z[0], mag, s5_t[0], 0.0, ALU.mult, ALU.add), f"zr{k}")
                    then(nc.vector.tensor_tensor_scan(s5_z[1], mag, s5_t[2], 0.0, ALU.mult, ALU.add), f"zi{k}")
                    then(tt(s5_t[1], s5_z[0], s5_cos, ALU.mult), f"x0{k}")
                    then(tt(s5_t[0], s5_z[1], s5_sin, ALU.mult), f"x1{k}")
                    then(tt(s5_t[2], s5_z[0], s5_sin, ALU.mult), f"x2{k}")
                    then(tt(s5_t[3], s5_z[1], s5_cos, ALU.mult), f"x3{k}")
                    then(tt(s5_t[1], s5_t[1], s5_t[0], ALU.subtract), f"xr{k}")
                    then(tt(s5_t[2], s5_t[2], s5_t[3], ALU.add), f"xi{k}")
                S.wait(dve, "y3", i)
                then(stt(out=s5_y, in0=s5_in, scalar=prm[:, bass.ds(i + PRM_SD, 1)], in1=ps[:, 6, :],
                         op0=ALU.mult, op1=ALU.add), "y")
                V.finish()

        glu_gate = [slots(arena, j) for j in range(8)]
        glu_sg = [slots(arena, 8), slots(arena, 9)]
        glu_hi = sem("glu_hi")
        glu_lo = sem("glu_lo")
        glu_mul = sem("glu_mul")
        glu_mix = sem("glu_mix")
        GLU_TAKEN = N_GLU - 16

        def glu_tensor(pe):
            for j in range(8):
                n = N_ZB + j
                gemm(pe, n, n % 2, free=(evac_act, n - 17))
            pe.wait_ge(evac_act, GLU_TAKEN)
            for j in range(4):
                n = N_GLU + j
                gemm(pe, n, n % 2, free=(evac_act, GLU_TAKEN + max(0, 2 * j - 1)), outputs=2,
                     act_ready=(glu_lo, 0) if j == 0 else None)

        def glu_scalar(act):
            for j in range(8):
                n = N_ZB + j
                taken(act, n, n % 2, lambda: nc.scalar.activation(glu_gate[j], ps[:, n % 2, :], ACT.Silu))
            for j in range(8):
                nc.scalar.activation(act_hi[:, j, :], mix_tile(8 + j), ACT.Copy).then_inc(glu_hi, 1)
            for o in range(8):
                n, h = N_GLU + o // 2, o % 2
                if h == 0:
                    cast(act, n * 2 + 4, (2 * n) % 4)
                act.wait_ge(pe_half, n * 2 + h + 1)
                if o >= 2:
                    act.wait_ge(glu_mul, o - 1)
                nc.scalar.activation(glu_sg[h], ps[:, h, :], ACT.Sigmoid,
                                     bias=prm[:, PRM_BGLU + o:PRM_BGLU + o + 1]).then_inc(evac_act, 1)
                if h == 1:
                    cast(act, n * 2 + 5, (2 * n + 1) % 4)

        def glu_vector(dve):
            for j in range(8):
                dve.wait_ge(glu_hi, j + 1)
                nc.vector.tensor_tensor(act_lo[:, j, :], mix_tile(8 + j), act_hi[:, j, :].bitcast(F32),
                                        ALU.subtract).then_inc(glu_lo, 1)
            for o in range(8):
                dve.wait_ge(evac_act, GLU_TAKEN + o + 1)
                nc.vector.tensor_tensor(glu_sg[o % 2], glu_sg[o % 2], mix_tile(8 + o),
                                        ALU.mult).then_inc(glu_sgm, 1)
                dve.wait_ge(glu_sgm, o + 1)
                nc.vector.tensor_tensor(mix_tile(8 + o), glu_sg[o % 2], glu_gate[o],
                                        ALU.mult).then_inc(glu_mul, 1)

        glu_sgm = sem("glu_sgm")

        out_nat = slots(arena, 0, 16).rearrange("p (b d) -> p b d", b=TB)

        def result_tensor(pe):
            with pe.Fori(0, KT // 2) as two:
                ft = two * 2
                for j in range(2):
                    pe.wait_ge(norm_t, ft + (3 * KT + j + 1))
                    pe.wait_ge(out_copied, ft + (j if j == 0 else 0))
                    for b in range(TB):
                        mm = pe.transpose(ps[:, 2 + j, b * P:(b + 1) * P],
                                          norm_in[j][:, b * P:(b + 1) * P], ident[:])
                    mm.then_inc(out_turned, 1)

        def result_scalar(act):
            for ft in range(KT):
                act.wait_ge(out_turned, ft + 1)
                nc.scalar.activation(out_nat[:, :, ft * P:(ft + 1) * P], blocks(ps[:, 2 + ft % 2, :]),
                                     ACT.Copy).then_inc(out_copied, 1)
                if ft % 4 == 3:
                    cols = slice((ft - 3) * P, (ft + 1) * P)
                    act.wait_ge(out_copied, ft + 1)
                    act.dma_start(out[:, cols].rearrange("(b p) d -> p b d", p=P),
                                  out_nat[:, :, cols]).then_inc(out_stored, 16)
            act.wait_ge(out_stored, 16 * 4)

        @block.tensor
        def _(pe):
            load_tensor(pe)
            gemm(pe, N_WDAD, 0, act_ready=(norm_lo, 0))
            rwkv_tensor(pe)
            meet(pe, 1)
            pool_tensor(pe)
            meet(pe, 2)
            sb_tensor(pe)
            meet(pe, 3)
            out_tensor(pe, 0, N_OUT1, N_OUT1)
            meet(pe, 4)
            s5_tensor(pe)
            meet(pe, 5)
            bias_tensor(pe)
            attention_tensor(pe, even)
            meet(pe, 6)
            glu_tensor(pe)
            meet(pe, 7)
            out_tensor(pe, 1, N_OUT2, GLU_TAKEN + 8)
            meet(pe, 8)
            forget_tensor(pe)
            attention_tensor(pe, odd)
            meet(pe, 9)
            out_tensor(pe, 2, N_OUT3, N_OUT3 - odd.shift)
            meet(pe, 10)
            result_tensor(pe)

        @block.scalar
        def _(act):
            load_scalar(act)
            norm_scalar(act, 0)
            taken(act, N_WDAD, 0, lambda: nc.scalar.activation(slots(arena, 29), ps[:, 0, :], ACT.Copy))
            rwkv_scalar(act)
            meet(act, 1)
            pool_scalar(act)
            meet(act, 2)
            sb_scalar(act)
            meet(act, 3)
            mix_split_scalar(act, 0)
            out_scalar(act, 0, N_OUT1)
            norm_scalar(act, 1)
            meet(act, 4)
            s5_scalar(act)
            meet(act, 5)
            bias_scalar(act)
            attention_scalar(act, even)
            meet(act, 6)
            glu_scalar(act)
            meet(act, 7)
            mix_split_scalar(act, 1)
            out_scalar(act, 1, N_OUT2)
            norm_scalar(act, 2)
            meet(act, 8)
            forget_scalar(act)
            attention_scalar(act, odd)
            meet(act, 9)
            mix_split_scalar(act, 2)
            out_scalar(act, 2, N_OUT3)
            norm_scalar(act, 3)
            meet(act, 10)
            result_scalar(act)

        @block.vector
        def _(dve):
            dve.wait_ge(consts_loaded, 64)
            load_vector(dve)
            norm_vector(dve, 0)
            rwkv_vector(dve)
            meet(dve, 1)
            pool_vector(dve)
            meet(dve, 2)
            sb_vector(dve)
            meet(dve, 3)
            mix_split_vector(dve, 0)
            out_vector(dve, 0, N_OUT1)
            norm_vector(dve, 1)
            meet(dve, 4)
            s5_vector(dve)
            meet(dve, 5)
            bias_vector(dve)
            attention_vector(dve, even)
            meet(dve, 6)
            glu_vector(dve)
            meet(dve, 7)
            mix_split_vector(dve, 1)
            out_vector(dve, 1, N_OUT2)
            norm_vector(dve, 2)
            meet(dve, 8)
            forget_vector(dve)
            attention_vector(dve, odd)
            meet(dve, 9)
            mix_split_vector(dve, 2)
            out_vector(dve, 2, N_OUT3)
            meet(dve, 10)
            norm_vector(dve, 3)


def weight_tile(w, cols):
    k = w.shape[0] // P
    t = w[:, cols:cols + P].reshape(k, P, P).transpose(1, 0, 2)
    return np.stack([t[:, :k // 2], t[:, k // 2:]]).reshape(2, P, -1)


def weight_stream(i):
    w1, w2, w3 = i["w_in"][0], i["w_in_even_2"][0], i["w_in_odd_2"][0]
    tiles = [weight_tile(w1, 3072)]
    tiles += [weight_tile(w1, 768 * j + P * p) for p in range(RW_PAIRS) for j in range(4)]
    tiles += [weight_tile(w1, 3200 + T * j + P * g) for g in range(POOL_GROUPS) for j in range(2)]
    tiles += [weight_tile(w1, 4224 + 768 * j + P * p) for p in range(SB_PAIRS) for j in range(4)]
    tiles += [weight_tile(i["w_out"][0], P * c) for c in range(KT)]
    tiles += [weight_tile(w2, 3072 + P * c) for c in range(8)]
    tiles += [weight_tile(w2, c + P * p) for p in range(EV_PAIRS) for c in (0, 1024, 2048, 4096)]
    tiles += [weight_tile(w2, 5120 + P * c) for c in range(8)]
    glu = [i["w_glu_2"][0][:, P * c:P * c + P].reshape(8, P, P).transpose(1, 0, 2).reshape(P, -1) for c in range(8)]
    tiles += [np.stack([glu[c], glu[c + 1]]) for c in range(0, 8, 2)]
    tiles += [weight_tile(i["w_out_even_2"][0], P * c) for c in range(KT)]
    tiles += [weight_tile(np.pad(w3[:, 8192:8208], ((0, 0), (0, P - 16))), 0)]
    tiles += [weight_tile(w3, 2048 * j + P * h) for h in range(ODD_HEADS) for j in range(4)]
    tiles += [weight_tile(i["w_out_odd_2"][0], P * c) for c in range(KT)]
    return np.stack(tiles)


def parameters(i):
    def tiles(a):
        return a.reshape(-1, P)
    rw = [tiles(i["mu_a"][0][768 * j:768 * j + 768]) for j in range(4)]
    rw += [tiles(i[k][0].reshape(-1)) for k in ("w0", "a0", "k_k", "k_a", "r_k", "gn_g", "gn_b")]
    rows = [tiles(i[k].reshape(-1)) for k in ("norm_g", "norm_even_g_2", "norm_odd_g_2", "final_norm_g_2")]
    rows += [tiles(i["mu_a"][0][3072:3200]), np.stack(rw, 1).reshape(-1, P), tiles(i["pool_scale"][0])]
    rows += [np.tile(i["qn_g"], 2), np.tile(i["kn_g"], 2)]
    rows += [tiles(i["s5_lambda_re_2"][0]), tiles(i["s5_lambda_im_2"][0])]
    rows += [tiles(np.repeat(i["s5_log_dt_2"][0], 64)), tiles(i["s5_d_2"][0]), tiles(i["b_glu_2"][0])]
    rows += [np.pad(i["b_forget_2"][0], (0, P - 16))[None]]
    return np.ascontiguousarray(np.concatenate(rows, 0).T)


def kernel(**inputs):
    import concourse.bacc as bacc
    from concourse.bass_utils import run_bass_kernel_spmd

    i = {k: np.asarray(v) for k, v in inputs.items()}

    def s5_side(a):
        return np.ascontiguousarray(a.reshape(32, P, 16).transpose(1, 0, 2))

    arrays = {
        "stream": weight_stream(i),
        "x": np.ascontiguousarray(i["x"][0]),
        "params": parameters(i),
        "consts": constants(),
        "rel_bias": np.ascontiguousarray(i["rel_bias_2"][0]),
        "lora": np.stack([np.concatenate([i[k][0][:, P * p:P * p + P] for k in ("w_up", "a_up")])
                          for p in range(6)]),
        "pool_w": np.ascontiguousarray(i["pool_w"][0]),
        "s5_b": np.stack([s5_side(i["s5_b_re_2"][0]), s5_side(i["s5_b_im_2"][0])]),
        "s5_c": np.stack([s5_side(i["s5_c_re_2"][0].transpose(0, 2, 1)),
                          s5_side(i["s5_c_im_2"][0].transpose(0, 2, 1))]),
    }
    nc = bacc.Bacc("TRN2", target_bir_lowering=False, num_devices=1)
    aps = [nc.dram_tensor(k, a.shape, F32, kind="ExternalInput").ap() for k, a in arrays.items()]
    out = nc.dram_tensor("out", (T, D), F32, kind="ExternalOutput").ap()
    build_program(nc, *aps, out)
    r = run_bass_kernel_spmd(nc, [arrays], core_ids=[0])
    return r.results[0]["out"].reshape(1, T, D)
```

```python
from contextlib import ExitStack

import numpy as np

import concourse.bass as bass
from concourse import mybir

F32 = mybir.dt.float32
F32R = mybir.dt.float32r
I32 = mybir.dt.int32
ACT = mybir.ActivationFunctionType
ALU = mybir.AluOpType
AX = mybir.AxisListType

P = 128
T = 512
TB = T // P
D = 2048
KT = D // P
HK = KT // 2

RW_PAIRS, POOL_GROUPS, SB_PAIRS, EV_PAIRS, ODD_HEADS = 6, 4, 6, 8, 16
N_WDAD = 0
N_RWKV = 1
N_POOL = N_RWKV + 4 * RW_PAIRS
N_SB = N_POOL + 2 * POOL_GROUPS
N_OUT1 = N_SB + 4 * SB_PAIRS
N_U = N_OUT1 + KT
N_ZB = N_U + 8
N_EVEN = N_ZB + 8
N_GLU = N_EVEN + 4 * EV_PAIRS
N_OUT2 = N_GLU + 4
N_F = N_OUT2 + KT
N_ODD = N_F + 1
N_OUT3 = N_ODD + 4 * ODD_HEADS
N_TILES = N_OUT3 + KT

NEG = -1.0e30
RMS_EPS = 1e-6
GN_EPS = 64e-5

PRM_G = 0
PRM_MU_WDAD = PRM_G + 4 * KT
PRM_RW = PRM_MU_WDAD + 1
RW_MU, RW_W0, RW_A0, RW_KK, RW_KA, RW_RK, RW_GNG, RW_GNB, RW_COLS = 0, 4, 5, 6, 7, 8, 9, 10, 11
PRM_POOL = PRM_RW + 6 * RW_COLS
PRM_QN = PRM_POOL + POOL_GROUPS
PRM_KN = PRM_QN + 1
PRM_LRE = PRM_KN + 1
PRM_LIM = PRM_LRE + 32
PRM_LDT = PRM_LIM + 32
PRM_SD = PRM_LDT + 32
PRM_BGLU = PRM_SD + 8
PRM_BF = PRM_BGLU + 8
PRM_COLS = PRM_BF + 1

C_IDENT = 0
C_HEAD = C_IDENT + P
C_ONES = C_HEAD + P
C_SB = C_ONES + P
C_INV = C_SB + 4 * P
C_RW = C_INV + 4 * 16
C_RW_MASK = C_RW
C_RW_LEVEL = C_RW_MASK + 2 * P
C_RW_CHUNK = C_RW_LEVEL + 6 * P
C_ODD = C_RW_CHUNK + T
C_TIME = C_ODD + P
C_FLIP = C_TIME + T
C_COLS = C_FLIP + P
CHUNK = 64


def constants():
    c = np.zeros((P, C_COLS), np.float32)
    i, j = np.arange(P)[:, None], np.arange(P)[None, :]
    c[:, C_IDENT:C_IDENT + P] = i == j
    c[:, C_HEAD:C_HEAD + P] = i // 64 == j // 64
    c[:, C_ONES:C_ONES + P] = 1
    c[:, C_SB:C_SB + P] = i < j
    c[:, C_SB + P:C_SB + 2 * P] = np.where(i < j, 0, NEG)
    c[:, C_SB + 2 * P:C_SB + 3 * P] = -(i >= j).astype(np.float32)
    c[:, C_SB + 3 * P:C_SB + 4 * P] = -1
    for g in range(4):
        c[:, C_INV + 16 * g:C_INV + 16 * g + 16] = 1.0 / np.minimum(np.arange(1, 17), 2 << g)
    same = i // CHUNK == j // CHUNK
    c[:, C_RW_MASK:C_RW_MASK + P] = same & (i < j)
    c[:, C_RW_MASK + P:C_RW_MASK + 2 * P] = same & (i <= j)
    for lv in range(6):
        c[:, C_RW_LEVEL + lv * P:C_RW_LEVEL + (lv + 1) * P] = (
            (i >> (lv + 1) == j >> (lv + 1)) & ((i >> lv) % 2 == 0) & ((j >> lv) % 2 == 1))
    c[:, C_RW_CHUNK:C_RW_CHUNK + T] = np.arange(T) % CHUNK != 0
    c[:, C_ODD:C_ODD + P] = np.where(j > i, NEG, 0)
    c[:, C_TIME:C_TIME + T] = np.arange(1, T + 1)
    c[:, C_FLIP:C_FLIP + P] = i + j == P - 1
    return c


def slots(arena, first, count=1):
    return arena[:, first * T:(first + count) * T]


class Order:

    def __init__(self, eng, sem, base=0):
        self.eng, self.sem, self.base, self.turn, self.per, self.k = eng, sem, base, 0, 0, 0

    def loop(self, turn, per):
        self.turn, self.per, self.k = turn, per, 0

    def check(self):
        assert self.k == self.per, f"{self.k} increments, not {self.per}"

    def done(self, ins):
        ins.then_inc(self.sem, 1)
        self.k += 1
        return self.turn * self.per + (self.base + self.k)

    def then(self, ins):
        self.eng.wait_ge(self.sem, self.done(ins))


class Steps:

    def __init__(self, sem, names):
        self.sem, self.names = sem, names.split()
        assert len(set(self.names)) == len(self.names)

    def start(self, unit):
        self.unit, self.k = unit, 0

    def mark(self, ins, name):
        assert self.names[self.k] == name, (self.names[self.k], name)
        ins.then_inc(self.sem, 1)
        self.k += 1

    def finish(self):
        assert self.k == len(self.names), self.names[self.k]

    def wait(self, eng, name, unit):
        eng.wait_ge(self.sem, unit * len(self.names) + (self.names.index(name) + 1))

    def wait_before(self, eng, unit):
        if not (isinstance(unit, int) and unit == 0):
            eng.wait_ge(self.sem, unit * len(self.names))


def build_program(nc, stream, x, params, consts, rel_bias, lora, pool_w, s5_b, s5_c, out):
    with ExitStack() as ctx:
        def sb(name, shape, dt=F32):
            return ctx.enter_context(nc.sbuf_tensor(name, shape, dt))

        def sem(name):
            return ctx.enter_context(nc.semaphore(name))

        act_hi = sb("act_hi", [P, KT, T], F32R)
        act_lo = sb("act_lo", [P, KT, T], F32R)
        mix = sb("mix", [P, KT * T])
        raw = sb("raw", [P, 2, HK, P])
        w_hi = sb("w_hi", [P, 4, HK, P], F32R)
        w_lo = sb("w_lo", [P, 4, HK, P], F32R)
        arena = sb("arena", [P, 30 * T])
        ident = sb("ident", [P, P])
        head_ones = sb("head_ones", [P, P])
        ones = sb("ones", [P, P])
        prm = sb("prm", [P, PRM_COLS])
        eps = sb("eps", [P, 8])
        ps = ctx.enter_context(nc.psum_tensor("ps", [P, 8, T], F32))
        psf = ps[:, :, :].rearrange("p b t -> p (b t)")
        residual = nc.dram_tensor("residual", (KT, P, T), F32, kind="Internal").ap()

        raw_loaded = [sem("raw_loaded0"), sem("raw_loaded1")]
        cast_done = sem("cast_done")
        split_done = sem("split_done")
        pe_half = sem("pe_half")
        evac_act = sem("evac_act")
        evac_dve = sem("evac_dve")
        consts_loaded = sem("consts_loaded")
        eps_set = sem("eps_set")
        x_loaded = sem("x_loaded")
        x_turned = sem("x_turned")
        x_tile = sem("x_tile")
        res_stored = sem("res_stored")
        res_loaded = [sem("res_loaded0"), sem("res_loaded1")]
        norm_sq = sem("norm_sq")
        norm_acc = sem("norm_acc")
        norm_mm = sem("norm_mm")
        norm_root = sem("norm_root")
        norm_rstd = sem("norm_rstd")
        norm_t = sem("norm_t")
        norm_hi = sem("norm_hi")
        norm_lo = sem("norm_lo")
        mix_hi = sem("mix_hi")
        mix_lo = sem("mix_lo")
        met = sem("met")
        sb_const = sem("sb_const")
        sb_sq = sem("sb_sq")
        sb_sum = sem("sb_sum")
        sb_root = sem("sb_root")
        sb_qk = sem("sb_qk")
        sb_turn = sem("sb_turn")
        sb_vn = sem("sb_vn")
        sb_z = sem("sb_z")
        sb_dve = sem("sb_dve")
        sb_n = sem("sb_n")
        sb_e = sem("sb_e")
        sb_l = sem("sb_l")
        sb_sp = sem("sb_sp")
        sb_tri = sem("sb_tri")
        sb_neg = sem("sb_neg")
        sb_w = sem("sb_w")
        sb_pv = sem("sb_pv")
        sb_mix = sem("sb_mix")
        pl_dve = sem("pl_dve")
        pl_const = sem("pl_const")
        pl_d = sem("pl_d")
        pl_y = sem("pl_y")
        pl_mix = sem("pl_mix")
        out_turned = sem("out_turned")
        out_copied = sem("out_copied")
        out_stored = sem("out_stored")

        block = ctx.enter_context(nc.Block())

        def meet(eng, k):
            eng.drain().then_inc(met, 1)
            eng.wait_ge(met, 3 * k)

        @block.sync
        def _(sp):
            sp.dma_start(ident[:], consts[:, C_IDENT:C_IDENT + P]).then_inc(consts_loaded, 16)
            sp.dma_start(head_ones[:], consts[:, C_HEAD:C_HEAD + P]).then_inc(consts_loaded, 16)
            sp.dma_start(ones[:], consts[:, C_ONES:C_ONES + P]).then_inc(consts_loaded, 16)
            sp.dma_start(prm[:], params).then_inc(consts_loaded, 16)

            def load(tile, h):
                return sp.dma_start(raw[:, h, :, :].rearrange("p k c -> p (k c)"),
                                    stream[bass.ds(tile, 1), h, :, :].rearrange("a p w -> (a p) w"))
            load(0, 0).then_inc(raw_loaded[0], 16)
            load(0, 1).then_inc(raw_loaded[1], 16)
            with sp.Fori(1, N_TILES) as n:
                for h in range(2):
                    sp.wait_ge(split_done, n * 2 + h - 1)
                    load(n, h).then_inc(raw_loaded[h], 16)

        def gemm(pe, n, par, free=None, act_ready=None, halves=(0, 1), outputs=1):
            for h in halves:
                if h == 0 or outputs == 2:
                    if free is not None:
                        pe.wait_ge(free[0], free[1] + (h if outputs == 2 else 0))
                bank = h if outputs == 2 else par
                slot = 2 * par + h
                pe.wait_ge(split_done, n * 2 + h + 1)
                for j in range(HK):
                    kt = j if outputs == 2 else HK * h + j
                    if act_ready is not None and (outputs == 1 or h == 0):
                        pe.wait_ge(act_ready[0], act_ready[1] + kt + 1)
                    dst = ps[:, bank, :]
                    first = kt == 0
                    last = kt == (HK - 1 if outputs == 2 else KT - 1)
                    pe.matmul(dst, w_hi[:, slot, j, :], act_hi[:, kt, :], start=first, stop=False)
                    pe.matmul(dst, w_lo[:, slot, j, :], act_hi[:, kt, :], start=False, stop=False)
                    mm = pe.matmul(dst, w_hi[:, slot, j, :], act_lo[:, kt, :], start=False,
                                   stop=last)
                mm.then_inc(pe_half, 1)

        def gemm_two(pe, n, ready, count):
            pe.wait_ge(split_done, n * 2 + 4)
            for kt in range(KT):
                h, j = kt // HK, kt % HK
                pe.wait_ge(ready, count + kt + 1)
                for tile in (n, n + 1):
                    dst, slot = ps[:, tile % 2, :], 2 * (tile % 2) + h
                    a = pe.matmul(dst, w_hi[:, slot, j, :], act_hi[:, kt, :], start=kt == 0, stop=False)
                    pe.matmul(dst, w_lo[:, slot, j, :], act_hi[:, kt, :], start=False, stop=False)
                    b = pe.matmul(dst, w_hi[:, slot, j, :], act_lo[:, kt, :], start=False, stop=kt == KT - 1)
                    if tile == n and j == HK - 1:
                        b.then_inc(pe_half, 1)
                    if tile > n and kt == KT - 1:
                        a.then_inc(pe_half, 1)
                        b.then_inc(pe_half, 1)

        sq = [slots(arena, 24), slots(arena, 25)]
        sq_sum = slots(arena, 21)
        root, rstd = slots(arena, 26), slots(arena, 27)
        norm_in = [slots(arena, 16 + j) for j in range(4)]
        res_in = [slots(arena, 22), slots(arena, 23)]

        def mix_tile(ft):
            return mix[:, bass.ds(ft * T, T)] if not isinstance(ft, int) else mix[:, ft * T:(ft + 1) * T]

        def norm_tensor(pe, norm):
            pe.wait_ge(norm_acc, KT * (norm + 1))
            pe.matmul(ps[:, 7, :], ones[:], sq_sum, start=True, stop=True).then_inc(norm_mm, 1)

        def accumulate(dve, norm, ft, j):
            dve.wait_ge(norm_sq, ft + (KT * norm + 1))
            if isinstance(ft, int) and ft == 0:
                if norm:
                    dve.wait_ge(norm_mm, norm)
                nc.vector.tensor_copy(sq_sum, sq[j]).then_inc(norm_acc, 1)
            else:
                dve.wait_ge(norm_acc, ft + KT * norm)
                nc.vector.tensor_tensor(sq_sum, sq_sum, sq[j], ALU.add).then_inc(norm_acc, 1)

        def out_tensor(pe, layer, n0, before):
            pe.wait_ge(evac_act, before)
            gemm_two(pe, n0, mix_lo, KT * layer)
            with pe.Fori(1, KT // 2) as two:
                ft = two * 2
                for j in range(2):
                    gemm(pe, ft + (n0 + j), (n0 + j) % 2, free=(evac_dve, ft + (KT * layer + j - 1)))
            norm_tensor(pe, layer + 1)

        def out_vector(dve, layer, n0):
            def pair(ft):
                for j in range(2):
                    dve.wait_ge(res_loaded[j], ft * 8 + (16 * 8 * layer + 16))
                    dve.wait_ge(pe_half, ft * 2 + (2 * (n0 + j) + 2))
                    nc.vector.tensor_tensor(mix_tile(ft + j), ps[:, (n0 + j) % 2, :], res_in[j],
                                            ALU.add).then_inc(evac_dve, 1)
                    if j or not isinstance(ft, int):
                        accumulate(dve, layer + 1, ft + (j - 1), 1 - j)

            pair(0)
            with dve.Fori(1, KT // 2) as two:
                pair(two * 2)
            accumulate(dve, layer + 1, KT - 1, 1)

        def res_load(act, ft, j):
            return act.dma_start(res_in[j], residual[bass.ds(ft, 1), :, :].rearrange("a p t -> (a p) t"))

        def res_store(act, ft):
            return act.dma_start(residual[bass.ds(ft, 1), :, :].rearrange("a p t -> (a p) t"), mix_tile(ft))

        def square(act, norm, ft, j):
            if not (isinstance(ft, int) and ft < 2):
                act.wait_ge(norm_acc, ft + (KT * norm - 1))
            nc.scalar.activation(sq[j], mix_tile(ft), ACT.Square).then_inc(norm_sq, 1)

        def out_scalar(act, layer, n0):
            last_layer = layer == 2
            act.wait_ge(res_stored, 16 * KT * (layer + 1))
            for j in range(2):
                res_load(act, j, j).then_inc(res_loaded[j], 16)

            def tile(ft, j, more=True):
                if more:
                    cast(act, ft * 2 + 2 * (n0 + j + 2), (2 * (n0 + j)) % 4)
                act.wait_ge(evac_dve, ft + (KT * layer + j + 1))
                square(act, layer + 1, ft + j, j)
                if not last_layer:
                    res_store(act, ft + j).then_inc(res_stored, 16)
                if more:
                    cast(act, ft * 2 + (2 * (n0 + j + 2) + 1), (2 * (n0 + j) + 1) % 4)

            for j in range(2):
                tile(0, j)
                res_load(act, 2 + j, j).then_inc(res_loaded[j], 16)
            with act.Fori(1, KT // 2 - 1) as two:
                ft = two * 2
                for j in range(2):
                    tile(ft, j)
                    res_load(act, ft + 2 + j, j).then_inc(res_loaded[j], 16)
            for j in range(2):
                tile(KT - 2, j, more=not last_layer)
            if not last_layer:
                act.wait_ge(res_stored, 16 * KT * (layer + 2))

        def mix_split_scalar(act, layer):
            act.wait_ge(pe_half, 2 * (N_OUT1, N_OUT2, N_OUT3)[layer])
            with act.Fori(0, KT) as ft:
                nc.scalar.activation(act_hi[:, bass.ds(ft, 1), :].rearrange("p a t -> p (a t)"),
                                     mix_tile(ft), ACT.Copy).then_inc(mix_hi, 1)

        def mix_split_vector(dve, layer):
            with dve.Fori(0, KT) as ft:
                dve.wait_ge(mix_hi, ft + (KT * layer + 1))
                nc.vector.tensor_tensor(act_lo[:, bass.ds(ft, 1), :].rearrange("p a t -> p (a t)"),
                                        mix_tile(ft),
                                        act_hi[:, bass.ds(ft, 1), :].rearrange("p a t -> p (a t)").bitcast(F32),
                                        ALU.subtract).then_inc(mix_lo, 1)

        def norm_scalar(act, norm):
            act.wait_ge(norm_mm, norm + 1)
            nc.scalar.activation(root, ps[:, 7, :], ACT.Sqrt, bias=eps[:, 1:2],
                                 scale=1.0 / D).then_inc(norm_root, 1)
            if norm == 3:
                return
            with act.Fori(0, KT // 4) as four:
                ft = four * 4
                for j in range(4):
                    act.wait_ge(norm_t, ft + (KT * norm + j + 1))
                    nc.scalar.activation(act_hi[:, bass.ds(ft + j, 1), :].rearrange("p a t -> p (a t)"),
                                         norm_in[j], ACT.Copy).then_inc(norm_hi, 1)

        def norm_vector(dve, norm):
            dve.wait_ge(norm_root, norm + 1)
            nc.vector.reciprocal(rstd, root).then_inc(norm_rstd, 1)
            dve.wait_ge(norm_rstd, norm + 1)

            def four_tiles(ft):
                for j in range(4):
                    if not (isinstance(ft, int) and ft == 0):
                        if norm == 3:
                            dve.wait_ge(out_turned, ft + (j - 3))
                        else:
                            dve.wait_ge(norm_lo, ft + (KT * norm + j - 3))
                    nc.vector.scalar_tensor_tensor(
                        out=norm_in[j], in0=mix_tile(ft + j), scalar=prm[:, bass.ds(ft + (PRM_G + KT * norm + j), 1)],
                        in1=rstd, op0=ALU.mult, op1=ALU.mult).then_inc(norm_t, 1)

            four_tiles(0)
            with dve.Fori(1, KT // 4) as four:
                four_tiles(four * 4)

        def norm_gpsimd(pool, norm):
            for ft in range(KT):
                pool.wait_ge(norm_hi, KT * norm + ft + 1)
                nc.gpsimd.tensor_tensor(act_lo[:, ft, :], norm_in[ft % 4], act_hi[:, ft, :].bitcast(F32),
                                        ALU.subtract).then_inc(norm_lo, 1)

        def cast(act, m, s):
            act.wait_ge(raw_loaded[s % 2], (m - s) * 8 + (16 * (s // 2) + 16))
            if not (isinstance(m, int) and m < 4):
                act.wait_ge(pe_half, m - 3)
            nc.scalar.activation(w_hi[:, s, :, :], raw[:, s % 2, :, :], ACT.Copy).then_inc(cast_done, 1)

        def taken(act, n, par, body):
            cast(act, n * 2 + 4, (2 * par) % 4)
            act.wait_ge(pe_half, n * 2 + 2)
            body().then_inc(evac_act, 1)
            cast(act, n * 2 + 5, (2 * par + 1) % 4)

        x_in = slots(arena, 0, 16).rearrange("p (b d) -> p b d", b=TB)

        def load_tensor(pe):
            pe.wait_ge(consts_loaded, 64)
            pe.wait_ge(x_loaded, 64)
            for ft in range(KT):
                if ft >= 2:
                    pe.wait_ge(x_tile, ft - 1)
                for b in range(TB):
                    mm = pe.transpose(ps[:, 2 + ft % 2, b * P:(b + 1) * P],
                                      x_in[:, b, ft * P:(ft + 1) * P], ident[:])
                mm.then_inc(x_turned, 1)
            norm_tensor(pe, 0)

        def load_vector(dve):
            for ft in range(KT):
                dve.wait_ge(x_turned, ft + 1)
                nc.vector.tensor_copy(mix_tile(ft), ps[:, 2 + ft % 2, :]).then_inc(x_tile, 1)
                if ft:
                    accumulate(dve, 0, ft - 1, (ft - 1) % 2)
            accumulate(dve, 0, KT - 1, 1)

        def load_scalar(act):
            for b in range(TB):
                act.dma_start(x_in[:, b, :], x[b * P:(b + 1) * P, :]).then_inc(x_loaded, 16)
            act.wait_ge(eps_set, 1)
            for m in range(4):
                cast(act, m, m)
            for ft in range(KT):
                act.wait_ge(x_tile, ft + 1)
                if ft >= 2:
                    act.wait_ge(norm_acc, ft - 1)
                nc.scalar.activation(sq[ft % 2], mix_tile(ft), ACT.Square).then_inc(norm_sq, 1)
                res_store(act, ft).then_inc(res_stored, 16)
            act.wait_ge(res_stored, 16 * KT)

        pl_raw, pl_gate = slots(arena, 0), slots(arena, 1)
        pl_w = slots(arena, 2).rearrange("p (g d) -> p g d", g=POOL_GROUPS)
        pl_inv = slots(arena, 3)[:, 0:POOL_GROUPS * 16].rearrange("p (g t) -> p g t", g=POOL_GROUPS)
        pl_sum = [slots(arena, 4), slots(arena, 5)]
        pl_in = slots(arena, 6)

        def pool_tensor(pe):
            for g in range(POOL_GROUPS):
                for n in range(N_POOL + 2 * g + 2, N_POOL + 2 * g + 4):
                    gemm(pe, n, n % 2, free=(evac_act, n - 1))
                if g == 0:
                    pe.wait_ge(pl_const, 32)
                pe.wait_ge(pl_d, g + 1)
                if g >= 1:
                    pe.wait_ge(pl_mix, g)
                pe.matmul(ps[:, 2, :], pl_w[:, g, :], pl_in, start=True, stop=True).then_inc(pl_y, 1)

        def pool_scalar(act):
            act.dma_start(pl_w, pool_w.rearrange("g c d -> c g d")).then_inc(pl_const, 16)
            act.dma_start(slots(arena, 3)[:, 0:POOL_GROUPS * 16],
                          consts[:, C_INV:C_INV + POOL_GROUPS * 16]).then_inc(pl_const, 16)
            for g in range(POOL_GROUPS):
                n = N_POOL + 2 * g
                if g >= 1:
                    act.wait_ge(pl_d, g)
                taken(act, n, n % 2, lambda: nc.scalar.activation(pl_raw, ps[:, n % 2, :], ACT.Copy))
                if g >= 1:
                    act.wait_ge(pl_mix, g)
                n += 1
                taken(act, n, n % 2, lambda: nc.scalar.activation(pl_gate, ps[:, n % 2, :], ACT.Silu))

        def pool_vector(dve):
            order = Order(dve, pl_dve)
            dve.wait_ge(pl_const, 32)
            for g in range(POOL_GROUPS):
                window = 2 << g
                n = N_POOL + 2 * g
                dve.wait_ge(evac_act, n + 1)
                cur, shift, k = pl_raw, 1, 0
                while shift < window:
                    nxt = pl_sum[k % 2]
                    order.done(nc.vector.tensor_copy(nxt[:, 0:shift], cur[:, 0:shift]))
                    order.then(nc.vector.tensor_tensor(nxt[:, shift:T], cur[:, shift:T],
                                                       cur[:, 0:T - shift], ALU.add))
                    cur, shift, k = nxt, 2 * shift, k + 1
                if g >= 1:
                    dve.wait_ge(pl_y, g)
                mean = pl_sum[k % 2]
                order.done(nc.vector.tensor_tensor(mean[:, 0:16], cur[:, 0:16], pl_inv[:, g, :], ALU.mult))
                order.then(nc.vector.tensor_scalar(mean[:, 16:T], cur[:, 16:T], 1.0 / window, None, ALU.mult))
                nc.vector.tensor_tensor(pl_in, mean, pl_raw, ALU.subtract).then_inc(pl_d, 1)
                dve.wait_ge(pl_d, g + 1)
                dve.wait_ge(pl_y, g + 1)
                dve.wait_ge(evac_act, n + 2)
                nc.vector.scalar_tensor_tensor(
                    out=mix_tile(6 + g), in0=ps[:, 2, :], scalar=prm[:, PRM_POOL + g:PRM_POOL + g + 1],
                    in1=pl_gate, op0=ALU.mult, op1=ALU.mult).then_inc(pl_mix, 1)

        sq_q, sq_k = slots(arena, 7), slots(arena, 8)
        sb_q, sb_k, sb_v, sb_gate = (slots(arena, i) for i in range(4))
        sb_qn, sb_kn, sb_vt = (slots(arena, i) for i in range(4, 7))
        sb_rt = [slots(arena, 9), slots(arena, 10)]
        ZW = 1280
        sb_m, sb_l_, sb_spt, sb_wt = (slots(arena, i, 3)[:, 0:ZW] for i in (11, 14, 17, 20))
        sb_c = slots(arena, 23)
        c_valid, c_neg, c_ntri, c_nones = (sb_c[:, i * P:(i + 1) * P] for i in range(4))
        ZOFF = (0, 512, 1024, 896)
        zb = psf[:, 2 * T:2 * T + ZW]

        def diag(view, which):
            if which == 0:
                return view[:, 0:1152].rearrange("p (a b) -> p a b", b=128)[:, 0:9:4, :]
            return view[:, 896:1024].rearrange("p (a b) -> p a b", a=1)

        def sb_tensor(pe):
            pe.wait_ge(sb_const, 16)

            def sums(u):
                pe.wait_ge(sb_sq, u * 2 + 1)
                pe.matmul(ps[:, 6, :], head_ones[:], sq_q, start=True, stop=True).then_inc(sb_sum, 1)
                pe.wait_ge(sb_sq, u * 2 + 2)
                pe.matmul(ps[:, 7, :], head_ones[:], sq_k, start=True, stop=True).then_inc(sb_sum, 1)

            def unit(u, more):
                n = u * 4 + N_SB
                pe.wait_ge(evac_act, n + 3)
                pe.wait_ge(sb_root, u * 2 + 2)
                for b in range(TB):
                    mm = pe.transpose(ps[:, 7, b * P:(b + 1) * P], sb_v[:, b * P:(b + 1) * P], ident[:])
                mm.then_inc(sb_turn, 1)
                for hd in range(2):
                    rows = slice(64 * hd, 64 * hd + 64)
                    if more:
                        gemm(pe, n + (4 + 2 * hd), 1, free=(evac_act, n + (3 + 2 * hd)))
                    pe.wait_ge(sb_qk, u * 2 + 2)
                    if not (isinstance(u, int) and u == 0 and hd == 0):
                        pe.wait_ge(sb_w, u * 2 + hd)
                    for kb in range(TB):
                        mm = pe.matmul(ps_z(kb, kb), sb_kn[rows, kb * P:(kb + 1) * P],
                                       sb_qn[rows, kb * P:T], start=kb != 3, stop=False,
                                       skip_group_check=True)
                    mm.then_inc(sb_z, 1)
                    if more:
                        gemm(pe, n + (5 + 2 * hd), 0, free=(evac_act, n + (4 + 2 * hd)))
                    pe.wait_ge(sb_sp, u * 4 + (2 * hd + 2))
                    for kb in range(TB):
                        for jb in range(kb, TB):
                            mm = pe.matmul(ps_z(kb, jb), c_ntri if jb == kb else c_nones,
                                           sb_spt[:, ZOFF[jb]:ZOFF[jb] + (TB - jb) * P],
                                           start=False, stop=True, skip_group_check=True)
                    mm.then_inc(sb_tri, 1)
                    pe.wait_ge(sb_vn, u + 1)
                    if hd and more:
                        sums(u + 1)
                    if hd == 0 and not (isinstance(u, int) and u == 0):
                        pe.wait_ge(sb_mix, u)
                    pe.wait_ge(sb_w, u * 2 + hd + 1)
                    for kb in range(TB):
                        mm = pe.matmul(ps[rows, 5, kb * P:T],
                                       sb_vt[:, kb * P + 64 * hd:kb * P + 64 * hd + 64],
                                       sb_wt[:, ZOFF[kb]:ZOFF[kb] + (TB - kb) * P],
                                       start=kb == 0, stop=kb == TB - 1, skip_group_check=True)
                    mm.then_inc(sb_pv, 1)

            def ps_z(kb, jb):
                return zb[:, ZOFF[kb] + (jb - kb) * P:ZOFF[kb] + (TB - kb) * P]

            for j in (2, 3):
                gemm(pe, N_SB + j, (N_SB + j) % 2, free=(evac_act, N_SB + j - 1))
            sums(0)
            unit(0, True)
            with pe.Fori(1, SB_PAIRS - 1) as u:
                unit(u, True)
            unit(SB_PAIRS - 1, False)

        def sb_scalar(act):
            def take(u, j):
                n = u * 4 + (N_SB + j)
                par = (N_SB + j) % 2
                if j < 3:
                    dst, fn = (sb_q, sb_k, sb_v)[j], ACT.Copy
                else:
                    dst, fn = sb_gate, ACT.Silu
                taken(act, n, par, lambda: nc.scalar.activation(dst, ps[:, par, :], fn))

            def unit(u, more):
                if not (isinstance(u, int) and u == 0):
                    act.wait_ge(sb_qk, u * 2)
                act.wait_ge(sb_sum, u * 2 + 1)
                nc.scalar.activation(sb_rt[0], ps[:, 6, :], ACT.Sqrt, bias=eps[:, 0:1],
                                     scale=1.0).then_inc(sb_root, 1)
                act.wait_ge(sb_sum, u * 2 + 2)
                nc.scalar.activation(sb_rt[1], ps[:, 7, :], ACT.Sqrt, bias=eps[:, 1:2],
                                     scale=1.0 / 64).then_inc(sb_root, 1)
                if not (isinstance(u, int) and u == 0):
                    act.wait_ge(sb_mix, u)
                    take(u, 3)
                act.wait_ge(sb_turn, u + 1)
                if not (isinstance(u, int) and u == 0):
                    act.wait_ge(sb_pv, u * 2)
                nc.scalar.activation(sb_vt, ps[:, 7, :], ACT.Copy).then_inc(sb_vn, 1)
                for hd in range(2):
                    if more:
                        if hd == 0:
                            act.wait_ge(sb_qk, u * 2 + 1)
                            take(u + 1, 0)
                        else:
                            act.wait_ge(sb_vn, u + 1)
                            take(u + 1, 2)
                            squares(u + 1)
                    act.wait_ge(sb_n, u * 2 + hd + 1)
                    if not (isinstance(u, int) and u == 0 and hd == 0):
                        act.wait_ge(sb_sp, u * 4 + 2 * hd)
                    nc.scalar.activation(sb_l_, sb_spt, ACT.Exp).then_inc(sb_e, 1)
                    act.wait_ge(sb_e, u * 2 + hd + 1)
                    nc.scalar.activation(sb_l_, sb_l_, ACT.Ln, bias=eps[:, 3:4]).then_inc(sb_l, 1)
                    if more:
                        if hd == 0:
                            act.wait_ge(sb_qk, u * 2 + 2)
                            take(u + 1, 1)
                    act.wait_ge(sb_neg, u * 4 + 2 * hd + 2)
                    if not (isinstance(u, int) and u == 0 and hd == 0):
                        act.wait_ge(sb_pv, u * 2 + hd)
                    nc.scalar.activation(sb_wt, zb, ACT.Exp).then_inc(sb_w, 1)

            def squares(u):
                act.wait_ge(evac_act, u * 4 + (N_SB + 2))
                if not (isinstance(u, int) and u == 0):
                    act.wait_ge(sb_sum, u * 2)
                nc.scalar.activation(sq_q, sb_q, ACT.Square).then_inc(sb_sq, 1)
                nc.scalar.activation(sq_k, sb_k, ACT.Square).then_inc(sb_sq, 1)

            act.dma_start(sb_c, consts[:, C_SB:C_SB + T]).then_inc(sb_const, 16)
            for j in range(4):
                take(0, j)
            squares(0)
            unit(0, True)
            with act.Fori(1, SB_PAIRS - 1) as u:
                unit(u, True)
            unit(SB_PAIRS - 1, False)

        def sb_vector(dve):
            dve.wait_ge(sb_const, 16)
            order = Order(dve, sb_dve)

            def unit(u):
                order.loop(u, 6)
                for i, (src, dst, g) in enumerate(((sb_q, sb_qn, PRM_QN), (sb_k, sb_kn, PRM_KN))):
                    dve.wait_ge(sb_root, u * 2 + i + 1)
                    order.then(nc.vector.reciprocal(sb_rt[i], sb_rt[i]))
                    if not (isinstance(u, int) and u == 0):
                        dve.wait_ge(sb_z, u * 2)
                    nc.vector.scalar_tensor_tensor(out=dst, in0=src, scalar=prm[:, g:g + 1], in1=sb_rt[i],
                                                   op0=ALU.mult, op1=ALU.mult).then_inc(sb_qk, 1)
                for hd in range(2):
                    dve.wait_ge(sb_z, u * 2 + hd + 1)
                    if not (isinstance(u, int) and u == 0 and hd == 0):
                        dve.wait_ge(sb_tri, u * 2 + hd)
                    order.then(nc.vector.tensor_scalar(sb_m, zb, 0.0, None, ALU.max))
                    nc.vector.scalar_tensor_tensor(out=sb_spt, in0=sb_m, scalar=-2.0, in1=zb,
                                                   op0=ALU.mult, op1=ALU.add).then_inc(sb_n, 1)
                    dve.wait_ge(sb_l, u * 2 + hd + 1)
                    order.then(nc.vector.tensor_tensor(sb_spt, sb_m, sb_l_, ALU.add))
                    for which, n in ((0, 3), (1, 1)):
                        d = diag(sb_spt, which)
                        ins = nc.vector.tensor_tensor(
                            d, d, c_valid.rearrange("p (a b) -> p a b", a=1).broadcast_to([P, n, P]), ALU.mult)
                        ins.then_inc(sb_sp, 1)
                    dve.wait_ge(sb_tri, u * 2 + hd + 1)
                    for which, n in ((0, 3), (1, 1)):
                        d = diag(zb, which)
                        nc.vector.tensor_tensor(
                            d, d, c_neg.rearrange("p (a b) -> p a b", a=1).broadcast_to([P, n, P]),
                            ALU.add).then_inc(sb_neg, 1)
                dve.wait_ge(sb_pv, u * 2 + 2)
                dve.wait_ge(evac_act, u * 4 + (N_SB + 4))
                nc.vector.tensor_tensor(mix_tile(u + 10), ps[:, 5, :], sb_gate, ALU.mult).then_inc(sb_mix, 1)
                order.check()

            unit(0)
            with dve.Fori(1, SB_PAIRS - 1) as u:
                unit(u)
            unit(SB_PAIRS - 1)

        LEVELS = 6
        NB = T // P
        NC = T // CHUNK
        rw_pc = sb("rw_pc", [P, NC])
        rw_fold = sb("rw_fold", [P, CHUNK])
        rw_up = sb("rw_up", [P, P])
        rw_pre = sem("rw_pre")
        rw_folded = sem("rw_folded")
        rw_up_loaded = sem("rw_up_loaded")
        rw_consts = sem("rw_consts")
        rw_shift = Steps(sem("rw_shift"), " ".join(f"d_{s_} d0_{s_} s_{s_}" for s_ in "rkvg"))
        dve_names = ["kk0", "cs", "csp", "t", "kn", "rk", "qr_r", "pc", "kdt", "kkmax", "kkrec", "kk", "qr_k",
                      "b", "bt", "bon", "ln0", "mq0", "ln1", "mq1"]
        dve_names += ["lt0_0", "lt0_1", "z0_0", "z0_1"]
        for e in range(2):
            dve_names += [f"x0_{e}", f"lt1_{e}"]
        for lv in range(1, LEVELS):
            if lv < LEVELS - 1:
                dve_names += [f"lt{lv + 1}_0", f"lt{lv + 1}_1", f"x{lv}_0", f"x{lv}_1"]
            dve_names += [f"z{lv}_0", f"z{lv}_1"]
        dve_names += ["zero", "at0_0", "at0_1", "f0", "at1_0", "at1_1", "f1"]
        dve_names += [f"st{c}" for c in range(1, NC - 1)]
        dve_names += ["rg", "yc", "vrec", "yn", "ynb", "mix"]
        rw_dve = Steps(sem("rw_dve"), " ".join(dve_names))
        rw_act = Steps(sem("rw_act"), "sg a kksq p pinv pprev kkroot n_kq n_b n_kd n_v gs "
                       + " ".join(f"u{lv}_{e}" for lv in range(1, LEVELS) for e in range(2))
                       + " mv gh0 gh1 y0 y1 ysq vroot")
        rw_pe = Steps(sem("rw_pe"), "w a kksum bonus t_kq t_b t_kd t_v ln0 mq0 ln1 mq1 u0_0 u0_1 "
                      + " ".join(f"u{lv}_0 u{lv}_1 " + (f"x{lv}_0 x{lv}_1 " if lv < LEVELS - 1 else "")
                                 + f"z{lv}_0 z{lv}_1" for lv in range(1, LEVELS))
                      + " mv gh0 gh1 ng atf " + " ".join(f"st{c}" for c in range(1, NC - 1))
                      + " y mu var")

        def spare(i, count=1):
            return mix[:, (6 + i) * T:(6 + i + count) * T]

        rw_tw = slots(arena, 0)
        rw_raw = [slots(arena, 1 + j) for j in range(4)]
        rw_r, rw_k, rw_v = rw_raw[0:3]
        rw_gate = slots(arena, 8)
        rw_tmp, rw_sg, rw_cs, rw_p, rw_pinv, rw_pprev, rw_a, rw_kk, rw_kn = (
            slots(arena, 9 + j) for j in range(9))
        rw_qr = slots(arena, 18, 2).rearrange("p (g a t) -> p g a t", g=NB, a=2)
        rw_bt, rw_kdt, rw_bon, rw_sq = (slots(arena, 20 + j) for j in range(4))
        rw_km = spare(0, 2).rearrange("p (e g a c) -> p e g a c", e=2, g=NB, a=2)
        rw_bn, rw_kdn, rw_vn = (spare(2 + j).rearrange("p (g c) -> p g c", g=NB) for j in range(3))
        rw_mask = spare(5)[:, 0:2 * P]
        rw_level = spare(6, 2)[:, 0:LEVELS * P]
        rw_chunk = spare(8)
        rw_ln = [slots(arena, 9 + 2 * e, 2).rearrange("p (g a t) -> p g a t", g=NB, a=2) for e in range(2)]
        rw_mq = [slots(arena, 13 + 2 * e, 2).rearrange("p (g a t) -> p g a t", g=NB, a=2) for e in range(2)]
        rw_x = [slots(arena, 24), slots(arena, 25)]
        rw_z = [slots(arena, 26), slots(arena, 27)]
        rw_u = [slots(arena, 28), slots(arena, 29)]
        rw_lt = [slots(arena, 17), slots(arena, 5)]
        rw_gh = [slots(arena, 6), slots(arena, 7)]
        rw_at = slots(arena, 24, 2).rearrange("p (c w) -> p c w", c=NC)
        rw_state = slots(arena, 20).rearrange("p (c w) -> p c w", c=NC)
        rw_rg, rw_y = slots(arena, 28), slots(arena, 29)
        rw_yc, rw_ysq, rw_vr = slots(arena, 24), slots(arena, 26), slots(arena, 27)

        def blocks(view):
            return view.rearrange("p (g t) -> p g t", g=NB)

        def over_blocks(view, width):
            return view.rearrange("p (a w) -> p a w", a=1).broadcast_to([P, NB, width])

        def rw_col(u, j):
            return prm[:, bass.ds(u * RW_COLS + (PRM_RW + j), 1)] if not isinstance(u, int) else \
                prm[:, PRM_RW + u * RW_COLS + j:PRM_RW + u * RW_COLS + j + 1]

        def rwkv_tensor(pe):
            A, V, S = rw_act, rw_dve, rw_pe

            def unit(u, more):
                n = u * 4 + N_RWKV
                S.start(u)

                def fill(j, halves=(0, 1)):
                    if more or j < 2:
                        gemm(pe, n + (4 + j), (N_RWKV + j) % 2, free=(evac_act, n + (3 + j)), halves=halves)

                if not (isinstance(u, int) and u == 0):
                    A.wait_before(pe, u)
                pe.wait_ge(rw_up_loaded, u * 16 + 16)
                pe.wait_ge(rw_pre, 4)
                S.mark(pe.matmul(ps[:, 2, :], rw_up[0:64, :], rw_tw[0:64, :], start=True, stop=True), "w")
                S.mark(pe.matmul(ps[:, 3, :], rw_up[64:128, :], rw_tw[64:128, :], start=True,
                                 stop=True), "a")
                fill(0)
                A.wait(pe, "kksq", u)
                V.wait(pe, "kk0", u)
                S.mark(pe.matmul(ps[:, 4, :], head_ones[:], rw_sq, start=True, stop=True), "kksum")
                V.wait(pe, "rk", u)
                S.mark(pe.matmul(ps[:, 5, :], head_ones[:], rw_sg, start=True, stop=True), "bonus")
                fill(1)
                V.wait(pe, "bon", u)
                A.wait(pe, "kkroot", u)
                for bank, name, src in ((2, "t_kq", None), (3, "t_b", rw_bt), (4, "t_kd", rw_kdt),
                                        (5, "t_v", rw_v)):
                    for g in range(NB):
                        view = rw_qr[:, g, 0, :] if src is None else src[:, g * P:(g + 1) * P]
                        mm = pe.transpose(ps[:, bank, g * P:(g + 1) * P], view, ident[:])
                    S.mark(mm, name)
                for e, left, bank, name in ((0, rw_bt, 6, "ln0"), (0, rw_kdt, 2, "mq0"),
                                            (1, rw_bt, 4, "ln1"), (1, rw_kdt, 6, "mq1")):
                    rows = slice(64 * e, 64 * e + 64)
                    if bank == 2:
                        A.wait(pe, "n_b", u)
                    elif name == "ln1":
                        A.wait(pe, "n_v", u)
                    elif name == "mq1":
                        V.wait(pe, "ln0", u)
                    for g in range(NB):
                        mm = pe.matmul(psf[:, bank * T + 256 * g:bank * T + 256 * g + 256],
                                       left[rows, g * P:(g + 1) * P],
                                       rw_qr[rows, g, :, :].rearrange("p a t -> p (a t)"),
                                       start=g % 2 == 0, stop=True, skip_group_check=True)
                    S.mark(mm, name)
                for e in range(2):
                    V.wait(pe, f"lt0_{e}", u)
                    for g in range(NB):
                        mm = pe.matmul(ps[:, 2 + e, g * P:(g + 1) * P], rw_lt[e][:, g * P:(g + 1) * P],
                                       ident[:], start=True, stop=True, skip_group_check=True)
                    S.mark(mm, f"u0_{e}")
                fill(2, (0,))
                for lv in range(1, LEVELS):
                    for e in range(2):
                        V.wait(pe, f"x{lv - 1}_{e}", u)
                        V.wait(pe, f"lt{lv}_{e}", u)
                        for g in range(NB):
                            c = slice(g * P, (g + 1) * P)
                            mm = pe.matmul(ps[:, 2 + e, c], rw_lt[e][:, c], rw_x[e][:, c], start=True,
                                           stop=True, skip_group_check=True)
                        S.mark(mm, f"u{lv}_{e}")
                    for e in range(2):
                        if lv < LEVELS - 1:
                            A.wait(pe, f"u{lv}_{e}", u)
                            V.wait(pe, f"z{lv - 1}_{e}", u)
                            for g in range(NB):
                                c = slice(g * P, (g + 1) * P)
                                mm = pe.matmul(ps[:, 4 + e, c], rw_z[e][:, c], rw_u[e][:, c], start=True,
                                               stop=True, skip_group_check=True)
                            S.mark(mm, f"x{lv}_{e}")
                    for e in range(2):
                        A.wait(pe, f"u{lv}_{e}", u)
                        V.wait(pe, f"z{lv - 1}_{e}", u)
                        for g in range(NB):
                            c = slice(g * P, (g + 1) * P)
                            mm = pe.matmul(ps[:, 6 + e, c], rw_u[e][:, c], rw_z[e][:, c], start=True,
                                           stop=True, skip_group_check=True)
                        S.mark(mm, f"z{lv}_{e}")
                for e in range(2):
                    for g in range(NB):
                        mm = pe.matmul(ps[:, 2, e * 256 + g * 64:e * 256 + g * 64 + 64],
                                       rw_mq[e][:, g, 0, :], rw_vn[:, g, 64 * e:64 * e + 64],
                                       start=e == 0 and g == 0, stop=True, skip_group_check=True)
                S.mark(mm, "mv")
                A.wait(pe, "mv", u)
                for e in range(2):
                    V.wait(pe, f"z{LEVELS - 1}_{e}", u)
                    for g in range(NB):
                        c = slice(g * P, (g + 1) * P)
                        mm = pe.matmul(ps[:, 4 + e, c], rw_z[e][:, c],
                                       rw_km[:, e, g, :, :].rearrange("p a c -> p (a c)"),
                                       start=True, stop=True, skip_group_check=True)
                    S.mark(mm, f"gh{e}")
                A.wait(pe, "gh1", u)
                for e in range(2):
                    for g in range(NB):
                        mm = pe.matmul(ps[64 * e:64 * e + 64, 4, g * P:(g + 1) * P],
                                       rw_gh[e][:, g * P:g * P + 64], rw_ln[e][:, g, 1, :], start=g == 0,
                                       stop=True, skip_group_check=True)
                S.mark(mm, "ng")
                for half in range(2):
                    rows = slice(64 * half, 64 * half + 64)
                    for e in range(2):
                        o = slice(64 * e, 64 * e + 64)
                        for g in range(NB):
                            gh = rw_gh[e]
                            at = ps[o, 6 + half, g * P:g * P + 64]
                            f = ps[o, 6 + half, g * P + 64:g * P + 128]
                            pe.matmul(at, gh[rows, g * P:g * P + 64], rw_bn[rows, g, o], start=g == 0,
                                      stop=True, skip_group_check=True)
                            pe.matmul(f, rw_bn[rows, g, o], gh[rows, g * P + 64:g * P + 128], start=False,
                                      stop=False, skip_group_check=True)
                            mm = pe.matmul(f, rw_kdn[rows, g, o], rw_vn[rows, g, o], start=False, stop=True,
                                           skip_group_check=True)
                S.mark(mm, "atf")
                fill(2, (1,))
                for c in range(1, NC - 1):
                    V.wait(pe, "f1" if c == 1 else f"st{c - 1}", u)
                    mm = pe.matmul(ps[:, 2, 0:64], rw_at[:, c, :], rw_state[:, c - 1, :], start=True, stop=True)
                    S.mark(mm, f"st{c}")
                V.wait(pe, "rg", u)
                for e in range(2):
                    rows = slice(64 * e, 64 * e + 64)
                    for g in range(NB):
                        dst = ps[rows, 5 + e, g * P:(g + 1) * P]
                        pe.matmul(dst, rw_gh[e][:, g * P + 64:(g + 1) * P], rw_ln[e][:, g, 1, :],
                                  start=g == 0, stop=False, skip_group_check=True)
                        mm = pe.matmul(dst, rw_vn[:, g, rows], rw_mq[e][:, g, 1, :], start=False,
                                       stop=False, skip_group_check=True)
                    for c in range(1, NC):
                        t = slice(c * CHUNK, (c + 1) * CHUNK)
                        mm = pe.matmul(ps[rows, 5 + e, t], rw_state[rows, c - 1, :], rw_rg[rows, t],
                                       start=False, stop=True, skip_group_check=True)
                S.mark(mm, "y")
                fill(3, (0,))
                A.wait(pe, "y1", u)
                S.mark(pe.matmul(ps[:, 7, :], head_ones[:], rw_y, start=True, stop=True), "mu")
                A.wait(pe, "ysq", u)
                S.mark(pe.matmul(ps[:, 2, :], head_ones[:], rw_ysq, start=True, stop=True), "var")
                fill(3, (1,))
                S.finish()

            for n in range(N_RWKV + 1, N_RWKV + 4):
                gemm(pe, n, n % 2, free=(evac_act, n - 1))
            unit(0, True)
            with pe.Fori(1, RW_PAIRS - 1) as u:
                unit(u, True)
            unit(RW_PAIRS - 1, False)

        DECAY = float(np.exp(-0.5))

        def rwkv_scalar(act):
            A, V, S = rw_act, rw_dve, rw_pe
            for dst, c0, w in ((rw_mask, C_RW_MASK, 2 * P), (rw_level, C_RW_LEVEL, LEVELS * P),
                               (rw_chunk, C_RW_CHUNK, T)):
                act.dma_start(dst, consts[:, c0:c0 + w]).then_inc(rw_consts, 16)
            def load_up(u):
                act.dma_start(rw_up[:], lora[bass.ds(u, 1), :, :].rearrange("a p c -> (a p) c")).then_inc(
                    rw_up_loaded, 16)

            load_up(0)
            act.wait_ge(rw_pre, 3)
            nc.scalar.activation(rw_tw[0:64, :], rw_tw[0:64, :], ACT.Tanh).then_inc(rw_pre, 1)

            def take(u, j):
                par = (N_RWKV + j) % 2
                taken(act, u * 4 + (N_RWKV + j), par,
                      lambda: nc.scalar.activation(rw_raw[j], ps[:, par, :], ACT.Copy))

            def unit(u, more):
                A.start(u)

                def fill(j):
                    if more:
                        if j < 3:
                            V.wait(act, ("qr_r", "kn", "bon")[j], u)
                        if j == 2:
                            S.wait(act, "t_v", u)
                        if j == 3:
                            A.wait(act, "gs", u)
                        take(u + 1, j)

                S.wait(act, "w", u)
                A.mark(nc.scalar.activation(rw_sg, ps[:, 2, :], ACT.Sigmoid, bias=rw_col(u, RW_W0)), "sg")
                S.wait(act, "a", u)
                A.mark(nc.scalar.activation(rw_a, ps[:, 3, :], ACT.Sigmoid, bias=rw_col(u, RW_A0)), "a")
                if more:
                    load_up(u + 1)
                V.wait(act, "kk0", u)
                A.mark(nc.scalar.activation(rw_sq, rw_kk, ACT.Square), "kksq")
                V.wait(act, "cs", u)
                A.mark(nc.scalar.activation(rw_p, rw_cs, ACT.Exp, scale=-DECAY), "p")
                A.mark(nc.scalar.activation(rw_pinv, rw_cs, ACT.Exp, scale=DECAY), "pinv")
                V.wait(act, "csp", u)
                A.mark(nc.scalar.activation(rw_pprev, rw_pprev, ACT.Exp, scale=-DECAY), "pprev")
                fill(0)
                S.wait(act, "kksum", u)
                A.mark(nc.scalar.activation(rw_sq, ps[:, 4, :], ACT.Sqrt), "kkroot")
                fill(1)
                S.wait(act, "t_kq", u)
                A.mark(nc.scalar.activation(
                    rw_km[:, :, :, 0, :], ps[:, 2, :].rearrange("p (g e c) -> p e g c", g=NB, e=2),
                    ACT.Copy), "n_kq")
                for bank, name, dst in ((3, "b", rw_bn), (4, "kd", rw_kdn), (5, "v", rw_vn)):
                    S.wait(act, "t_" + name, u)
                    A.mark(nc.scalar.activation(dst, blocks(ps[:, bank, :]), ACT.Copy), "n_" + name)
                rw_shift.wait(act, "s_g", u)
                A.mark(nc.scalar.activation(rw_gate, rw_raw[3], ACT.Silu), "gs")
                for lv in range(1, LEVELS):
                    for e in range(2):
                        S.wait(act, f"u{lv}_{e}", u)
                        A.mark(nc.scalar.activation(rw_u[e], ps[:, 2 + e, :], ACT.Copy), f"u{lv}_{e}")
                S.wait(act, "mv", u)
                A.mark(nc.scalar.activation(
                    rw_km[:, :, :, 1, :], ps[:, 2, :].rearrange("p (e g c) -> p e g c", g=NB, e=2),
                    ACT.Copy), "mv")
                for e in range(2):
                    S.wait(act, f"gh{e}", u)
                    A.mark(nc.scalar.activation(rw_gh[e], ps[:, 4 + e, :], ACT.Copy), f"gh{e}")
                fill(2)
                S.wait(act, "y", u)
                for e in range(2):
                    rows = slice(64 * e, 64 * e + 64)
                    A.mark(nc.scalar.activation(rw_y[rows, :], ps[rows, 5 + e, :], ACT.Copy), f"y{e}")
                V.wait(act, "yc", u)
                A.mark(nc.scalar.activation(rw_ysq, rw_yc, ACT.Square), "ysq")
                S.wait(act, "var", u)
                A.mark(nc.scalar.activation(rw_vr, ps[:, 2, :], ACT.Sqrt, bias=eps[:, 2:3],
                                            scale=1.0 / 64), "vroot")
                fill(3)
                A.finish()

            for j in range(4):
                take(0, j)
            unit(0, True)
            with act.Fori(1, RW_PAIRS - 1) as u:
                unit(u, True)
            unit(RW_PAIRS - 1, False)

        def rwkv_vector(dve):
            A, V, S = rw_act, rw_dve, rw_pe
            tt, ts, stt = nc.vector.tensor_tensor, nc.vector.tensor_scalar, nc.vector.scalar_tensor_tensor
            order = Order(dve, rw_pre)
            dve.wait_ge(rw_consts, 16 * 3)

            def shifted(dst, src, mu, tmp, then):
                then(tt(tmp[:, 1:T], src[:, 0:T - 1], src[:, 1:T], ALU.subtract), 0)
                then(ts(tmp[:, 0:1], src[:, 0:1], -1.0, None, ALU.mult), 1)
                then(stt(out=dst, in0=tmp, scalar=mu, in1=src, op0=ALU.mult, op1=ALU.add), 2)

            dve.wait_ge(evac_act, 1)
            shifted(rw_tw, slots(arena, 29), prm[:, PRM_MU_WDAD:PRM_MU_WDAD + 1], slots(arena, 9),
                    lambda ins, _: order.then(ins))
            tt(rw_fold[:], ident[:, 0:CHUNK], ident[:, CHUNK:P], ALU.add).then_inc(rw_folded, 1)

            def shift(u, j):
                if j == 0:
                    rw_shift.start(u)

                def then(ins, i):
                    name = ("d_", "d0_", "s_")[i] + "rkvg"[j]
                    rw_shift.mark(ins, name)
                    rw_shift.wait(dve, name, u)

                dve.wait_ge(evac_act, u * 4 + (j + 2))
                shifted(rw_raw[j], rw_raw[j], rw_col(u, RW_MU + j), slots(arena, 6), then)

            def unit(u, more=True):
                V.start(u)

                def then(ins, name):
                    V.mark(ins, name)
                    V.wait(dve, name, u)

                then(ts(rw_kk, rw_k, rw_col(u, RW_KK), None, ALU.mult), "kk0")
                A.wait(dve, "sg", u)
                then(nc.vector.tensor_tensor_scan(rw_cs, rw_chunk, rw_sg, 0.0, ALU.mult, ALU.add), "cs")
                then(tt(rw_pprev, rw_cs, rw_sg, ALU.subtract), "csp")
                A.wait(dve, "a", u)
                then(ts(rw_tmp, rw_a, 1.0, rw_col(u, RW_KA), ALU.subtract, ALU.mult), "t")
                then(stt(out=rw_kn, in0=rw_tmp, scalar=1.0, in1=rw_k, op0=ALU.add, op1=ALU.mult), "kn")
                then(stt(out=rw_sg, in0=rw_r, scalar=rw_col(u, RW_RK), in1=rw_kn, op0=ALU.mult,
                         op1=ALU.mult), "rk")
                shift(u, 2)
                A.wait(dve, "p", u)
                then(tt(rw_qr[:, :, 1, :], blocks(rw_r), blocks(rw_p), ALU.mult), "qr_r")
                then(nc.vector.tensor_copy(rw_pc[:], rw_p[:, CHUNK - 1:T:CHUNK]), "pc")
                A.wait(dve, "pinv", u)
                then(tt(rw_kdt, rw_kn, rw_pinv, ALU.mult), "kdt")
                A.wait(dve, "kkroot", u)
                then(ts(rw_sq, rw_sq, 1e-12, None, ALU.max), "kkmax")
                then(nc.vector.reciprocal(rw_sq, rw_sq), "kkrec")
                then(tt(rw_kk, rw_kk, rw_sq, ALU.mult), "kk")
                A.wait(dve, "pprev", u)
                then(stt(out=rw_qr[:, :, 0, :], in0=blocks(rw_pprev), scalar=-1.0, in1=blocks(rw_kk),
                         op0=ALU.mult, op1=ALU.mult), "qr_k")
                then(tt(rw_tmp, rw_kk, rw_a, ALU.mult), "b")
                then(tt(rw_bt, rw_tmp, rw_pinv, ALU.mult), "bt")
                S.wait(dve, "bonus", u)
                then(tt(rw_bon, ps[:, 5, :], rw_v, ALU.mult), "bon")
                shift(u, 3)
                for name, bank in (("ln0", 6), ("mq0", 2), ("ln1", 4), ("mq1", 6)):
                    dst = (rw_ln if name[:2] == "ln" else rw_mq)[int(name[2])]
                    S.wait(dve, name, u)
                    then(tt(dst.rearrange("p g a t -> p g (a t)"),
                            psf[:, bank * T:(bank + 2) * T].rearrange("p (g w) -> p g w", g=NB),
                            over_blocks(rw_mask, 2 * P), ALU.mult), name)

                def level(lv, e):
                    then(tt(blocks(rw_lt[e]), rw_ln[e][:, :, 0, :],
                            over_blocks(rw_level[:, lv * P:(lv + 1) * P], P), ALU.mult), f"lt{lv}_{e}")

                for e in range(2):
                    level(0, e)
                for e in range(2):
                    then(tt(blocks(rw_z[e]), blocks(rw_lt[e]), over_blocks(ident[:], P), ALU.add), f"z0_{e}")
                for e in range(2):
                    S.wait(dve, f"u0_{e}", u)
                    then(tt(blocks(rw_x[e]), blocks(ps[:, 2 + e, :]), over_blocks(ident[:], P), ALU.add),
                         f"x0_{e}")
                    level(1, e)
                for lv in range(1, LEVELS):
                    if lv < LEVELS - 1:
                        for e in range(2):
                            S.wait(dve, f"u{lv}_{e}", u)
                            level(lv + 1, e)
                        for e in range(2):
                            S.wait(dve, f"x{lv}_{e}", u)
                            then(tt(rw_x[e], ps[:, 4 + e, :], rw_x[e], ALU.add), f"x{lv}_{e}")
                    for e in range(2):
                        S.wait(dve, f"z{lv}_{e}", u)
                        then(tt(rw_z[e], ps[:, 6 + e, :], rw_z[e], ALU.add), f"z{lv}_{e}")
                    if more and lv in (1, 2):
                        shift(u + 1, lv - 1)
                then(nc.vector.memset(slots(arena, 24, 2), 0.0), "zero")
                S.wait(dve, "atf", u)
                dve.wait_ge(rw_folded, 1)
                at = rw_at.rearrange("p (g q) w -> p g q w", q=2)
                start = rw_state.rearrange("p (g q) w -> p g q w", q=2)
                pc = rw_pc[:].rearrange("p (g q) -> p g q", q=2)
                for q in range(2):
                    bank = blocks(ps[:, 6 + q, :])
                    for e in range(2):
                        rows = slice(64 * e, 64 * e + 64)
                        fold = rw_fold[rows].rearrange("p (a w) -> p a w", a=1).broadcast_to([64, NB, CHUNK])
                        then(tt(at[rows, :, q, rows], bank[rows, :, 0:64], fold, ALU.add), f"at{q}_{e}")
                    then(tt(start[:, :, q, :], bank[:, :, 64:128],
                            pc[:, :, q:q + 1].broadcast_to([P, NB, CHUNK]), ALU.mult), f"f{q}")
                for c in range(1, NC - 1):
                    S.wait(dve, f"st{c}", u)
                    then(stt(out=rw_state[:, c, :], in0=ps[:, 2, 0:64], scalar=rw_pc[:, c:c + 1],
                             in1=rw_state[:, c, :], op0=ALU.mult, op1=ALU.add), f"st{c}")
                S.wait(dve, "ng", u)
                then(tt(blocks(rw_rg), blocks(ps[:, 4, :]), rw_qr[:, :, 1, :], ALU.add), "rg")
                S.wait(dve, "mu", u)
                then(stt(out=rw_yc, in0=ps[:, 7, :], scalar=-1.0 / 64, in1=rw_y, op0=ALU.mult, op1=ALU.add),
                     "yc")
                A.wait(dve, "vroot", u)
                then(nc.vector.reciprocal(rw_vr, rw_vr), "vrec")
                then(stt(out=rw_yc, in0=rw_yc, scalar=rw_col(u, RW_GNG), in1=rw_vr, op0=ALU.mult,
                         op1=ALU.mult), "yn")
                then(stt(out=rw_yc, in0=rw_yc, scalar=rw_col(u, RW_GNB), in1=rw_bon, op0=ALU.add,
                         op1=ALU.add), "ynb")
                then(tt(mix_tile(u), rw_yc, rw_gate, ALU.mult), "mix")
                V.finish()

            shift(0, 0)
            shift(0, 1)
            unit(0)
            with dve.Fori(1, RW_PAIRS - 1) as u:
                unit(u)
            unit(RW_PAIRS - 1, more=False)

        at_q_in, at_k_in, at_v_in, at_gate = (slots(arena, j) for j in range(4))
        at_q, at_k, at_v = (slots(arena, 4 + j) for j in range(3))
        at_p = slots(arena, 7, 4).rearrange("p (b k) -> p b k", b=TB)
        at_pt = slots(arena, 11, 3)[:, 0:ZW]
        at_bias = slots(arena, 18, 8).rearrange("p (h k) -> p h k", k=256)
        at_cmask = slots(arena, 15)[:, 0:P]
        at_cum, at_ncum = slots(arena, 16), slots(arena, 17)
        at_st = sb("at_st", [P, 3, TB])
        at_const = sem("at_const")
        bias_rows = nc.dram_tensor("bias_rows", (16, 384), F32, kind="Internal").ap()
        bias_ready = sem("bias_ready")
        bias_stored = sem("bias_stored")
        bias_loaded = sem("bias_loaded")
        bias_flipped = sem("bias_flipped")
        bias_copied = sem("bias_copied")
        bias_masked = sem("bias_masked")
        at_flip = slots(arena, 26)[:, 0:P]

        class Attention:

            def __init__(self, name, layer, n0, units, heads, shift, tile0, scale):
                self.layer, self.n0, self.units, self.heads, self.shift = layer, n0, units, heads, shift
                self.tile0, self.scale = tile0, scale
                hs = range(heads)
                self.pe = Steps(sem(name + "_pe"), "vt " + " ".join(f"s{h} tp{h} pv{h}" for h in hs))
                self.act = Steps(sem(name + "_act"), "vn " + " ".join(
                    " ".join(f"e{h}_{b}" for b in range(TB)) + f" pt{h}" for h in hs))
                pre = "" if heads == 2 else "nc "
                self.dve = Steps(sem(name + "_dve"), "qc kc " + pre + " ".join(
                    (f"near{h} diag{h} " if heads == 2 else f"diag{h} ")
                    + " ".join(f"mx{h}_{b}" for b in range(TB)) + f" rec{h} "
                    + " ".join(f"sc{h}_{b}" for b in range(TB)) for h in hs) + " mix")

        even = Attention("ev", 1, N_EVEN, EV_PAIRS, 2, 16, 0, 0.125)
        odd = Attention("od", 2, N_ODD, ODD_HEADS, 1, 28, 0, float(P) ** -0.5)

        def attention_tensor(pe, at):
            A, V, S = at.act, at.dve, at.pe
            width = P // at.heads

            def unit(u, more):
                n = u * 4 + at.n0
                S.start(u)

                def fill(j):
                    if more:
                        gemm(pe, n + (4 + j), (at.n0 + j) % 2, free=(evac_act, n + (3 + j - at.shift)))

                A.wait_before(pe, u)
                pe.wait_ge(evac_act, n + (3 - at.shift))
                for b in range(TB):
                    mm = pe.transpose(ps[:, 7, b * P:(b + 1) * P], at_v_in[:, b * P:(b + 1) * P], ident[:])
                S.mark(mm, "vt")
                for h in range(at.heads):
                    rows = slice(width * h, width * h + width)
                    V.wait(pe, "kc" if at.heads == 2 else "nc", u)
                    if h:
                        A.wait(pe, "pt0", u)
                    for b in range(TB):
                        dst = ps[:, 2 + b, 0:(b + 1) * P]
                        mm = pe.matmul(dst, at_q[rows, b * P:(b + 1) * P], at_k[rows, 0:(b + 1) * P],
                                       start=True, stop=at.heads == 2)
                        if at.heads == 1:
                            mm = pe.matmul(dst, ones[0:16, :], at_ncum[0:16, 0:(b + 1) * P], start=False,
                                           stop=True)
                    S.mark(mm, f"s{h}")
                    fill(2 * h)
                    V.wait(pe, f"sc{h}_3", u)
                    for kb in range(TB):
                        for qb in range(kb, TB):
                            mm = pe.transpose(
                                zb[:, ZOFF[kb] + (qb - kb) * P:ZOFF[kb] + (qb - kb + 1) * P],
                                at_p[:, qb, kb * P:(kb + 1) * P], ident[:])
                    S.mark(mm, f"tp{h}")
                    fill(2 * h + 1)
                    A.wait(pe, f"pt{h}", u)
                    if h == 0:
                        V.wait_before(pe, u)
                    for kb in range(TB):
                        mm = pe.matmul(ps[rows, 6, kb * P:T],
                                       at_v[:, kb * P + width * h:kb * P + width * h + width],
                                       at_pt[:, ZOFF[kb]:ZOFF[kb] + (TB - kb) * P],
                                       start=kb == 0, stop=kb == TB - 1, skip_group_check=True)
                    S.mark(mm, f"pv{h}")
                if at.heads == 1:
                    fill(2)
                    fill(3)
                S.finish()

            for j in range(at.heads, 4):
                gemm(pe, at.n0 + j, (at.n0 + j) % 2, free=(evac_act, at.n0 + j - 1 - at.shift))
            if at.heads == 2:
                bias_tensor(pe)
            unit(0, True)
            with pe.Fori(1, at.units - 1) as u:
                unit(u, True)
            unit(at.units - 1, False)

        def attention_scalar(act, at):
            A, V, S = at.act, at.dve, at.pe

            def take(u, j):
                par = (at.n0 + j) % 2
                src = ps[:, par, :]

                def body():
                    if j == 0:
                        return nc.scalar.activation(at_q_in, src, ACT.Copy, scale=at.scale)
                    if j == 3:
                        return nc.scalar.activation(at_gate, src, ACT.Silu)
                    return nc.scalar.activation((at_q_in, at_k_in, at_v_in)[j], src, ACT.Copy)
                taken(act, u * 4 + (at.n0 + j), par, body)

            def unit(u, more):
                A.start(u)

                def fill(j):
                    if more:
                        if j < 2:
                            V.wait(act, "qc" if j == 0 else "kc", u)
                        if j == 3:
                            V.wait(act, "mix", u)
                        take(u + 1, j)

                S.wait_before(act, u)
                S.wait(act, "vt", u)
                A.mark(nc.scalar.activation(at_v, ps[:, 7, :], ACT.Copy), "vn")
                for h in range(at.heads):
                    if h:
                        S.wait(act, f"tp{h - 1}", u)
                    for b in range(TB):
                        V.wait(act, f"mx{h}_{b}", u)
                        A.mark(nc.scalar.activation(
                            at_p[:, b, 0:(b + 1) * P], ps[:, 2 + b, 0:(b + 1) * P], ACT.Exp,
                            bias=at_st[:, 0, b:b + 1], accum_out=at_st[:, 1, b:b + 1]), f"e{h}_{b}")
                    fill(2 * h)
                    S.wait(act, f"tp{h}", u)
                    if h:
                        S.wait(act, f"pv{h - 1}", u)
                    A.mark(nc.scalar.activation(at_pt, zb, ACT.Copy), f"pt{h}")
                    if at.heads == 1:
                        fill(1)
                    elif h == 0:
                        fill(1)
                if at.heads == 1:
                    fill(2)
                fill(3)
                A.finish()

            for j in range(4):
                take(0, j)
            unit(0, True)
            with act.Fori(1, at.units - 1) as u:
                unit(u, True)
            unit(at.units - 1, False)

        def attention_vector(dve, at):
            A, V, S = at.act, at.dve, at.pe
            tt, ts = nc.vector.tensor_tensor, nc.vector.tensor_scalar

            def unit(u):
                V.start(u)

                def then(ins, name):
                    V.mark(ins, name)
                    V.wait(dve, name, u)

                S.wait_before(dve, u)
                dve.wait_ge(evac_act, u * 4 + (at.n0 + 1 - at.shift))
                V.mark(nc.vector.tensor_copy(at_q, at_q_in), "qc")
                dve.wait_ge(evac_act, u * 4 + (at.n0 + 2 - at.shift))
                V.mark(nc.vector.tensor_copy(at_k, at_k_in), "kc")
                if at.heads == 1:
                    then(ts(at_ncum[0:16, :], at_cum[0:16, :], ident_col(u), -1.0, ALU.mult, ALU.mult), "nc")
                for h in range(at.heads):
                    S.wait(dve, f"s{h}", u)
                    if at.heads == 2:
                        near = psf[:, 3 * T:3 * T + 3 * 640].rearrange("p (b k) -> p b k", b=3)[:, :, 0:256]
                        bias = at_bias[:, bass.ds(u * 2 + h, 1), :]
                        V.mark(tt(near, near, bias.broadcast_to([P, 3, 256]), ALU.add), f"near{h}")
                        then(tt(ps[:, 2, 0:P], ps[:, 2, 0:P],
                                bias.rearrange("p a k -> p (a k)")[:, P:2 * P], ALU.add), f"diag{h}")
                        V.wait(dve, f"near{h}", u)
                    else:
                        d = psf[:, 2 * T:2 * T + 3 * 640 + P + 512][:, 0:4 * 640].rearrange(
                            "p (b k) -> p b k", b=4)[:, :, 0:P]
                        then(tt(d, d, at_cmask.rearrange("p (a k) -> p a k", a=1).broadcast_to([P, TB, P]),
                                ALU.add), f"diag{h}")
                    for b in range(TB):
                        V.mark(nc.vector.tensor_reduce(at_st[:, 0, b:b + 1], ps[:, 2 + b, 0:(b + 1) * P],
                                                       AX.X, ALU.max, negate=True), f"mx{h}_{b}")
                    A.wait(dve, f"e{h}_3", u)
                    then(nc.vector.reciprocal(at_st[:, 2, :], at_st[:, 1, :]), f"rec{h}")
                    for b in range(TB):
                        V.mark(ts(at_p[:, b, 0:(b + 1) * P], at_p[:, b, 0:(b + 1) * P],
                                  at_st[:, 2, b:b + 1], None, ALU.mult), f"sc{h}_{b}")
                S.wait(dve, f"pv{at.heads - 1}", u)
                dve.wait_ge(evac_act, u * 4 + (at.n0 + 4 - at.shift))
                V.mark(tt(mix_tile(u + at.tile0), ps[:, 6, :], at_gate, ALU.mult), "mix")
                V.finish()

            def ident_col(u):
                return ident[0:16, bass.ds(u, 1)] if not isinstance(u, int) else ident[0:16, u:u + 1]

            unit(0)
            with dve.Fori(1, at.units - 1) as u:
                unit(u)
            unit(at.units - 1)

        def bias_scalar(act):
            act.dma_start(slots(arena, 16)[0:16, 0:257], rel_bias).then_inc(bias_ready, 16)
            act.wait_ge(bias_ready, 18)
            act.dma_start(bias_rows, slots(arena, 17)[0:16, 0:384]).then_inc(bias_stored, 16)
            act.wait_ge(bias_stored, 16)
            act.dma_start(at_bias, bass.AP(bias_rows.tensor, 0, [[1, P], [384, 16], [1, 256]])).then_inc(
                bias_loaded, 16)
            act.dma_start(at_flip, consts[:, C_FLIP:C_FLIP + P]).then_inc(bias_loaded, 16)

        def bias_tensor(pe):
            pe.wait_ge(bias_loaded, 32)
            for j in range(8):
                if j >= 4:
                    pe.wait_ge(bias_copied, j - 3)
                pe.matmul(ps[:, 2 + j % 4, :], at_flip, slots(arena, 18 + j), start=True,
                          stop=True).then_inc(bias_flipped, 1)
            pe.wait_ge(bias_copied, 8)

        def bias_vector(dve):
            rows, rel = slots(arena, 17)[0:16, 0:384], slots(arena, 16)[0:16, 0:257]
            dve.wait_ge(bias_ready, 16)
            nc.vector.memset(rows, 0.0).then_inc(bias_ready, 1)
            dve.wait_ge(bias_ready, 17)
            nc.vector.tensor_scalar(rows[:, 127:383], rel[:, 256:0:-1], rel[:, 256:257], None,
                                    ALU.subtract).then_inc(bias_ready, 1)
            for j in range(8):
                dve.wait_ge(bias_flipped, j + 1)
                nc.vector.tensor_copy(slots(arena, 18 + j), ps[:, 2 + j % 4, :]).then_inc(bias_copied, 1)
            dve.wait_ge(bias_copied, 8)
            nc.vector.memset(at_bias[0:64, :, 192:256], NEG).then_inc(bias_masked, 1)
            dve.wait_ge(bias_masked, 1)

        fg = Steps(sem("fg"), "y mn n e l ls cum")
        fg_t = [slots(arena, 18 + j)[0:16, :] for j in range(4)]

        def forget_tensor(pe):
            pe.wait_ge(evac_dve, 2 * KT)
            gemm_two(pe, N_F, norm_lo, 2 * KT)

        def forget_scalar(act):
            act.dma_start(at_cmask, consts[:, C_ODD:C_ODD + P]).then_inc(at_const, 16)
            par = N_F % 2
            cast(act, N_F * 2 + 4, (2 * par) % 4)
            act.wait_ge(pe_half, N_F * 2 + 2)
            nc.scalar.activation(fg_t[0], ps[0:16, par, :], ACT.Identity,
                                 bias=prm[0:16, PRM_BF:PRM_BF + 1]).then_inc(evac_act, 1)
            cast(act, N_F * 2 + 5, (2 * par + 1) % 4)
            fg.wait(act, "n", 0)
            nc.scalar.activation(fg_t[2], fg_t[2], ACT.Exp).then_inc(fg.sem, 1)
            fg.wait(act, "e", 0)
            nc.scalar.activation(fg_t[2], fg_t[2], ACT.Ln, bias=eps[0:16, 3:4]).then_inc(fg.sem, 1)

        def forget_vector(dve):
            dve.wait_ge(at_const, 16)
            dve.wait_ge(evac_act, N_F + 1 - odd.shift)
            nc.vector.memset(fg_t[3], 1.0).then_inc(fg.sem, 1)
            fg.wait(dve, "y", 0)
            nc.vector.tensor_scalar(fg_t[1], fg_t[0], 0.0, None, ALU.min).then_inc(fg.sem, 1)
            fg.wait(dve, "mn", 0)
            nc.vector.scalar_tensor_tensor(out=fg_t[2], in0=fg_t[1], scalar=2.0, in1=fg_t[0], op0=ALU.mult,
                                           op1=ALU.subtract).then_inc(fg.sem, 1)
            fg.wait(dve, "l", 0)
            nc.vector.tensor_tensor(fg_t[1], fg_t[1], fg_t[2], ALU.subtract).then_inc(fg.sem, 1)
            fg.wait(dve, "ls", 0)
            nc.vector.tensor_tensor_scan(at_cum[0:16, :], fg_t[3], fg_t[1], 0.0, ALU.mult,
                                         ALU.add).then_inc(fg.sem, 1)
            fg.wait(dve, "cum", 0)

        S5_TILES = 8
        TWO_PI = 2 * np.pi
        PI_A = 6.28125
        PI_B = float(np.float32(np.round((TWO_PI - PI_A) * 2 ** 21) / 2 ** 21))
        PI_C = float(np.float32(TWO_PI - PI_A - PI_B))
        ROUND = 12582912.0
        UNDER_2PI = float(np.nextafter(np.float32(TWO_PI), np.float32(0)))
        s5_bt = [slots(arena, 8 + 2 * e, 2) for e in range(2)]
        s5_ct = [slots(arena, 12 + 2 * e, 2) for e in range(2)]
        s5_time = slots(arena, 16)
        s5_ph, s5_cos, s5_sin = ([slots(arena, 2 * a + j) for j in range(2)] for a in range(3))
        s5_abs = slots(arena, 6)
        s5_in = slots(arena, 7)
        s5_t = [slots(arena, 17 + j) for j in range(4)]
        s5_x = [slots(arena, 21 + j) for j in range(4)]
        s5_z = [slots(arena, 25), slots(arena, 26)]
        s5_lower = [mix_tile(k) for k in range(4)]
        s5_upper = [mix_tile(6), mix_tile(7), slots(arena, 27), slots(arena, 28)]
        s5_parts = sem("s5_parts")
        s5_bs, s5_cs = (slots(arena, 29)[:, 0:256], slots(arena, 29)[:, 256:512])
        s5_p = sb("s5_p", [P, 16, 32])
        (s5_dt, s5_la, s5_ang, s5_mag, s5_k, s5_r, s5_w3, s5_fh, s5_fl, s5_are, s5_aim, s5_cr, s5_ci,
         s5_den, s5_w1, s5_w2) = (s5_p[:, j, :] for j in range(16))
        s5_loaded = sem("s5_loaded")
        s5_pre = sem("s5_pre")
        s5_pre_act = sem("s5_pre_act")
        s5_pre_pe = sem("s5_pre_pe")
        s5_pe = Steps(sem("s5_pe"), "bu0 bu1 y0 bu2 y1 bu3 y2")
        s5_act = Steps(sem("s5_act"), "cb cu sin0 abs0 cos0 cc " + " ".join(
            f"sin{k} abs{k} cos{k}" for k in (1, 2, 3)))
        s5_pool = Steps(sem("s5_pool"), " ".join(f"a{k} rd{k} ph{k} pl{k} cl{k}" for k in range(4)))
        s5_dve = Steps(sem("s5_dve"), " ".join(
            f"v0{k} v1{k} v2{k} v3{k} vr{k} vi{k} zr{k} zi{k} x0{k} x2{k} x1{k} x3{k}" for k in range(4)))
        s5_last = sem("s5_last")
        s5_out = sem("s5_out")
        s5_gelu = sem("s5_gelu")
        gates = nc.dram_tensor("gates", (8, P, T), F32, kind="Internal").ap()
        gate_stored = sem("gate_stored")
        gate_loaded = sem("gate_loaded")

        def s5_first_tensor(pe):
            pe.wait_ge(evac_dve, KT)
            gemm_two(pe, N_U, norm_lo, KT)

        def s5_tensor(pe):
            for n in range(N_U + 2, N_U + S5_TILES):
                gemm(pe, n, n % 2, free=(evac_act, n - 17))
            for e in range(2):
                pe.wait_ge(s5_pre, S5_PRE_BB + 4 * e)
                for i in range(S5_TILES):
                    mm = pe.transpose(psf[:, (2 + 2 * e) * T + i * P:(2 + 2 * e) * T + (i + 1) * P],
                                      s5_big(e)[:, i * P:(i + 1) * P], ident[:])
                mm.then_inc(s5_pre_pe, 1)
            A, V, S = s5_act, s5_dve, s5_pe
            pe.wait_ge(s5_pre_act, S5_ACT_DONE)

            def states_in(i, k):
                if k >= 2:
                    V.wait(pe, f"v3{k - 2}", i)
                elif not (isinstance(i, int) and i == 0):
                    V.wait(pe, f"v3{k + 2}", i - 1)
                for e in range(2):
                    mm = pe.matmul(ps[:, 2 + 2 * (k % 2) + e, :], s5_bs[32 * k:32 * k + 32, e * P:(e + 1) * P],
                                   s5_in[32 * k:32 * k + 32, :], start=True, stop=True)
                S.mark(mm, f"bu{k}")

            def states_out(i, k):
                V.wait(pe, f"x3{k}", i)
                for j, e in enumerate((0, 1, 0, 1)):
                    mm = pe.matmul(ps[32 * k:32 * k + 32, 6, :], s5_cs[:, e * P + 32 * k:e * P + 32 * k + 32],
                                   s5_x[j], start=j == 0, stop=j == 3, skip_group_check=True)
                return mm

            def tile(i, later, par):
                S.start(i)
                n = i + N_ZB
                A.wait(pe, "cu", i)
                states_in(i, 0)
                if later:
                    states_out(i - 1, 3).then_inc(s5_last, 1)
                states_in(i, 1)
                A.wait(pe, "cc", i)
                if later:
                    pe.wait_ge(s5_out, i)
                S.mark(states_out(i, 0), "y0")
                gemm(pe, n, par, free=(evac_act, n - 17), halves=(0,))
                for k in (1, 2):
                    states_in(i, k + 1)
                    S.mark(states_out(i, k), f"y{k}")
                    if k == 1:
                        gemm(pe, n, par, free=(evac_act, n - 17), halves=(1,))
                S.finish()

            tile(0, False, N_ZB % 2)
            with pe.Fori(0, S5_TILES // 2 - 1) as two:
                for j in (1, 2):
                    tile(two * 2 + j, True, (N_ZB + j) % 2)
            tile(S5_TILES - 1, True, (N_ZB + 1) % 2)
            states_out(S5_TILES - 1, 3).then_inc(s5_last, 1)
            for n in (N_EVEN, N_EVEN + 1):
                gemm(pe, n, n % 2, free=(evac_act, n - 17))

        def s5_big(e):
            return slots(arena, 21 + 2 * e, 2)

        S5_ACT_DONE = 4 + 2

        def s5_scalar(act):
            act.dma_start(s5_time, consts[:, C_TIME:C_TIME + T]).then_inc(s5_loaded, 16)
            for e in range(2):
                act.dma_start(slots(arena, 17 + e), s5_b[e].rearrange("p q c -> p (q c)")).then_inc(s5_loaded, 16)
            for e in range(2):
                act.dma_start(slots(arena, 27 + e), s5_c[e].rearrange("p q c -> p (q c)")).then_inc(s5_loaded, 16)
            for j in range(S5_TILES):
                n = N_U + j
                taken(act, n, n % 2, lambda: nc.scalar.activation(mix_tile(8 + j), ps[:, n % 2, :], ACT.Copy))
            act.wait_ge(s5_pre, S5_PRE_R)
            nc.scalar.activation(s5_aim, s5_r, ACT.Sin).then_inc(s5_pre_act, 1)
            nc.scalar.activation(s5_w1, s5_r, ACT.Abs).then_inc(s5_pre_act, 1)
            act.wait_ge(s5_pre_act, 2)
            nc.scalar.activation(s5_are, s5_w1, ACT.Sin, bias=eps[:, 4:5], scale=-1.0).then_inc(s5_pre_act, 1)
            act.wait_ge(s5_pre_act, 3)
            nc.scalar.activation(s5_w2, s5_w1, ACT.Copy).then_inc(s5_pre_act, 1)
            for e in range(2):
                act.wait_ge(s5_pre_pe, e + 1)
                nc.scalar.activation(s5_bt[e], psf[:, (2 + 2 * e) * T:(4 + 2 * e) * T],
                                     ACT.Copy).then_inc(s5_pre_act, 1)
            act.wait_ge(s5_pre_act, S5_ACT_DONE)
            act.wait_ge(s5_pre, S5_PRE_END)
            A, V, S, G = s5_act, s5_dve, s5_pe, s5_pool

            def matrices(dst, slot, i, name):
                both = slots(arena, slot, 4).rearrange("p (e w) -> p e w", e=2)
                src = both[:, :, bass.ds(i * P, P)] if not isinstance(i, int) else both[:, :, i * P:(i + 1) * P]
                A.mark(nc.scalar.activation(dst.rearrange("p (e w) -> p e w", e=2), src, ACT.Copy), name)

            def parts(i, k):
                c = i * 4 + k
                for dst, src in ((s5_upper[k], s5_fh), (s5_lower[k], s5_fl)):
                    col = src[:, c:c + 1] if isinstance(i, int) else src[:, bass.ds(c, 1)]
                    nc.scalar.activation(dst, s5_time, ACT.Copy, scale=col).then_inc(s5_parts, 1)

            def tables(i, k, later, more=True):
                if k >= 2:
                    V.wait(act, f"x3{k - 2}", i)
                elif later:
                    V.wait(act, f"x3{k + 2}", i - 1)
                G.wait(act, f"cl{k}", i)
                A.mark(nc.scalar.activation(s5_sin[k % 2], s5_ph[k % 2], ACT.Sin, scale=UNDER_2PI), f"sin{k}")
                if k:
                    A.wait(act, f"cos{k - 1}", i)
                elif later:
                    A.wait(act, "cos3", i - 1)
                A.mark(nc.scalar.activation(s5_abs, s5_ph[k % 2], ACT.Abs), f"abs{k}")
                A.wait(act, f"abs{k}", i)
                A.mark(nc.scalar.activation(s5_cos[k % 2], s5_abs, ACT.Sin, bias=eps[:, 4:5],
                                            scale=-UNDER_2PI), f"cos{k}")
                if k < 2:
                    parts(i, k + 2)
                elif more:
                    parts(i + 1, k - 2)

            def gelu(i):
                nc.scalar.activation(mix_tile(i + 8), mix_tile(i + 8), ACT.Gelu_apprx_tanh).then_inc(s5_gelu, 1)

            def gate(i, par):
                place = mix_tile(4 + par)
                if not (isinstance(i, int) and i == 0):
                    act.wait_ge(gate_stored, i * 16)
                n = i + N_ZB
                taken(act, n, par, lambda: nc.scalar.activation(place, ps[:, par, :], ACT.Silu))
                act.wait_ge(evac_act, n - 15)
                act.dma_start(gates[bass.ds(i, 1), :, :].rearrange("a p t -> (a p) t"), place).then_inc(
                    gate_stored, 16)

            def tile(i, later, more=True, par=0):
                A.start(i)
                if later:
                    gate(i - 1, par)
                if later:
                    S.wait(act, "bu3", i - 1)
                matrices(s5_bs, 8, i, "cb")
                A.mark(nc.scalar.activation(s5_in, mix_tile(i + 8), ACT.Copy), "cu")
                tables(i, 0, later)
                if later:
                    act.wait_ge(s5_last, i)
                matrices(s5_cs, 12, i, "cc")
                tables(i, 1, later)
                if later:
                    act.wait_ge(s5_out, i)
                tables(i, 2, later, more)
                if later:
                    gelu(i - 1)
                tables(i, 3, later, more)
                A.finish()

            parts(0, 0)
            parts(0, 1)
            tile(0, False)
            for i in (1, 2):
                tile(i, True, par=(N_ZB + i - 1) % 2)
            with act.Fori(1, S5_TILES // 2 - 1) as two:
                for j in (1, 2):
                    tile(two * 2 + j, True, par=(N_ZB + j - 1) % 2)
            tile(S5_TILES - 1, True, False, par=N_ZB % 2)
            gate(S5_TILES - 1, (N_ZB + 1) % 2)
            act.wait_ge(s5_out, S5_TILES)
            gelu(S5_TILES - 1)

        def s5_gpsimd(pool, rest):
            tt, ts = nc.gpsimd.tensor_tensor, nc.gpsimd.tensor_scalar
            A, G = s5_act, s5_pool
            pool.wait_ge(s5_pre, S5_PRE_END)
            for i in range(S5_TILES):
                G.start(i)
                for k in range(4):
                    if i and k in (2, 3):
                        m = 2 * (N_ZB + 1 + i) + k - 2
                        rest(m, m % 4)
                    w = s5_w3[:, i * 4 + k:i * 4 + k + 1]
                    ph = s5_ph[k % 2]

                    def then(ins, name):
                        G.mark(ins, name)
                        G.wait(pool, name, i)

                    if k >= 2:
                        A.wait(pool, f"cos{k - 2}", i)
                    elif i:
                        A.wait(pool, f"cos{k + 2}", i - 1)
                    then(ts(ph, s5_time, w, ROUND, ALU.mult, ALU.add), f"a{k}")
                    then(ts(ph, ph, ROUND, None, ALU.subtract), f"rd{k}")
                    pool.wait_ge(s5_parts, 2 * (4 * i + k + 1))
                    then(tt(ph, s5_upper[k], ph, ALU.subtract), f"ph{k}")
                    then(tt(ph, ph, s5_lower[k], ALU.add), f"pl{k}")
                    then(ts(ph, ph, 0.5, -0.5, ALU.min, ALU.max), f"cl{k}")
                G.finish()

        S5_PRE_R, S5_PRE_BB, S5_PRE_END = 40, 65, 74
        LN2_A = 0.693359375
        LN2_B = float(np.log(2) - LN2_A)

        def s5_vector(dve):
            tt, ts, stt = nc.vector.tensor_tensor, nc.vector.tensor_scalar, nc.vector.scalar_tensor_tensor
            pre = Order(dve, s5_pre)
            lre, lim = prm[:, PRM_LRE:PRM_LRE + 32], prm[:, PRM_LIM:PRM_LIM + 32]
            dve.wait_ge(s5_loaded, 16 * 5)

            def exp(dst, src):
                x, k, bits = s5_w1, s5_k, s5_w2
                pre.then(ts(x, src, 100.0, -100.0, ALU.min, ALU.max))
                pre.then(ts(k, x, float(1 / np.log(2)), ROUND, ALU.mult, ALU.add))
                pre.then(ts(k, k, ROUND, 128.0, ALU.subtract, ALU.min))
                pre.then(ts(k, k, -127.0, None, ALU.max))
                pre.then(stt(out=x, in0=k, scalar=-LN2_A, in1=x, op0=ALU.mult, op1=ALU.add))
                pre.then(stt(out=x, in0=k, scalar=-LN2_B, in1=x, op0=ALU.mult, op1=ALU.add))
                pre.then(ts(dst, x, 1 / 5040, None, ALU.mult))
                for c in (1 / 720, 1 / 120, 1 / 24, 1 / 6, 0.5, 1.0):
                    pre.then(stt(out=dst, in0=dst, scalar=c, in1=x, op0=ALU.add, op1=ALU.mult))
                pre.then(ts(bits.bitcast(I32), k, 2.0 ** 23, 127 * 2.0 ** 23, ALU.mult, ALU.add))
                pre.then(ts(dst, dst, 1.0, None, ALU.add))
                pre.then(tt(dst, dst, bits, ALU.mult))

            exp(s5_dt, prm[:, PRM_LDT:PRM_LDT + 32])
            pre.then(tt(s5_ang, lim, s5_dt, ALU.mult))
            pre.then(tt(s5_la, lre, s5_dt, ALU.mult))
            exp(s5_mag, s5_la)
            pre.then(ts(s5_k, s5_ang, 1 / TWO_PI, ROUND, ALU.mult, ALU.add))
            pre.then(ts(s5_k, s5_k, ROUND, None, ALU.subtract))
            pre.then(stt(out=s5_r, in0=s5_k, scalar=-PI_A, in1=s5_ang, op0=ALU.mult, op1=ALU.add))
            pre.then(stt(out=s5_r, in0=s5_k, scalar=-PI_B, in1=s5_r, op0=ALU.mult, op1=ALU.add))
            pre.then(stt(out=s5_r, in0=s5_k, scalar=-PI_C, in1=s5_r, op0=ALU.mult, op1=ALU.add))
            pre.then(ts(s5_r, s5_r, UNDER_2PI / 2, -UNDER_2PI / 2, ALU.min, ALU.max))
            assert pre.k == S5_PRE_R, pre.k
            pre.then(ts(s5_w3, s5_r, 1 / TWO_PI, None, ALU.mult))
            pre.then(ts(s5_fl, s5_w3, 4097.0, None, ALU.mult))
            pre.then(tt(s5_fh, s5_fl, s5_w3, ALU.subtract))
            pre.then(tt(s5_fh, s5_fl, s5_fh, ALU.subtract))
            pre.then(tt(s5_fl, s5_w3, s5_fh, ALU.subtract))
            dve.wait_ge(s5_pre_act, 4)
            pre.then(tt(s5_are, s5_are, s5_mag, ALU.mult))
            pre.then(tt(s5_aim, s5_aim, s5_mag, ALU.mult))
            pre.then(ts(s5_are, s5_are, 1.0, None, ALU.subtract))
            pre.then(tt(s5_den, lre, lre, ALU.mult))
            pre.then(tt(s5_w1, lim, lim, ALU.mult))
            pre.then(tt(s5_den, s5_den, s5_w1, ALU.add))
            pre.then(nc.vector.reciprocal(s5_den, s5_den))
            pre.then(tt(s5_w1, s5_are, lre, ALU.mult))
            pre.then(tt(s5_w2, s5_aim, lim, ALU.mult))
            pre.then(tt(s5_w1, s5_w1, s5_w2, ALU.add))
            pre.then(tt(s5_cr, s5_w1, s5_den, ALU.mult))
            pre.then(tt(s5_w1, s5_aim, lre, ALU.mult))
            pre.then(tt(s5_w2, s5_are, lim, ALU.mult))
            pre.then(tt(s5_w1, s5_w1, s5_w2, ALU.subtract))
            pre.then(tt(s5_ci, s5_w1, s5_den, ALU.mult))

            def by_pair(view):
                return view.rearrange("p (q a) -> p q a", a=1).broadcast_to([P, 32, 16])

            def chans(view):
                return view.rearrange("p (q c) -> p q c", c=16)

            br, bi, tmp = slots(arena, 17), slots(arena, 18), slots(arena, 19)
            pre.then(nc.vector.memset(slots(arena, 21, 4), 0.0))
            for e, (x0, x1, op) in enumerate(((br, bi, ALU.subtract), (bi, br, ALU.add))):
                pre.then(tt(chans(tmp), chans(x0), by_pair(s5_cr), ALU.mult))
                pre.then(tt(chans(slots(arena, 20)), chans(x1), by_pair(s5_ci), ALU.mult))
                big = s5_big(e).rearrange("p (q g c) -> p q g c", g=2, c=16)
                for g in range(2):
                    rows = slice(64 * g, 64 * g + 64)
                    ins = tt(big[rows, :, g, :], chans(tmp)[rows], chans(slots(arena, 20))[rows], op)
                    pre.then(ins)
            pre.then(nc.vector.memset(slots(arena, 12, 4), 0.0))
            for e in range(2):
                big = s5_ct[e].rearrange("p (q g c) -> p q g c", g=2, c=16)
                src = chans(slots(arena, 27 + e))
                for g in range(2):
                    rows = slice(64 * g, 64 * g + 64)
                    pre.then(ts(big[rows, :, g, :], src[rows], -1.0 if e else 1.0, None, ALU.mult))
            assert pre.k == S5_PRE_END, pre.k

            A, V, S = s5_act, s5_dve, s5_pe
            dve.wait_ge(s5_pre_act, S5_ACT_DONE)

            def output(i):
                dve.wait_ge(s5_last, i + 1)
                u = mix_tile(i + 8)
                d = prm[:, PRM_SD + i:PRM_SD + i + 1] if isinstance(i, int) else prm[:, bass.ds(i + PRM_SD, 1)]
                stt(out=u, in0=u, scalar=d, in1=ps[:, 6, :], op0=ALU.mult, op1=ALU.add).then_inc(s5_out, 1)

            def tile(i, later):
                V.start(i)
                for k in range(4):
                    def col(view):
                        c = i * 4 + k
                        return view[:, c:c + 1] if isinstance(i, int) else view[:, bass.ds(c, 1)]

                    re, im = ps[:, 2 + 2 * (k % 2), :], ps[:, 3 + 2 * (k % 2), :]
                    cos, sin = s5_cos[k % 2], s5_sin[k % 2]
                    t, z, x = s5_t, s5_z, s5_x
                    if k:
                        V.wait(dve, f"x3{k - 1}", i)
                    elif later:
                        V.wait(dve, "x33", i - 1)
                    S.wait(dve, f"bu{k}", i)
                    A.wait(dve, f"cos{k}", i)
                    V.mark(tt(t[0], re, cos, ALU.mult), f"v0{k}")
                    V.mark(tt(t[1], im, sin, ALU.mult), f"v1{k}")
                    V.mark(tt(t[2], im, cos, ALU.mult), f"v2{k}")
                    V.mark(tt(t[3], re, sin, ALU.mult), f"v3{k}")
                    V.wait(dve, f"v1{k}", i)
                    V.mark(tt(t[0], t[0], t[1], ALU.add), f"vr{k}")
                    V.wait(dve, f"v3{k}", i)
                    V.mark(tt(t[2], t[2], t[3], ALU.subtract), f"vi{k}")
                    mag = col(s5_mag).broadcast_to([P, T])
                    V.wait(dve, f"vr{k}", i)
                    V.mark(nc.vector.tensor_tensor_scan(z[0], mag, t[0], 0.0, ALU.mult, ALU.add), f"zr{k}")
                    V.wait(dve, f"vi{k}", i)
                    V.mark(nc.vector.tensor_tensor_scan(z[1], mag, t[2], 0.0, ALU.mult, ALU.add), f"zi{k}")
                    if k:
                        S.wait(dve, f"y{k - 1}", i)
                    elif later:
                        dve.wait_ge(s5_last, i)
                    V.wait(dve, f"zr{k}", i)
                    V.mark(tt(x[0], z[0], cos, ALU.mult), f"x0{k}")
                    V.mark(tt(x[1], z[0], sin, ALU.mult), f"x2{k}")
                    V.wait(dve, f"zi{k}", i)
                    V.mark(stt(out=x[2], in0=z[1], scalar=-1.0, in1=sin, op0=ALU.mult, op1=ALU.mult), f"x1{k}")
                    V.mark(tt(x[3], z[1], cos, ALU.mult), f"x3{k}")
                    if k == 0 and later:
                        output(i - 1)
                V.finish()

            tile(0, False)
            with dve.Fori(1, S5_TILES) as i:
                tile(i, True)
            output(S5_TILES - 1)

        glu_gate = [slots(arena, j) for j in range(8)]
        glu_sg = [slots(arena, 8), slots(arena, 9)]
        glu_hi = sem("glu_hi")
        glu_lo = sem("glu_lo")
        glu_mul = sem("glu_mul")
        GLU_TAKEN = N_GLU - 16

        def glu_tensor(pe):
            pe.wait_ge(evac_act, GLU_TAKEN)
            for j in range(4):
                n = N_GLU + j
                gemm(pe, n, n % 2, free=(evac_act, GLU_TAKEN + max(0, 2 * j - 1)), outputs=2,
                     act_ready=(glu_lo, 0) if j == 0 else None)

        def glu_scalar(act):
            act.wait_ge(gate_stored, 16 * 8)
            act.dma_start(slots(arena, 0, 8).rearrange("p (j t) -> p j t", j=8),
                          gates.rearrange("j p t -> p j t")).then_inc(gate_loaded, 16)
            for j in range(8):
                nc.scalar.activation(act_hi[:, j, :], mix_tile(8 + j), ACT.Copy).then_inc(glu_hi, 1)
            for o in range(8):
                n, h = N_GLU + o // 2, o % 2
                if h == 0:
                    cast(act, n * 2 + 4, (2 * n) % 4)
                act.wait_ge(pe_half, n * 2 + h + 1)
                if o >= 2:
                    act.wait_ge(glu_mul, o - 1)
                nc.scalar.activation(glu_sg[h], ps[:, h, :], ACT.Sigmoid,
                                     bias=prm[:, PRM_BGLU + o:PRM_BGLU + o + 1]).then_inc(evac_act, 1)
                if h == 1:
                    cast(act, n * 2 + 5, (2 * n + 1) % 4)

        def glu_vector(dve):
            dve.wait_ge(gate_loaded, 16)
            for j in range(8):
                dve.wait_ge(glu_hi, j + 1)
                nc.vector.tensor_tensor(act_lo[:, j, :], mix_tile(8 + j), act_hi[:, j, :].bitcast(F32),
                                        ALU.subtract).then_inc(glu_lo, 1)
            for o in range(8):
                dve.wait_ge(evac_act, GLU_TAKEN + o + 1)
                nc.vector.tensor_tensor(glu_sg[o % 2], glu_sg[o % 2], mix_tile(8 + o),
                                        ALU.mult).then_inc(glu_sgm, 1)
                dve.wait_ge(glu_sgm, o + 1)
                nc.vector.tensor_tensor(mix_tile(8 + o), glu_sg[o % 2], glu_gate[o],
                                        ALU.mult).then_inc(glu_mul, 1)

        glu_sgm = sem("glu_sgm")

        out_nat = slots(arena, 0, 16).rearrange("p (b d) -> p b d", b=TB)

        def result_tensor(pe):
            for ft in range(KT):
                pe.wait_ge(norm_t, 3 * KT + ft + 1)
                if ft >= 2:
                    pe.wait_ge(out_copied, ft - 1)
                for b in range(TB):
                    mm = pe.transpose(ps[:, 2 + ft % 2, b * P:(b + 1) * P],
                                      norm_in[ft % 4][:, b * P:(b + 1) * P], ident[:])
                mm.then_inc(out_turned, 1)

        def result_scalar(act):
            for ft in range(KT):
                act.wait_ge(out_turned, ft + 1)
                nc.scalar.activation(out_nat[:, :, ft * P:(ft + 1) * P], blocks(ps[:, 2 + ft % 2, :]),
                                     ACT.Copy).then_inc(out_copied, 1)
                if ft % 4 == 3:
                    cols = slice((ft - 3) * P, (ft + 1) * P)
                    act.wait_ge(out_copied, ft + 1)
                    act.dma_start(out[:, cols].rearrange("(b p) d -> p b d", p=P),
                                  out_nat[:, :, cols]).then_inc(out_stored, 16)
            act.wait_ge(out_stored, 16 * 4)

        @block.gpsimd
        def _(pool):
            for c, v in enumerate((64 * RMS_EPS, RMS_EPS, GN_EPS, 1.0, np.pi / 2)):
                last = nc.gpsimd.memset(eps[:, c:c + 1], float(v))
            last.then_inc(eps_set, 1)

            def rest(m, s):
                pool.wait_ge(cast_done, m + 1)
                nc.gpsimd.tensor_tensor(w_lo[:, s, :, :], raw[:, s % 2, :, :],
                                        w_hi[:, s, :, :].bitcast(F32), ALU.subtract).then_inc(split_done, 1)

            def rests(m0, m1):
                for m in range(m0, min(m1, -(-m0 // 4) * 4)):
                    rest(m, m % 4)
                with pool.Fori(-(-m0 // 4), m1 // 4) as i:
                    for s in range(4):
                        rest(i * 4 + s, s)
                for m in range(m1 // 4 * 4, m1):
                    rest(m, m % 4)

            for m in range(4):
                rest(m, m)
            norm_gpsimd(pool, 0)
            rests(4, 2 * (N_U + 2))
            norm_gpsimd(pool, 1)
            rests(2 * (N_U + 2), 2 * (N_ZB + 2))
            s5_gpsimd(pool, rest)
            rests(2 * (N_EVEN + 1), 2 * (N_F + 2))
            norm_gpsimd(pool, 2)
            rests(2 * (N_F + 2), 2 * N_TILES)

        @block.tensor
        def _(pe):
            load_tensor(pe)
            gemm_two(pe, N_WDAD, norm_lo, 0)
            rwkv_tensor(pe)
            meet(pe, 1)
            pool_tensor(pe)
            meet(pe, 2)
            sb_tensor(pe)
            meet(pe, 3)
            out_tensor(pe, 0, N_OUT1, N_OUT1)
            s5_first_tensor(pe)
            meet(pe, 4)
            s5_tensor(pe)
            meet(pe, 5)
            attention_tensor(pe, even)
            meet(pe, 6)
            glu_tensor(pe)
            meet(pe, 7)
            out_tensor(pe, 1, N_OUT2, GLU_TAKEN + 8)
            forget_tensor(pe)
            meet(pe, 8)
            attention_tensor(pe, odd)
            meet(pe, 9)
            out_tensor(pe, 2, N_OUT3, N_OUT3 - odd.shift)
            meet(pe, 10)
            result_tensor(pe)

        @block.scalar
        def _(act):
            load_scalar(act)
            norm_scalar(act, 0)
            taken(act, N_WDAD, 0, lambda: nc.scalar.activation(slots(arena, 29), ps[:, 0, :], ACT.Copy))
            rwkv_scalar(act)
            meet(act, 1)
            pool_scalar(act)
            meet(act, 2)
            sb_scalar(act)
            meet(act, 3)
            mix_split_scalar(act, 0)
            out_scalar(act, 0, N_OUT1)
            norm_scalar(act, 1)
            meet(act, 4)
            s5_scalar(act)
            meet(act, 5)
            bias_scalar(act)
            attention_scalar(act, even)
            meet(act, 6)
            glu_scalar(act)
            meet(act, 7)
            mix_split_scalar(act, 1)
            out_scalar(act, 1, N_OUT2)
            norm_scalar(act, 2)
            meet(act, 8)
            forget_scalar(act)
            attention_scalar(act, odd)
            meet(act, 9)
            mix_split_scalar(act, 2)
            out_scalar(act, 2, N_OUT3)
            norm_scalar(act, 3)
            meet(act, 10)
            result_scalar(act)

        @block.vector
        def _(dve):
            dve.wait_ge(consts_loaded, 64)
            load_vector(dve)
            norm_vector(dve, 0)
            rwkv_vector(dve)
            meet(dve, 1)
            pool_vector(dve)
            meet(dve, 2)
            sb_vector(dve)
            meet(dve, 3)
            mix_split_vector(dve, 0)
            out_vector(dve, 0, N_OUT1)
            norm_vector(dve, 1)
            meet(dve, 4)
            s5_vector(dve)
            meet(dve, 5)
            bias_vector(dve)
            attention_vector(dve, even)
            meet(dve, 6)
            glu_vector(dve)
            meet(dve, 7)
            mix_split_vector(dve, 1)
            out_vector(dve, 1, N_OUT2)
            norm_vector(dve, 2)
            meet(dve, 8)
            forget_vector(dve)
            attention_vector(dve, odd)
            meet(dve, 9)
            mix_split_vector(dve, 2)
            out_vector(dve, 2, N_OUT3)
            meet(dve, 10)
            norm_vector(dve, 3)


def weight_tile(w, cols):
    k = w.shape[0] // P
    t = w[:, cols:cols + P].reshape(k, P, P).transpose(1, 0, 2)
    return np.stack([t[:, :k // 2], t[:, k // 2:]]).reshape(2, P, -1)


def weight_stream(i):
    w1, w2, w3 = i["w_in"][0], i["w_in_even_2"][0], i["w_in_odd_2"][0]
    tiles = [weight_tile(w1, 3072)]
    tiles += [weight_tile(w1, 768 * j + P * p) for p in range(RW_PAIRS) for j in range(4)]
    tiles += [weight_tile(w1, 3200 + T * j + P * g) for g in range(POOL_GROUPS) for j in range(2)]
    tiles += [weight_tile(w1, 4224 + 768 * j + P * p) for p in range(SB_PAIRS) for j in range(4)]
    tiles += [weight_tile(i["w_out"][0], P * c) for c in range(KT)]
    tiles += [weight_tile(w2, 3072 + P * c) for c in range(8)]
    tiles += [weight_tile(w2, 5120 + P * c) for c in range(8)]
    tiles += [weight_tile(w2, c + P * p) for p in range(EV_PAIRS) for c in (0, 1024, 2048, 4096)]
    glu = [i["w_glu_2"][0][:, P * c:P * c + P].reshape(8, P, P).transpose(1, 0, 2).reshape(P, -1) for c in range(8)]
    tiles += [np.stack([glu[c], glu[c + 1]]) for c in range(0, 8, 2)]
    tiles += [weight_tile(i["w_out_even_2"][0], P * c) for c in range(KT)]
    tiles += [weight_tile(np.pad(w3[:, 8192:8208], ((0, 0), (0, P - 16))), 0)]
    tiles += [weight_tile(w3, 2048 * j + P * h) for h in range(ODD_HEADS) for j in range(4)]
    tiles += [weight_tile(i["w_out_odd_2"][0], P * c) for c in range(KT)]
    return np.stack(tiles)


def parameters(i):
    def tiles(a):
        return a.reshape(-1, P)
    rw = [tiles(i["mu_a"][0][768 * j:768 * j + 768]) for j in range(4)]
    rw += [tiles(i[k][0].reshape(-1)) for k in ("w0", "a0", "k_k", "k_a", "r_k", "gn_g", "gn_b")]
    rows = [tiles(i[k].reshape(-1)) for k in ("norm_g", "norm_even_g_2", "norm_odd_g_2", "final_norm_g_2")]
    rows += [tiles(i["mu_a"][0][3072:3200]), np.stack(rw, 1).reshape(-1, P), tiles(i["pool_scale"][0])]
    rows += [np.tile(i["qn_g"], 2), np.tile(i["kn_g"], 2)]
    rows += [tiles(i["s5_lambda_re_2"][0]), tiles(i["s5_lambda_im_2"][0])]
    rows += [tiles(np.repeat(i["s5_log_dt_2"][0], 64)), tiles(i["s5_d_2"][0]), tiles(i["b_glu_2"][0])]
    rows += [np.pad(i["b_forget_2"][0], (0, P - 16))[None]]
    return np.ascontiguousarray(np.concatenate(rows, 0).T)


def kernel(**inputs):
    import concourse.bacc as bacc
    from concourse.bass_utils import run_bass_kernel_spmd

    i = {k: np.asarray(v) for k, v in inputs.items()}

    def s5_side(a):
        return np.ascontiguousarray(a.reshape(32, P, 16).transpose(1, 0, 2))

    arrays = {
        "stream": weight_stream(i),
        "x": np.ascontiguousarray(i["x"][0]),
        "params": parameters(i),
        "consts": constants(),
        "rel_bias": np.ascontiguousarray(i["rel_bias_2"][0]),
        "lora": np.stack([np.concatenate([i[k][0][:, P * p:P * p + P] for k in ("w_up", "a_up")])
                          for p in range(6)]),
        "pool_w": np.ascontiguousarray(i["pool_w"][0]),
        "s5_b": np.stack([s5_side(i["s5_b_re_2"][0]), s5_side(i["s5_b_im_2"][0])]),
        "s5_c": np.stack([s5_side(i["s5_c_re_2"][0].transpose(0, 2, 1)),
                          s5_side(i["s5_c_im_2"][0].transpose(0, 2, 1))]),
    }
    nc = bacc.Bacc("TRN2", target_bir_lowering=False, num_devices=1)
    aps = [nc.dram_tensor(k, a.shape, F32, kind="ExternalInput").ap() for k, a in arrays.items()]
    out = nc.dram_tensor("out", (T, D), F32, kind="ExternalOutput").ap()
    build_program(nc, *aps, out)
    r = run_bass_kernel_spmd(nc, [arrays], core_ids=[0])
    return r.results[0]["out"].reshape(1, T, D)
```
